# Optimizing a Trainium2 kernel written in Bass

```python
import jax, jax.numpy as jnp
from jax import lax
import numpy as np

D_MODEL = 2048
BATCH = 1
SEQ = 256
DEPTH = 1
DEC_BATCH = 8
DEC_SEQ = 4
PAST_LEN = 2048
PAGE_SIZE = 128

N_HEADS = 16
N_KV_HEADS = 4
HEAD_DIM = 64
Q_GROUP = N_HEADS // N_KV_HEADS
ATTN_WIDTH = N_HEADS * HEAD_DIM
KV_WIDTH = N_KV_HEADS * HEAD_DIM
WINDOW = 128
ATTN_BLOCK = 128
ROPE_THETA = 10000.0
POOL_WINDOWS = (2, 4, 8, 16)
N_POOL_GROUPS = 4
POOL_WIDTH = D_MODEL // 2
POOL_GROUP = POOL_WIDTH // N_POOL_GROUPS
POOL_OUT_GROUP = D_MODEL // N_POOL_GROUPS
POOL_HIST = max(POOL_WINDOWS) - 1
IN_WIDTH = ATTN_WIDTH + 2 * KV_WIDTH + POOL_WIDTH + 2 * D_MODEL
PEER_HEADS = 8
N_KEYS = 128
N_EXPERTS = N_KEYS * N_KEYS
D_KEY = 256
HALF_KEY = D_KEY // 2
PEER_TOPK = 16
PEER_CHUNK = 128
ALPHA = (2.0 * DEPTH) ** 0.25
BETA = (8.0 * DEPTH) ** -0.25
LN_EPS = 1e-5
NEG_INF = -1e30

kernel_name = 'hybrid_pool_swa_peer_decode_step'

def _layer_norm(x, g, b):
    xf = x.astype(jnp.float32)
    mu = jnp.mean(xf, axis=-1, keepdims=True)
    xc = xf - mu
    var = jnp.mean(xc * xc, axis=-1, keepdims=True)
    return (xc * lax.rsqrt(var + LN_EPS) * g.astype(jnp.float32) + b.astype(jnp.float32)).astype(x.dtype)

def _rope(x, pos):
    half = HEAD_DIM // 2
    inv = ROPE_THETA ** (-jnp.arange(half, dtype=jnp.float32) / half)
    ang = pos.astype(jnp.float32)[:, None] * inv[None, :]
    cos = jnp.cos(ang)[:, None, :]
    sin = jnp.sin(ang)[:, None, :]
    xf = x.astype(jnp.float32)
    x1, x2 = xf[..., :half], xf[..., half:]
    return jnp.concatenate([x1 * cos - x2 * sin, x2 * cos + x1 * sin], axis=-1).astype(x.dtype)

def _in_proj(x, w_in, b_in):
    B, T, _ = x.shape
    z = jnp.einsum('btd,de->bte', x, w_in) + b_in
    o1 = ATTN_WIDTH
    o2 = o1 + KV_WIDTH
    o3 = o2 + KV_WIDTH
    o4 = o3 + POOL_WIDTH
    o5 = o4 + D_MODEL
    q = z[..., :o1].reshape(B, T, N_HEADS, HEAD_DIM)
    k = z[..., o1:o2].reshape(B, T, N_KV_HEADS, HEAD_DIM)
    v = z[..., o2:o3].reshape(B, T, N_KV_HEADS, HEAD_DIM)
    u = z[..., o3:o4]
    g_pool = z[..., o4:o5]
    g_attn = z[..., o5:]
    return q, k, v, u, g_pool, g_attn

def _sink_attention(q, k, v, q_pos, k_pos, sinks):
    s = jnp.einsum('...qkgd,...skd->...kgqs', q, k).astype(jnp.float32) * (HEAD_DIM ** -0.5)
    dist = q_pos[..., :, None] - k_pos[..., None, :]
    valid = (k_pos[..., None, :] >= 0) & (dist >= 0) & (dist < WINDOW)
    s = jnp.where(valid[..., None, None, :, :], s, NEG_INF)
    sink = sinks.astype(jnp.float32).reshape(N_KV_HEADS, Q_GROUP)[:, :, None, None]
    m = jnp.maximum(jnp.max(s, axis=-1, keepdims=True), sink)
    p = jnp.exp(s - m)
    denom = jnp.sum(p, axis=-1, keepdims=True) + jnp.exp(sink - m)
    p = (p / denom).astype(v.dtype)
    return jnp.einsum('...kgqs,...skd->...qkgd', p, v)

def _attn_prompt(q, k, v, sinks):
    B, T = q.shape[:2]
    nb = T // ATTN_BLOCK
    pos = jnp.arange(T, dtype=jnp.int32)
    q = _rope(q, pos)
    k = _rope(k, pos)
    qb = q.reshape(B, nb, ATTN_BLOCK, N_KV_HEADS, Q_GROUP, HEAD_DIM)

    def band(a):
        prev = jnp.pad(a, ((0, 0), (ATTN_BLOCK, 0), (0, 0), (0, 0)))[:, :T]
        prev = prev.reshape(B, nb, ATTN_BLOCK, N_KV_HEADS, HEAD_DIM)
        cur = a.reshape(B, nb, ATTN_BLOCK, N_KV_HEADS, HEAD_DIM)
        return jnp.concatenate([prev, cur], axis=2)

    kb, vb = band(k), band(v)
    start = jnp.arange(nb, dtype=jnp.int32)[:, None] * ATTN_BLOCK
    q_pos = (start + jnp.arange(ATTN_BLOCK, dtype=jnp.int32)[None, :])[None]
    k_pos = (start - ATTN_BLOCK + jnp.arange(2 * ATTN_BLOCK, dtype=jnp.int32)[None, :])[None]
    o = _sink_attention(qb, kb, vb, q_pos, k_pos, sinks)
    return o.reshape(B, T, ATTN_WIDTH), k, v

def _attn_sample(q, k, v, cache_k, cache_v, sinks):
    DB, T = q.shape[:2]
    L = cache_k.shape[1]
    pos = PAST_LEN + jnp.arange(T, dtype=jnp.int32)
    q = _rope(q, pos)
    k = _rope(k, pos)
    k_all = jnp.concatenate([cache_k, k], axis=1)
    v_all = jnp.concatenate([cache_v, v], axis=1)
    k_pos = jnp.concatenate([PAST_LEN - L + jnp.arange(L, dtype=jnp.int32), pos])[None]
    q_pos = pos[None]
    qg = q.reshape(DB, T, N_KV_HEADS, Q_GROUP, HEAD_DIM)
    o = _sink_attention(qg, k_all, v_all, q_pos, k_pos, sinks)
    return o.reshape(DB, T, ATTN_WIDTH), k_all[:, -L:], v_all[:, -L:]

def _pool_mix(u_all, n_hist, first_pos, w_pool, pool_scale):
    B, L, _ = u_all.shape
    T = L - n_hist
    uf = u_all.astype(jnp.float32)
    cs = jnp.pad(jnp.cumsum(uf, axis=1), ((0, 0), (1, 0), (0, 0)))
    pos = first_pos + jnp.arange(T, dtype=jnp.int32)
    outs = []
    for g, w in enumerate(POOL_WINDOWS):
        lo, hi = g * POOL_GROUP, (g + 1) * POOL_GROUP
        ext = jnp.pad(cs[..., lo:hi], ((0, 0), (w - 1, 0), (0, 0)))
        wsum = ext[:, n_hist + w:L + w] - ext[:, n_hist:L]
        cnt = jnp.minimum(w, pos + 1).astype(jnp.float32)[None, :, None]
        outs.append(wsum / cnt - uf[:, n_hist:, lo:hi])
    d = jnp.stack(outs, axis=2).astype(u_all.dtype)
    y = jnp.einsum('btgc,gce->btge', d, w_pool) * pool_scale
    return y.reshape(B, T, D_MODEL)

def _merge(pool_br, attn_heads, g_pool, g_attn, w_attn_br, w_out):
    attn_br = jnp.einsum('bta,ad->btd', attn_heads, w_attn_br)
    m = jax.nn.sigmoid(g_pool) * pool_br + jax.nn.sigmoid(g_attn) * attn_br
    return jnp.einsum('btd,de->bte', m, w_out)

def _peer(h, w_query, sub_keys, peer_u, peer_v):
    shp = h.shape
    hf = h.reshape(-1, D_MODEL)
    n = hf.shape[0]
    n_chunks = -(-n // PEER_CHUNK)
    pad = n_chunks * PEER_CHUNK - n
    hp = jnp.pad(hf, ((0, pad), (0, 0))).reshape(n_chunks, PEER_CHUNK, D_MODEL)

    def chunk(xc):
        q = (xc @ w_query).reshape(PEER_CHUNK, PEER_HEADS, 2, HALF_KEY)
        s = jnp.einsum('chpe,hpne->chpn', q, sub_keys).astype(jnp.float32)
        ts, ti = lax.top_k(s, PEER_TOPK)
        cand = ts[:, :, 0, :, None] + ts[:, :, 1, None, :]
        cs, ci = lax.top_k(cand.reshape(PEER_CHUNK, PEER_HEADS, PEER_TOPK * PEER_TOPK), PEER_TOPK)
        i1 = jnp.take_along_axis(ti[:, :, 0], ci // PEER_TOPK, axis=-1)
        i2 = jnp.take_along_axis(ti[:, :, 1], ci % PEER_TOPK, axis=-1)
        idx = i1 * N_KEYS + i2
        gate = jax.nn.softmax(cs, axis=-1)
        a = jnp.einsum('cd,chkd->chk', xc, peer_u[idx])
        act = (jax.nn.gelu(a.astype(jnp.float32), approximate=False) * gate).astype(xc.dtype)
        return jnp.einsum('chk,chkd->cd', act, peer_v[idx])

    out = lax.map(chunk, hp).reshape(-1, D_MODEL)[:n]
    return out.reshape(shp)

def _post_norm_block(x, tok, ln1_g, ln1_b, w_query, sub_keys, peer_u, peer_v, ln2_g, ln2_b):
    h = _layer_norm(ALPHA * x + tok, ln1_g, ln1_b)
    return _layer_norm(ALPHA * h + _peer(h, w_query, sub_keys, peer_u, peer_v), ln2_g, ln2_b)

def setup_inputs(seed: int = 0) -> dict:
    key = jax.random.key(seed)
    ks = jax.random.split(key, 24)
    f32 = jnp.float32
    buf = min(WINDOW, PAST_LEN)
    nrm = lambda k, shape, scale: jax.random.normal(k, shape, f32) * scale
    return {
        'x_prompt': nrm(ks[0], (BATCH, SEQ, D_MODEL), 1.0),
        'x_sample': nrm(ks[1], (DEC_BATCH, DEC_SEQ, D_MODEL), 1.0),
        'cache_k': nrm(ks[2], (DEC_BATCH, buf, N_KV_HEADS, HEAD_DIM), 1.0),
        'cache_v': nrm(ks[3], (DEC_BATCH, buf, N_KV_HEADS, HEAD_DIM), 1.0),
        'state_pool': nrm(ks[4], (DEC_BATCH, POOL_HIST, POOL_WIDTH), 1.0),
        'w_in': nrm(ks[5], (D_MODEL, IN_WIDTH), D_MODEL ** -0.5),
        'b_in': nrm(ks[6], (IN_WIDTH,), 0.02),
        'attn_sinks': nrm(ks[7], (N_HEADS,), 0.5),
        'w_attn_br': nrm(ks[8], (ATTN_WIDTH, D_MODEL), ATTN_WIDTH ** -0.5),
        'w_pool': nrm(ks[9], (N_POOL_GROUPS, POOL_GROUP, POOL_OUT_GROUP), POOL_GROUP ** -0.5),
        'pool_scale': 1.0 + nrm(ks[10], (N_POOL_GROUPS, POOL_OUT_GROUP), 0.1),
        'w_out': nrm(ks[11], (D_MODEL, D_MODEL), BETA * D_MODEL ** -0.5),
        'ln1_g': 1.0 + nrm(ks[12], (D_MODEL,), 0.02),
        'ln1_b': nrm(ks[13], (D_MODEL,), 0.02),
        'w_query': nrm(ks[14], (D_MODEL, PEER_HEADS * D_KEY), D_MODEL ** -0.5),
        'sub_keys': nrm(ks[15], (PEER_HEADS, 2, N_KEYS, HALF_KEY), HALF_KEY ** -0.5),
        'peer_u': nrm(ks[16], (N_EXPERTS, D_MODEL), D_MODEL ** -0.5),
        'peer_v': nrm(ks[17], (N_EXPERTS, D_MODEL), BETA),
        'ln2_g': 1.0 + nrm(ks[18], (D_MODEL,), 0.02),
        'ln2_b': nrm(ks[19], (D_MODEL,), 0.02),
    }

def reference(x_prompt, x_sample, cache_k, cache_v, state_pool, w_in, b_in, attn_sinks, w_attn_br,
              w_pool, pool_scale, w_out, ln1_g, ln1_b, w_query, sub_keys, peer_u, peer_v, ln2_g, ln2_b):
    x = x_prompt
    for _ in range(DEPTH):
        q, k, v, u, g_pool, g_attn = _in_proj(x, w_in, b_in)
        attn_p, k_rot, v_p = _attn_prompt(q, k, v, attn_sinks)
        pool_p = _pool_mix(u, 0, 0, w_pool, pool_scale)
        tok = _merge(pool_p, attn_p, g_pool, g_attn, w_attn_br, w_out)
        x = _post_norm_block(x, tok, ln1_g, ln1_b, w_query, sub_keys, peer_u, peer_v, ln2_g, ln2_b)
        L_p = min(WINDOW, x.shape[1])
        k_win_prompt = k_rot[:, -L_p:]
        v_win_prompt = v_p[:, -L_p:]
        pool_hist_prompt = u[:, -POOL_HIST:]
    y_prompt = x

    x = x_sample
    for _ in range(DEPTH):
        q, k, v, u, g_pool, g_attn = _in_proj(x, w_in, b_in)
        attn_s, k_win_sample, v_win_sample = _attn_sample(q, k, v, cache_k, cache_v, attn_sinks)
        u_all = jnp.concatenate([state_pool, u], axis=1)
        pool_s = _pool_mix(u_all, state_pool.shape[1], PAST_LEN, w_pool, pool_scale)
        tok = _merge(pool_s, attn_s, g_pool, g_attn, w_attn_br, w_out)
        x = _post_norm_block(x, tok, ln1_g, ln1_b, w_query, sub_keys, peer_u, peer_v, ln2_g, ln2_b)
        pool_hist_sample = u_all[:, -POOL_HIST:]
    y_sample = x

    return (y_prompt, y_sample, k_win_prompt, v_win_prompt, pool_hist_prompt, k_win_sample, v_win_sample, pool_hist_sample)


_drawn_inputs = setup_inputs


def setup_inputs(seed=0):
    import zlib

    import numpy as np

    out = dict(_drawn_inputs(seed))
    spreads = {}
    factors = {'b_in': 2.763, 'attn_sinks': 8.0, 'ln2_g': 2.841, 'ln2_b': 2.912}
    for name, (base, spread) in spreads.items():
        noise = np.random.default_rng([zlib.crc32(name.encode()), seed]).standard_normal(out[name].shape)
        drawn = base * np.exp(spread * noise) if base else spread * noise
        out[name] = __import__('jax').numpy.asarray(drawn.astype(out[name].dtype))
    for name, factor in factors.items():
        out[name] = (out[name] * factor).astype(out[name].dtype)
    return out
```

```python
from contextlib import ExitStack

import numpy as np

import concourse.bass as bass
from concourse import mybir

F32 = mybir.dt.float32
F32R = mybir.dt.float32r
U32 = mybir.dt.uint32
ALU = mybir.AluOpType
ACT = mybir.ActivationFunctionType
AX_X = mybir.AxisListType.X

P = 128
D = 2048
SEQ = 256
DB, DS = 8, 4
NS = DB * DS
T = SEQ + NS
PAST = 2048
HEADS, KVH, HD = 16, 4, 64
QG = HEADS // KVH
AW, KW = HEADS * HD, KVH * HD
WIN = 128
PW = D // 2
HIST = 15
PG = 4
PH, NK, HK, TOPK = 8, 128, 128, 16
ALPHA = 2.0 ** 0.25
EPS = 1e-5
NEG = -1e30
SCALE = HD ** -0.5
KT = D // P
HU = KT * P // 2
CH = 3
NHALF = 2 * PH

PHASES = {"u": (8, 1), "kv": (4, 1), "q": (8, 1), "gates": (32, 1), "pool": (2, 8), "attn": (8, 2),
          "out": (16, 1), "query": (16, 1), "peer_u": (128, 1), "peer_v": (128, 2)}
UNIT0, OUT0 = {}, {}
_u = _o = 0
for _name, (_n, _k) in PHASES.items():
    UNIT0[_name], OUT0[_name] = _u, _o
    _u += _n
    _o += _n * _k
UNITS = _u
ACT_EV0 = {"u": 0, "kv": 8, "q": 12, "gates": 20, "query": 52, "peer_u": 68}
DVE_EV0 = {"pool": 0, "attn": 16, "out": 32, "peer_v": 48}

SAMPLE_UNITS = 8
HEAD_UNITS = (32 - SAMPLE_UNITS) // QG
BLOCKS = 16
BEFORE, WITH = 5, 9
TOKS = T // (WITH * 8)
TG = TOKS * 8

CONST = {}
_c = 0
for _name, _n in (("ident", 128), ("cos", T), ("sin", T), ("mask", 2 * WIN), ("smask", WIN + NS),
                  ("ratio", PG * 16), ("iota", 128)):
    CONST[_name] = (_c, _c + _n)
    _c += _n
CONSTS = _c
VEC = {}
_c = 0
for _name, _n in (("b_in", 52), ("scale", 16), ("sink", 16), ("ssink", 4), ("g1", 16), ("b1", 16),
                  ("g2", 16), ("b2", 16)):
    VEC[_name] = (_c, _c + _n)
    _c += _n
VECS = _c


def const_table():
    t = np.zeros((P, CONSTS), np.float32)

    def put(name, a):
        t[:, CONST[name][0]:CONST[name][1]] = a

    put("ident", np.eye(P))
    half = HD // 2
    inv = np.float32(10000.0) ** (-np.arange(half, dtype=np.float32) / np.float32(half))
    pos = np.concatenate([np.arange(SEQ), PAST + np.tile(np.arange(DS), DB)]).astype(np.float32)
    ang = (pos[None, :] * inv.astype(np.float32)[:, None]).astype(np.float32)
    put("cos", np.tile(np.cos(ang), (4, 1)))
    put("sin", np.tile(np.sin(ang), (4, 1)))
    i, j = np.arange(P)[:, None], np.arange(2 * WIN)[None, :]
    put("mask", np.where((j <= WIN + i) & (j > i), 0.0, NEG))
    row = np.arange(P)[:, None]
    b, i = row % NS // DS, row % DS
    j = np.arange(WIN)[None, :]
    new = np.arange(NS)[None, :]
    put("smask", np.concatenate([np.where(j > i, 0.0, NEG),
                                 np.where((new // DS == b) & (new % DS <= i), 0.0, NEG)], 1))
    w = np.array([2, 4, 8, 16])[:, None]
    put("ratio", (w / np.minimum(w, np.arange(16)[None, :] + 1)).astype(np.float32).reshape(1, -1))
    put("iota", np.arange(128)[None, :])
    return t


class Tally:

    def __init__(self, sem):
        self.sem, self.base, self.k = sem, 0, 0

    def inc(self, instruction):
        instruction.then_inc(self.sem, 1)
        self.k += 1
        return self.base + self.k

    def start(self, i, per):
        self.saved, self.per = self.k, per
        self.base, self.k = self.saved + i * per, 0

    def stop(self, n):
        assert self.k == self.per, (self.k, self.per)
        self.base, self.k = 0, self.saved + n * self.per


def layer(nc, xT, w_in, w_pool, w_attn, w_out, w_query, keysT, peer_u, peer_v, vecs, consts,
          kcT, vc, stT, k_nat, st_nat,
          yT, kT, vT, uT, us, k_shift, v_shift, st_shift):
    ctx = ExitStack()
    with ctx:
        def sb(name, shape, dt=F32):
            return ctx.enter_context(nc.sbuf_tensor(name, shape, dt))

        def sem(name):
            return ctx.enter_context(nc.semaphore(name))

        a_dram = nc.dram_tensor("gelu_scratch", (2 * BLOCKS, P, 4 * T), F32, kind="Internal").ap()
        g_dram = nc.dram_tensor("gate_scratch", (WITH, P, P, TG), F32, kind="Internal").ap()

        raw = sb("raw", [P, 2, KT * P])
        wh = sb("w_hi", [P, 2, KT * P], F32R)
        wl = sb("w_lo", [P, 2, KT * P], F32R)
        R = sb("R", [P, KT, T])
        bh = sb("b_hi", [P, KT, T], F32R)
        bl = sb("b_lo", [P, KT, T], F32R)
        vec = sb("vec", [P, VECS])
        cst = sb("cst", [P, CONSTS])
        ones = sb("ones", [P, P])
        tiny = sb("tiny", [P, 2])
        ah = sb("a_hi", [P, KT, T], F32R)
        with nc.sbuf_tensor("a_lo", [P, KT, T], F32R) as al:
            pass
        with (nc.sbuf_tensor("g_stage", [P, P, TG], F32) as gs,
              nc.sbuf_tensor("gate_T", [P, T], F32) as gT):
            pass
        sb("a_lo_space", [P, KT, T])
        F = sb("F", [P, (212863 - 4 * (6 * KT * P + 5 * KT * T + VECS + CONSTS + P)) // 4 - 64])

        def carve(off, *shape):
            n = int(np.prod(shape))
            assert off + n <= F.shape[1], (off, shape, F.shape)
            ap = F[:, off:off + n]
            names = "abcd"[:len(shape)]
            if len(shape) > 1:
                ap = ap.rearrange(f"p ({' '.join(names)}) -> p {' '.join(names)}",
                                  **dict(zip(names, shape)))
            return ap, off + n

        GG, o_front = carve(0, 32, T)
        UP, o = carve(o_front, 8, 16 + SEQ)
        US, o = carve(o, 8, DB, 20)
        PT = []
        for _ in range(2):
            t1, o = carve(o, 2, 16 + SEQ)
            t2, o = carve(o, 2, DB, 20)
            PT.append((t1, t2))
        PD, o = carve(o, 2, T)
        QK = R[:, 0:8, :]
        K2 = R[:, 8:10, :]
        V2 = R[:, 10:12, :]
        RT = [R[:, 12:16, :], None]
        RT[1], _ = carve(o_front + 8 * (16 + SEQ) + 8 * DB * 20, 4, T)
        KC, o = carve(o_front, 2, DB, P)
        VC, o = carve(o, DB, KW)
        CS, o2 = carve(o_front + 2 * DB * P + DB * KW, 4, P)
        SM, o2 = carve(o2, 4, 2 * WIN)
        VN, o2 = carve(o2, 2, KW)
        VS, o2 = carve(o2, KW)
        SX, o2 = carve(o2, 4, 8)
        QW, o2 = carve(o2, 2, QG, NS)
        PS, o = carve(o_front, 2, 4, P)
        QS, o = carve(o, 2, T)
        SP_, o = carve(o, 4, 2 * WIN)
        SQ = GG[:, 0:16, :]
        MEAN, VAR, RSTD, TMP = (GG[:, 16 + n, :] for n in range(4))
        ST, o_st = carve(0, 2, 4, T)
        SK, o = carve(0, NHALF, P)
        QT, o = carve(o, 2, T)
        SC, o = carve(o, CH, NHALF, P)
        TV, o = carve(o, CH, NHALF, TOPK)
        TI, o = carve(o, CH, NHALF, TOPK)
        CV, o = carve(o, CH, PH, TOPK)
        CI, o = carve(o, CH, PH, TOPK)
        LS, o = carve(o, CH, TOPK * TOPK)
        LV, o = carve(o, CH, TOPK)
        LI, o = carve(o, CH, TOPK)
        X1, o = carve(o, CH, PH, TOPK)
        X2, o = carve(o, CH, PH, TOPK)
        GA, o = carve(o, CH, PH, TOPK)
        I1, o = carve(o, CH, PH, TOPK)
        I2, o = carve(o, CH, PH, TOPK)
        CS1, o = carve(o, CH, PH, 1)
        E4, _ = carve(o, PH * TOPK, TOPK)
        AB, o_ab = carve(o_st, 2, 8, T)
        GB, o_ab = carve(o_ab, 2, WITH, 8 * TG)
        OH, o_ab = carve(o_ab, 2, 2, TOKS, P)
        I1T, o_ab = carve(max(o, o_ab), T)
        I2T, o_ab = carve(o_ab, T)

        ps = ctx.enter_context(nc.psum_tensor("ps", [P, 8, 512], F32))
        SB4 = ps[:, 2:6, :]
        TB = ps[:, 6, :]
        OB = ps[:, 7, :]
        HO = (OB, ps[:, 3, :])
        ident = cst[:, CONST["ident"][0]:CONST["ident"][1]]

        def C(name):
            return cst[:, CONST[name][0]:CONST[name][1]]

        def V(name):
            return vec[:, VEC[name][0]:VEC[name][1]]

        loaded = [sem(f"half_loaded_{n}") for n in range(4)]
        hi_ready, lo_ready = sem("hi_ready"), sem("lo_ready")
        outs_done = sem("outs_done")
        ev_act, ev_dve = sem("evicted_by_act"), sem("evicted_by_dve")
        x_loaded = [sem(f"x_loaded_{n}") for n in range(4)]
        x_hi, x_lo = sem("x_hi_ready"), sem("x_lo_ready")
        consts_in, caches_in, state_in, keys_in, x_again = (
            sem(n) for n in ("consts_in", "caches_in", "state_in", "keys_in", "x_again"))
        d_split, k_rope, q_rope = sem("pooled_split"), sem("k_rotated"), sem("q_rotated")
        q_side = sem("sample_q_side_by_side")
        dve = sem("dve_order")
        v_turned, v_copied = sem("v_turned"), sem("v_copied")
        sc_cache, sc_copied, sc_turned = sem("s_cache_scores"), sem("s_scores_copied"), sem("s_scores_turned")
        s_sm, s_exp, s_prob = sem("s_shifted"), sem("s_exp"), sem("s_probs")
        s_pt, s_ptc, s_pv, s_oh, s_ol = (sem(n) for n in (
            "s_probs_turned", "s_probs_copied", "s_pv", "s_o_hi", "s_o_lo"))
        h_q, h_scores, h_masked, h_sm, h_exp, h_prob = (sem(n) for n in (
            "h_q_staged", "h_scores", "h_masked", "h_shifted", "h_exp", "h_probs"))
        h_pt, h_ptc, h_pv, h_oh, h_ol = (sem(n) for n in (
            "h_probs_turned", "h_probs_copied", "h_pv", "h_o_hi", "h_o_lo"))
        m_split = sem("merged_split")
        ln_pe, ln_act, ln_dve, n_aff, n_hi, n_lo = (sem(n) for n in (
            "ln_pe", "ln_act", "ln_dve", "ln_affine", "h_hi", "h_lo"))
        ln_scaled = sem("ln_scaled")
        sc_ev = sem("key_scores_copied")
        r_pe, r_exp_in, r_exp, r_idx, r_turned = (sem(n) for n in (
            "route_pe", "route_shifted", "route_exp", "route_choices", "route_turned"))
        oh_ready, g_ev, g_stored = sem("onehots_ready"), sem("gates_evicted"), sem("gates_stored")
        a_stored = [sem("gelu_stored_0"), sem("gelu_stored_1")]
        blk_in = [sem("block_in_0"), sem("block_in_1")]
        act_ready, y_init = sem("gated_ready"), sem("y_init")
        stored, u_stored, kv_stored = sem("outputs_stored"), sem("u_stored"), sem("kv_stored")
        ones_set = sem("ones_set")

        block = ctx.enter_context(nc.Block())

        def bc(ap, axis, n):
            a = ap.unsqueeze(axis)
            shape = list(a.shape)
            shape[axis] = n
            return a.broadcast_to(shape)

        def block_dma(sp, b, s):
            sp.dma_start(AB[:, s, :, :].rearrange("p (h e) t -> p h (e t)", h=2),
                         a_dram[bass.ds(2 * b, 2)].rearrange("h p n -> p h n")).then_inc(blk_in[s], 16)
            sp.dma_start(GB[:, s, :, :],
                         g_dram[:, :, bass.ds(8 * b, 8), :].rearrange("w p e t -> p w (e t)"))\
                .then_inc(blk_in[s], 16)

        def load_block(sp, b):
            if b == 0:
                sp.wait_ge(g_stored, 16 * WITH + 1)
                for n in range(2):
                    sp.wait_ge(a_stored[n], 33)
            block_dma(sp, b, b)

        def o_tiles(t, m, c):
            return t[:, 8:16, c * P:c * P + P].rearrange("p (a b) t -> p a b t", a=2)[
                :, :, bass.ds(m, 1), :].rearrange("p a b t -> p a (b t)")

        def norm_act(act, n):
            g, b = (V("g1"), V("b1")) if n == 0 else (V("g2"), V("b2"))
            act.wait_ge(ln_pe, 2 * n + 1)
            act.activation(MEAN, TB[:, 0:T], ACT.Copy, scale=1.0 / D).then_inc(ln_act, 1)
            for e in range(KT):
                act.wait_ge(ln_dve, KT * n + e + 1)
                act.activation(SQ[:, e, :], R[:, e, :], ACT.Square).then_inc(ln_act, 1)
            act.wait_ge(ln_pe, 2 * n + 2)
            act.activation(TMP, OB[:, 0:T], ACT.Copy, scale=1.0 / D, bias=EPS).then_inc(ln_act, 1)
            act.wait_ge(ln_act, (KT + 3) * n + KT + 2)
            act.activation(VAR, TMP, ACT.Sqrt).then_inc(ln_act, 1)
            for e in range(KT):
                act.wait_ge(ln_scaled, KT * n + e + 1)
                act.activation(R[:, e, :], R[:, e, :], ACT.Identity, scale=g[:, e:e + 1],
                               bias=b[:, e:e + 1]).then_inc(n_aff, 1)

        def norm_dve(ve, link, n):
            ve.wait_ge(ln_act, (KT + 3) * n + 1)
            for e in range(KT):
                ve.tensor_tensor(R[:, e, :], R[:, e, :], MEAN, ALU.subtract).then_inc(ln_dve, 1)
            ve.wait_ge(ln_act, (KT + 3) * (n + 1))
            link(ve.reciprocal(RSTD, VAR))
            link(ve.tensor_tensor(VAR, RSTD, RSTD, ALU.mult))
            link(ve.tensor_tensor(VAR, VAR, TMP, ALU.mult))
            link(ve.tensor_scalar(VAR, VAR, -0.5, 1.5, ALU.mult, ALU.add))
            link(ve.tensor_tensor(RSTD, RSTD, VAR, ALU.mult))
            for e in range(KT):
                ve.tensor_tensor(R[:, e, :], R[:, e, :], RSTD, ALU.mult).then_inc(ln_scaled, 1)

        def values(pe, c, probs):
            for g in range(KVH):
                r = slice(64 * (g % 2), 64 * (g % 2) + 64)
                out = HO[c][r, P * (g // 2):P * (g // 2) + P]
                for kb, pr in enumerate(probs):
                    last = pe.matmul(out, VN[:, kb, g * HD:g * HD + HD], pr[:, g, :],
                                     start=(kb == 0), stop=(kb == len(probs) - 1))
            return last


        @block.sync
        def _(sp):
            def load(src, u0, i, j, wait=True):
                for h in range(2):
                    if wait:
                        sp.wait_ge(lo_ready, 2 * (u0 + j) + h - 3 + i * 4)
                    sp.dma_start(raw[:, j % 2, h * HU:h * HU + HU], src[:, h * HU:h * HU + HU])\
                        .then_inc(loaded[2 * (j % 2) + h], 16)

            def stream(src, u0, n, first=0):
                with sp.Fori(0, n // 2) as i:
                    for j in range(2):
                        load(src[first + 2 * i + j], u0, i, j)

            for n in range(4):
                sp.dma_start(R[:, 4 * n:4 * n + 4, :], xT[:, 4 * n:4 * n + 4, :]).then_inc(x_loaded[n], 16)
                if n < 2:
                    load(w_in[n], 0, 0, n, wait=False)
            sp.dma_start(UP[:, :, 0:16], stT[:, 0:8, 0:16]).then_inc(state_in, 16)
            sp.dma_start(US[:, :, :, 0:16], stT[:, :, 16:16 + DB * 16].rearrange("p a (b s) -> p a b s", b=DB))\
                .then_inc(state_in, 16)
            stream(w_in, 2, 20, first=2)
            sp.wait_ge(d_split, PG)
            sp.wait_ge(u_stored, 32)
            sp.wait_ge(q_rope, 1)
            sp.dma_start(KC, kcT).then_inc(caches_in, 16)
            sp.dma_start(VC, vc).then_inc(caches_in, 16)
            stream(w_in, 22, 30, first=22)
            for n in range(2):
                load(w_pool[n], UNIT0["pool"], 0, n)
            stream(w_attn, UNIT0["attn"], 8)
            sp.wait_ge(h_pv, 2 * QG)
            sp.wait_ge(kv_stored, 32)
            sp.dma_start(R[:, :, :], xT).then_inc(x_again, 16)
            stream(w_out, UNIT0["out"], 16)
            stream(w_query, UNIT0["query"], 2)
            sp.wait_ge(n_lo, KT)
            sp.dma_start(SK, keysT).then_inc(keys_in, 16)
            stream(w_query, UNIT0["query"] + 2, 14, first=2)
            stream(peer_u, UNIT0["peer_u"], (BLOCKS - 1) * 8)
            load_block(sp, 0)
            load_block(sp, 1)
            stream(peer_u, UNIT0["peer_u"] + (BLOCKS - 1) * 8, 8, first=(BLOCKS - 1) * 8)
            with sp.Fori(0, BLOCKS // 2 - 1) as i:
                for s in range(2):
                    sp.wait_ge(act_ready, 8 * (2 * i + s + 1))
                    for n in range(2):
                        sp.wait_ge(a_stored[n], 16 * (2 * i + s + 3) + 1)
                    block_dma(sp, 2 * i + s + 2, s)
                    for j in range(8):
                        load(peer_v[16 * i + 8 * s + j], UNIT0["peer_v"] + 8 * s, 8 * i, j)
            stream(peer_v, UNIT0["peer_v"] + 112, 16, first=112)
            sp.wait_ge(stored, 16 * (3 + KT))

        @block.gpsimd
        def _(pool):
            with pool.Fori(0, UNITS // 2) as i:
                for j in range(2):
                    for h in range(2):
                        pool.wait_ge(hi_ready, 4 * i + 2 * j + h + 1)
                        s = slice(h * HU, h * HU + HU)
                        pool.tensor_tensor(wl[:, j, s], raw[:, j, s], wh[:, j, s].bitcast(F32),
                                           ALU.subtract).then_inc(lo_ready, 1)

        @block.scalar
        def _(act):

            def hi(phase, i, j):
                units, per = PHASES[phase]
                act.wait_ge(outs_done, OUT0[phase] + (i + j) * per + 1)
                k = (j + 1) % 2
                for h in range(2):
                    act.wait_ge(loaded[2 * k + h], 16 * (UNIT0[phase] // 2 + (j + 1) // 2 + 1) + i * 8)
                    s = slice(h * HU, h * HU + HU)
                    act.activation(wh[:, k, s], raw[:, k, s], ACT.Copy).then_inc(hi_ready, 1)

            def wait_out(phase, n):
                act.wait_ge(outs_done, OUT0[phase] + n + 2)

            def units(phase, n, first, body, step=2, skip_last=False):
                with act.Fori(0, n // step) as i:
                    for j in range(step):
                        hi(phase, first + step * i, j)
                        body(first + step * i, j)

            for s in (h_ptc, g_stored, *a_stored):
                act.sem_inc(s, 1)
            act.dma_start(vec[:, :], vecs).then_inc(consts_in, 16)
            act.dma_start(cst[:, :], consts).then_inc(consts_in, 16)
            for n in range(4):
                act.wait_ge(x_loaded[n], 16)
                act.activation(ah[:, 4 * n:4 * n + 4, :], R[:, 4 * n:4 * n + 4, :], ACT.Copy).then_inc(x_hi, 1)
                if n == 0:
                    for h in range(2):
                        act.wait_ge(loaded[h], 16)
                        s = slice(h * HU, h * HU + HU)
                        act.activation(wh[:, 0, s], raw[:, 0, s], ACT.Copy).then_inc(hi_ready, 1)
            act.wait_ge(consts_in, 32)

            def ev_u(i, j):
                wait_out("u", i + j)
                bias = V("b_in")[:, bass.ds(i + j, 1)]
                act.activation(UP[:, bass.ds(i + j, 1), 16:16 + SEQ], ps[:, j:j + 1, 0:SEQ], ACT.Identity, bias=bias)
                act.activation(US[:, bass.ds(i + j, 1), :, 16:20].rearrange("p a b s -> p (a b) s"),
                               ps[:, j, SEQ:T].rearrange("p (b s) -> p b s", b=DB),
                               ACT.Identity, bias=bias).then_inc(ev_act, 1)

            act.wait_ge(state_in, 32)
            units("u", 8, 0, ev_u)
            act.wait_ge(ev_act, 8)
            act.dma_start(uT, UP[:, :, 16 + SEQ - HIST:]).then_inc(u_stored, 16)
            act.dma_start(us, US[:, :, :, 16:20]).then_inc(u_stored, 16)
            act.wait_ge(x_lo, 4)

            def ev_kv(i, j):
                wait_out("kv", i + j)
                act.activation(R[:, bass.ds(8 + i + j, 1), :], ps[:, j:j + 1, 0:T], ACT.Identity,
                               bias=V("b_in")[:, bass.ds(8 + i + j, 1)]).then_inc(ev_act, 1)

            def ev_q(i, j):
                wait_out("q", i + j)
                act.activation(R[:, bass.ds(i + j, 1), :], ps[:, j:j + 1, 0:T], ACT.Identity,
                               bias=V("b_in")[:, bass.ds(12 + i + j, 1)]).then_inc(ev_act, 1)

            def ev_gate(i, j):
                wait_out("gates", i + j)
                act.activation(GG[:, bass.ds(i + j, 1), :], ps[:, j % 2:j % 2 + 1, 0:T], ACT.Sigmoid,
                               bias=V("b_in")[:, bass.ds(20 + i + j, 1)]).then_inc(ev_act, 1)

            units("kv", 4, 0, ev_kv)
            units("q", 8, 0, ev_q)
            act.wait_ge(k_rope, 1)
            act.dma_start(kT, K2).then_inc(kv_stored, 16)
            act.dma_start(vT, V2).then_inc(kv_stored, 16)
            act.dma_start(k_shift, k_nat[:, DS:, :]).then_inc(stored, 16)
            act.dma_start(v_shift, vc[DS:, :, :]).then_inc(stored, 16)
            act.dma_start(st_shift, st_nat[:, DS:, :]).then_inc(stored, 16)

            for j in range(SAMPLE_UNITS):
                if j == 0:
                    act.wait_ge(v_turned, 1)
                    act.wait_ge(d_split, PG)
                    act.activation(VN, TB.rearrange("p (a b) -> p a b", a=2), ACT.Copy).then_inc(v_copied, 1)
                    act.activation(VS[0:NS, :], OB[0:NS, 0:KW], ACT.Copy).then_inc(v_copied, 1)
                if j == 2:
                    act.wait_ge(sc_cache, 1)
                    act.activation(CS, SB4[:, :, 0:P], ACT.Copy).then_inc(sc_copied, 1)
                if j == 4:
                    act.wait_ge(s_sm, 2)
                    act.activation(SM[:, :, 0:WIN + NS], SM[:, :, 0:WIN + NS], ACT.Exp).then_inc(s_exp, 1)
                    act.activation(SX[:, 1, 0:4], SX[:, 1, 0:4], ACT.Exp).then_inc(s_exp, 1)
                if j == 5:
                    act.wait_ge(s_pt, 1)
                    act.activation(CS, TB.rearrange("p (a b) -> p a b", a=4), ACT.Copy).then_inc(s_ptc, 1)
                    act.activation(SM[0:NS, 0:2, :].rearrange("p a b -> p (a b)"),
                                   ps[0:NS, 2, :], ACT.Copy).then_inc(s_ptc, 1)
                if j == 7:
                    act.wait_ge(s_pv, 1)
                    act.activation(bh[:, 8:16, SEQ:T], OB[:, 0:256].rearrange("p (a b) -> p a b", a=8),
                                   ACT.Copy).then_inc(s_oh, 1)
                hi("gates", 0, j)
                ev_gate(0, j)

            with act.Fori(0, QG) as m:
                first = SAMPLE_UNITS + HEAD_UNITS * m
                for j in range(HEAD_UNITS):
                    if j == 1:
                        for c, n in ((0, WIN), (1, 2 * WIN)):
                            buf = SM if c == 0 else SP_
                            act.wait_ge(h_sm, 4 * m + 2 * c + 2)
                            act.activation(buf[:, :, 0:n], buf[:, :, 0:n], ACT.Exp).then_inc(h_exp, 1)
                            act.activation(SX[:, 1, 4 * c:4 * c + 4], SX[:, 1, 4 * c:4 * c + 4],
                                           ACT.Exp).then_inc(h_exp, 1)
                    if j in (3, 4, 5):
                        n = j - 3
                        act.wait_ge(h_pt, 3 * m + n + 1)
                        dst = (CS, PS[:, 0], PS[:, 1])[n]
                        act.activation(dst, TB.rearrange("p (a b) -> p a b", a=4), ACT.Copy).then_inc(h_ptc, 1)
                    hi("gates", first, j)
                    ev_gate(first, j)
                for c in range(2):
                    act.wait_ge(h_pv, 2 * m + c + 1)
                    act.activation(o_tiles(bh, m, c), HO[c][:, 0:256].rearrange("p (a b) -> p a b", a=2),
                                   ACT.Copy).then_inc(h_oh, 1)

            for j in range(2):
                hi("pool", 0, j)
            units("attn", 8, 0, lambda i, j: None)
            units("out", 16, 0, lambda i, j: None)

            norm_act(act, 0)
            for e in range(KT):
                act.wait_ge(n_aff, e + 1)
                act.activation(bh[:, e, :], R[:, e, :], ACT.Copy).then_inc(n_hi, 1)

            def ev_query(i, j):
                wait_out("query", i + j)
                act.activation(QT[:, j, :], ps[:, j, 0:T], ACT.Copy).then_inc(ev_act, 1)

            units("query", 16, 0, ev_query)

            def ev_peer(i, j):
                wait_out("peer_u", 8 * i + j)
                if j % 4 == 0:
                    act.wait_ge(a_stored[j // 4], 16 * i + 1)
                act.activation(ST[:, j // 4, j % 4, :], ps[:, j % 2, 0:T], ACT.Gelu).then_inc(ev_act, 1)

            def store_half(i, half):
                act.wait_ge(ev_act, ACT_EV0["peer_u"] + 8 * i + 4 * half + 4)
                act.dma_start(a_dram[2 * i + half], ST[:, half, :, :].rearrange("p e t -> p (e t)"))\
                    .then_inc(a_stored[half], 16)

            def peer_block(i):
                for j in range(8):
                    hi("peer_u", 8 * i, j)
                    if j == 4:
                        store_half(i, 0)
                    ev_peer(i, j)
                store_half(i, 1)

            act.wait_ge(sc_ev, NHALF + 2)
            with act.Fori(0, 3) as i:
                peer_block(i)
            act.wait_ge(r_exp_in, 1)
            act.activation(CV, CV, ACT.Exp).then_inc(r_exp, 1)
            with act.Fori(3, BEFORE) as i:
                peer_block(i)
            with act.Fori(0, WITH) as i:
                peer_block(BEFORE + i)
                act.wait_ge(g_ev, 8 * i + 9)
                act.dma_start(g_dram[i], gs[:, :, :]).then_inc(g_stored, 16)
            with act.Fori(BEFORE + WITH, BLOCKS) as i:
                peer_block(i)
            with act.Fori(0, 63) as i:
                for j in range(2):
                    hi("peer_v", 2 * i, j)
            hi("peer_v", 126, 0)
            norm_act(act, 1)
            for e in range(KT):
                act.wait_ge(n_aff, KT + e + 1)
                act.dma_start(yT[:, e, :], R[:, e, :]).then_inc(stored, 16)

        @block.vector
        def _(ve):
            own = Tally(dve)

            def link(instruction):
                ve.wait_ge(dve, own.inc(instruction))

            for s in (h_prob, h_ol, g_ev):
                ve.sem_inc(s, 1)
            ve.memset(tiny[:, :], 0.0)
            ve.memset(ones[:, :], 1.0).then_inc(ones_set, 1)
            ve.wait_ge(ones_set, 1)
            for n in range(4):
                ve.wait_ge(x_hi, n + 1)
                s = slice(4 * n, 4 * n + 4)
                ve.tensor_tensor(al[:, s, :], R[:, s, :], ah[:, s, :].bitcast(F32), ALU.subtract).then_inc(x_lo, 1)

            ve.wait_ge(ev_act, 8)
            ve.wait_ge(consts_in, 32)
            ratio = C("ratio").rearrange("p (g s) -> p g s", g=PG)
            for g in range(PG):
                t = slice(2 * g, 2 * g + 2)
                src = (UP[:, t], US[:, t])
                for level in range(g + 1):
                    step = 1 << level
                    lo = 2 * step
                    dst = PT[level % 2]
                    ve.tensor_tensor(dst[0][:, :, lo:], src[0][:, :, lo:], src[0][:, :, lo - step:-step], ALU.add)
                    link(ve.tensor_tensor(dst[1][:, :, :, lo:], src[1][:, :, :, lo:],
                                          src[1][:, :, :, lo - step:-step], ALU.add))
                    src = dst
                link(ve.tensor_tensor(src[0][:, :, 16:32], src[0][:, :, 16:32], bc(ratio[:, g, :], 1, 2), ALU.mult))
                w = 1.0 / (2 << g)
                ve.scalar_tensor_tensor(out=PD[:, :, 0:SEQ], in0=src[0][:, :, 16:], scalar=w,
                                        in1=UP[:, t, 16:], op0=ALU.mult, op1=ALU.subtract)
                for k in range(2):
                    last = ve.scalar_tensor_tensor(
                        out=PD[:, k, SEQ:T].rearrange("p (b s) -> p b s", b=DB), in0=src[1][:, k, :, 16:],
                        scalar=w, in1=US[:, 2 * g + k, :, 16:], op0=ALU.mult, op1=ALU.subtract)
                link(last)
                link(ve.tensor_copy(bh[:, t, :], PD))
                ve.tensor_tensor(bl[:, t, :], PD, bh[:, t, :].bitcast(F32), ALU.subtract).then_inc(d_split, 1)
                ve.wait_ge(d_split, g + 1)

            def rope(a, b, t0, t1, n, done):
                cos, sin = bc(C("cos"), 1, n), bc(C("sin"), 1, n)
                ve.tensor_tensor(t0, b, sin, ALU.mult)
                link(ve.tensor_tensor(t1, a, sin, ALU.mult))
                ve.tensor_tensor(a, a, cos, ALU.mult)
                link(ve.tensor_tensor(b, b, cos, ALU.mult))
                ve.tensor_tensor(a, a, t0, ALU.subtract)
                last = ve.tensor_tensor(b, b, t1, ALU.add)
                last.then_inc(done, 1)

            ve.wait_ge(ev_act, 12)
            rope(K2[:, 0:1], K2[:, 1:2], RT[0][:, 0:1], RT[1][:, 0:1], 1, k_rope)
            ve.wait_ge(ev_act, 20)
            ve.wait_ge(k_rope, 1)
            qp = QK.rearrange("p (m h) t -> p h m t", h=2)
            rope(qp[:, 0], qp[:, 1], RT[0], RT[1], 4, q_rope)

            def softmax(buf, n, sink, x, shifted):
                link(ve.tensor_reduce(SX[:, 0, x], buf[:, :, 0:n], AX_X, ALU.max))
                link(ve.tensor_tensor(SX[:, 0, x], SX[:, 0, x], sink, ALU.max))
                ve.tensor_tensor(SX[:, 1, x], sink, SX[:, 0, x], ALU.subtract).then_inc(shifted, 1)
                ve.tensor_tensor(buf[:, :, 0:n], buf[:, :, 0:n], bc(SX[:, 0, x], 2, n), ALU.subtract)\
                    .then_inc(shifted, 1)

            def divide(buf, n, x, exped, value, done):
                ve.wait_ge(exped, value)
                link(ve.tensor_reduce(SX[:, 2, x], buf[:, :, 0:n], AX_X, ALU.add))
                link(ve.tensor_tensor(SX[:, 2, x], SX[:, 2, x], SX[:, 1, x], ALU.add))
                link(ve.reciprocal(SX[:, 3, x], SX[:, 2, x]))
                ve.tensor_tensor(buf[:, :, 0:n], buf[:, :, 0:n], bc(SX[:, 3, x], 2, n), ALU.mult)\
                    .then_inc(done, 1)

            ve.wait_ge(q_rope, 1)
            for half in range(2):
                last = ve.tensor_copy(QW[:, half], qp[:, half, :, SEQ:T])
            last.then_inc(q_side, 1)

            ve.wait_ge(sc_turned, 1)
            mask = C("smask")
            ve.scalar_tensor_tensor(out=SM[:, :, 0:WIN], in0=TB.rearrange("p (a b) -> p a b", a=4), scalar=SCALE,
                                    in1=bc(mask[:, 0:WIN], 1, 4), op0=ALU.mult, op1=ALU.add)
            link(ve.scalar_tensor_tensor(out=SM[:, :, WIN:WIN + NS], in0=SB4[:, :, 256:256 + NS], scalar=SCALE,
                                         in1=bc(mask[:, WIN:], 1, 4), op0=ALU.mult, op1=ALU.add))
            softmax(SM, WIN + NS, V("ssink"), slice(0, 4), s_sm)
            divide(SM, WIN + NS, slice(0, 4), s_exp, 2, s_prob)
            ve.wait_ge(s_oh, 1)
            ve.tensor_tensor(bl[:, 8:16, SEQ:T], OB[:, 0:256].rearrange("p (a b) -> p a b", a=8),
                             bh[:, 8:16, SEQ:T].bitcast(F32), ALU.subtract).then_inc(s_ol, 1)

            ve.wait_ge(s_ol, 1)
            with ve.Fori(0, QG) as m:
                own.start(m, 2 * 6)
                ve.wait_ge(h_scores, 2 * m + 1)
                ve.tensor_copy(QS, R[:, bass.ds(2 * m, 2), :]).then_inc(h_q, 1)
                sink = V("sink")[:, bass.ds(4 * m, 4)]
                for c, n in ((0, WIN), (1, 2 * WIN)):
                    buf = SM if c == 0 else SP_
                    x = slice(4 * c, 4 * c + 4)
                    ve.wait_ge(h_scores, 2 * m + 3)
                    link(ve.scalar_tensor_tensor(
                        out=buf[:, :, 0:n], in0=SB4[:, :, 0:WIN] if c == 0 else SB4[:, :, WIN:3 * WIN],
                        scalar=SCALE, in1=bc(C("mask")[:, 2 * WIN - n:], 1, 4), op0=ALU.mult, op1=ALU.add))
                    softmax(buf, n, sink, x, h_sm)
                for c, n in ((0, WIN), (1, 2 * WIN)):
                    divide(SM if c == 0 else SP_, n, slice(4 * c, 4 * c + 4), h_exp, 4 * m + 2 * c + 2, h_prob)
                for c in range(2):
                    ve.wait_ge(h_oh, 2 * m + c + 1)
                    ve.tensor_tensor(o_tiles(bl, m, c), HO[c][:, 0:256].rearrange("p (a b) -> p a b", a=2),
                                     o_tiles(bh, m, c).bitcast(F32), ALU.subtract).then_inc(h_ol, 1)
                own.stop(QG)

            for o in range(16):
                ve.wait_ge(outs_done, OUT0["pool"] + o + 2)
                ve.scalar_tensor_tensor(out=GG[:, o, :], in0=ps[:, o % 2, 0:T], scalar=V("scale")[:, o:o + 1],
                                        in1=GG[:, o, :], op0=ALU.mult, op1=ALU.mult).then_inc(ev_dve, 1)
            ve.wait_ge(ev_dve, 16)
            with ve.Fori(0, 8) as i:
                own.start(i, 2 * 2)
                for j in range(2):
                    o = 2 * i + j
                    ve.wait_ge(outs_done, OUT0["attn"] + o + 2)
                    ve.tensor_tensor(GG[:, bass.ds(16 + o, 1), :], ps[:, j:j + 1, 0:T],
                                     GG[:, bass.ds(16 + o, 1), :], ALU.mult).then_inc(ev_dve, 1)
                    ve.wait_ge(ev_dve, DVE_EV0["attn"] + o + 1)
                    link(ve.tensor_tensor(GG[:, bass.ds(o, 1), :], GG[:, bass.ds(16 + o, 1), :],
                                          GG[:, bass.ds(o, 1), :], ALU.add))
                    link(ve.tensor_copy(ah[:, bass.ds(o, 1), :], GG[:, bass.ds(o, 1), :]))
                    ve.tensor_tensor(al[:, bass.ds(o, 1), :], GG[:, bass.ds(o, 1), :],
                                     ah[:, bass.ds(o, 1), :].bitcast(F32), ALU.subtract).then_inc(m_split, 1)
                own.stop(8)

            ve.wait_ge(x_again, 16)
            with ve.Fori(0, 8) as i:
                for j in range(2):
                    o = 2 * i + j
                    ve.wait_ge(outs_done, OUT0["out"] + o + 2)
                    ve.scalar_tensor_tensor(out=R[:, bass.ds(o, 1), :], in0=R[:, bass.ds(o, 1), :], scalar=ALPHA,
                                            in1=ps[:, j:j + 1, 0:T], op0=ALU.mult, op1=ALU.add).then_inc(ev_dve, 1)
            norm_dve(ve, link, 0)
            for e in range(KT):
                ve.wait_ge(n_hi, e + 1)
                ve.tensor_tensor(bl[:, e, :], R[:, e, :], bh[:, e, :].bitcast(F32), ALU.subtract).then_inc(n_lo, 1)

            ve.wait_ge(n_lo, KT)
            ve.tensor_scalar(R[:, :, :], R[:, :, :], ALPHA, None, ALU.mult).then_inc(y_init, 1)
            ve.sem_inc(sc_ev, 1)
            ve.memset(SC[:, 2], 0.0).then_inc(sc_ev, 1)
            ve.wait_ge(sc_ev, 2)
            with ve.Fori(0, NHALF // 2) as i:
                for j in range(2):
                    ve.wait_ge(r_pe, 2 * i + j + 1)
                    ve.tensor_copy(SC[:, 0:2, bass.ds(2 * i + j, 1), :].rearrange("p c a n -> p c (a n)"),
                                   ps[:, 2 + j, 0:256].rearrange("p (c n) -> p c n", c=2))
                    ve.tensor_copy(SC[0:NS, 2, bass.ds(2 * i + j, 1), :], ps[0:NS, 2 + j, 256:384].unsqueeze(1))\
                        .then_inc(sc_ev, 1)
            ve.wait_ge(sc_ev, NHALF + 2)

            def hold(mark):
                ve.wait_ge(dve, mark)
                ve.tensor_copy(tiny[:, 1:2], tiny[:, 0:1])

            def top16(scores, best, index):
                def stage(make):
                    for c in range(CH):
                        mark = own.inc(make(c))
                    return mark

                hold(stage(lambda c: ve.max(best[c][:, 0:8], scores[c])))
                hold(stage(lambda c: ve.max_index(index[c][:, 0:8], best[c][:, 0:8], scores[c])))
                hold(stage(lambda c: ve.match_replace(scores[c], best[c][:, 0:8], scores[c], -3.0e38)))
                hold(stage(lambda c: ve.max(best[c][:, 8:16], scores[c])))
                ve.wait_ge(dve, stage(lambda c: ve.max_index(index[c][:, 8:16], best[c][:, 8:16], scores[c])))

            with ve.Fori(0, NHALF) as i:
                own.start(i, 1 + 15)
                hold(own.inc(ve.tensor_copy(LS[:, :, 0:P],
                                            SC[:, :, bass.ds(i, 1), :].rearrange("p c a n -> p c (a n)"))))
                top16([LS[:, c, 0:P] for c in range(CH)], [LV[:, c, :] for c in range(CH)],
                      [LI[:, c, :].bitcast(U32) for c in range(CH)])
                ve.tensor_copy(TV[:, :, bass.ds(i, 1), :].rearrange("p c a n -> p c (a n)"), LV)
                ve.tensor_copy(TI[:, :, bass.ds(i, 1), :].rearrange("p c a n -> p c (a n)"),
                               LI.bitcast(U32)).then_inc(r_idx, 1)
                ve.wait_ge(r_idx, i + 1)
                own.stop(NHALF)
            with ve.Fori(0, PH) as h:
                own.start(h, CH + 15)
                for c in range(CH):
                    a = TV[:, c, bass.ds(2 * h, 1), :].rearrange("p a n -> p (a n)")
                    b = TV[:, c, bass.ds(2 * h + 1, 1), :].rearrange("p a n -> p (a n)")
                    mark = own.inc(ve.tensor_tensor(LS[:, c, :].rearrange("p (a b) -> p a b", a=16),
                                                    bc(a, 2, 16), bc(b, 1, 16), ALU.add))
                hold(mark)
                top16([LS[:, c, :] for c in range(CH)], [LV[:, c, :] for c in range(CH)],
                      [LI[:, c, :].bitcast(U32) for c in range(CH)])
                ve.tensor_copy(CV[:, :, bass.ds(h, 1), :].rearrange("p c a n -> p c (a n)"), LV)
                ve.tensor_copy(CI[:, :, bass.ds(h, 1), :].rearrange("p c a n -> p c (a n)").bitcast(U32),
                               LI.bitcast(U32)).then_inc(r_idx, 1)
                ve.wait_ge(r_idx, NHALF + h + 1)
                own.stop(PH)

            link(ve.tensor_copy(CS1, CV[:, :, :, 0:1]))
            flat = lambda t: t.rearrange("p c h k -> p (c h) k")
            ve.tensor_tensor(flat(CV), flat(CV), flat(CS1).broadcast_to([P, CH * PH, TOPK]), ALU.subtract)\
                .then_inc(r_exp_in, 1)
            cu = CI.bitcast(U32)
            ve.tensor_scalar(I1.bitcast(U32), cu, 4, None, ALU.logical_shift_right)
            link(ve.tensor_scalar(I2.bitcast(U32), cu, 15, None, ALU.bitwise_and))
            ve.tensor_copy(X1, I1.bitcast(U32))
            link(ve.tensor_copy(X2, I2.bitcast(U32)))
            iota16 = C("iota")[:, 0:16]
            for c in range(CH):
                for half, (x, out) in enumerate(((X1, I1), (X2, I2))):
                    e4 = E4.rearrange("p (h k) j -> p h k j", h=PH)
                    ks = bc(bc(iota16, 1, PH), 2, TOPK)
                    link(ve.tensor_tensor(e4, bc(x[:, c], 3, 16), ks, ALU.is_equal))
                    names = TI[:, c].rearrange("p (h s) j -> p s h j", s=2)[:, half]
                    link(ve.tensor_tensor(e4, e4, bc(names, 2, TOPK), ALU.mult))
                    link(ve.tensor_reduce(out[:, c].rearrange("p h k -> p (h k)"), E4, AX_X, ALU.add))
            ve.wait_ge(r_exp, 1)
            link(ve.tensor_reduce(flat(CS1).rearrange("p a b -> p (a b)"), flat(CV), AX_X, ALU.add))
            link(ve.reciprocal(CS1, CS1))
            ve.tensor_tensor(flat(GA), flat(CV), flat(CS1).broadcast_to([P, CH * PH, TOPK]), ALU.mult)\
                .then_inc(r_idx, 1)
            for n, dst in enumerate((I1T, I2T, gT[:, :])):
                ve.wait_ge(r_pe, NHALF + n + 1)
                link(ve.tensor_copy(dst, ps[:, 4, 0:T] if n == 0 else (ps[:, 5, 0:T] if n == 1 else TB[:, 0:T])))
            iota = C("iota")

            with ve.Fori(0, WITH) as i:
                for j in range(8):
                    n = 8 * i + j
                    ve.wait_ge(r_pe, NHALF + 3 + n - 1)
                    for t in range(TOKS):
                        tok = TG * i + TOKS * j + t
                        ve.tensor_scalar(OH[:, j % 2, 0, t, :], iota, I2T[:, bass.ds(tok, 1)], None, ALU.is_equal)
                        last = ve.tensor_scalar(OH[:, j % 2, 1, t, :], iota, I1T[:, bass.ds(tok, 1)],
                                                gT[:, bass.ds(tok, 1)], ALU.is_equal, ALU.mult)
                    last.then_inc(oh_ready, 1)
                    ve.wait_ge(r_pe, NHALF + 3 + n + 1)
                    if j == 0:
                        ve.wait_ge(g_stored, 16 * i + 1)
                    ve.tensor_copy(gs[:, :, TOKS * j:TOKS * j + TOKS].rearrange("p e t -> p t e"),
                                   ps[:, 2 + j % 2, :].rearrange("p (t e) -> p t e", t=TOKS)).then_inc(g_ev, 1)

            def gate(s, e):
                a = AB[:, s, e, :].rearrange("p (w t) -> p w t", w=WITH)
                g = GB[:, s].rearrange("p w (e t) -> p w e t", e=8)[:, :, e, :]
                link(ve.tensor_tensor(a, a, g, ALU.mult))
                link(ve.tensor_copy(ah[:, 8 * s + e, :], AB[:, s, e, :]))
                ve.tensor_tensor(al[:, 8 * s + e, :], AB[:, s, e, :], ah[:, 8 * s + e, :].bitcast(F32),
                                 ALU.subtract).then_inc(act_ready, 1)

            def take(o, j, i):
                ve.wait_ge(outs_done, OUT0["peer_v"] + i + o + 2)
                ve.tensor_tensor(R[:, j, :], R[:, j, :], ps[:, o % 2, 0:T], ALU.add).then_inc(ev_dve, 1)

            ve.wait_ge(g_ev, 8 * WITH + 1)
            ve.wait_ge(blk_in[0], 32)
            for e in range(8):
                gate(0, e)
            ve.wait_ge(y_init, 1)

            def v_block(i, s, prepare):
                if prepare:
                    ve.wait_ge(blk_in[1 - s], 32 * (i + s + 1))
                    ve.wait_ge(outs_done, OUT0["peer_v"] + 32 * i + 16 * s + 1)
                for u in range(8):
                    if prepare:
                        gate(1 - s, u)
                    for j in range(2):
                        take(16 * s + 2 * u + j, 2 * u + j, 32 * i)

            with ve.Fori(0, BLOCKS // 2 - 1) as i:
                own.start(i, 32)
                for s in range(2):
                    v_block(i, s, True)
                own.stop(BLOCKS // 2 - 1)
            v_block(BLOCKS // 2 - 1, 0, True)
            v_block(BLOCKS // 2 - 1, 1, False)
            norm_dve(ve, link, 1)

        @block.tensor
        def _(pe):
            def product(bank, slot, tiles, mh, ml, u, x_wait=False):
                out = ps[:, bank, 0:T]
                for n, (t, k) in enumerate(tiles):
                    w = wh[:, slot, t * P:t * P + P]
                    if t % 8 == 0:
                        pe.wait_ge(hi_ready, 2 * u + t // 8 + 1)
                    if x_wait and n % 4 == 0:
                        pe.wait_ge(x_lo, n // 4 + 1)
                    pe.matmul(out, w, mh(k), start=(n == 0), stop=False)
                    pe.matmul(out, w, ml(k), start=False, stop=False)
                for n, (t, k) in enumerate(tiles):
                    if t % 8 == 0:
                        pe.wait_ge(lo_ready, 2 * u + t // 8 + 1)
                    last = pe.matmul(out, wl[:, slot, t * P:t * P + P], mh(k), start=False,
                                     stop=(n == len(tiles) - 1))
                last.then_inc(outs_done, 1)

            def a_op(t):
                return lambda k: t[:, k, :]

            FULL = [(k, k) for k in range(KT)]

            def unit(phase, evicted, ev0, i, j, mh, ml, wait=True, x_wait=False):
                if wait:
                    pe.wait_ge(evicted, ev0 + i + j - 1)
                product(j % 2, j % 2, FULL, mh, ml, UNIT0[phase] + i + j, x_wait)

            def units(phase, n, first, evicted, ev0, t, step=2):
                with pe.Fori(0, n // step) as i:
                    for j in range(step):
                        unit(phase, evicted, ev0, first + step * i, j, a_op(t[0]), a_op(t[1]))

            for s in (h_scores, outs_done):
                pe.sem_inc(s, 1)
            x = (ah, al)
            unit("u", ev_act, 0, 0, 0, a_op(ah), a_op(al), wait=False, x_wait=True)
            unit("u", ev_act, 0, 0, 1, a_op(ah), a_op(al), wait=False)
            units("u", 6, 2, ev_act, 0, x)
            units("kv", 4, 0, ev_act, ACT_EV0["kv"], x)
            units("q", 8, 0, ev_act, ACT_EV0["q"], x)

            def gate_unit(first, j):
                unit("gates", ev_act, ACT_EV0["gates"], first, j, a_op(ah), a_op(al))

            pe.wait_ge(ev_act, 12)
            for c in range(2):
                for v in range(2):
                    pe.transpose(TB[:, (2 * c + v) * P:(2 * c + v + 1) * P], V2[:, v, c * P:c * P + P], ident)
            for v in range(2):
                last = pe.transpose(OB[0:NS, v * P:v * P + P], V2[:, v, SEQ:T], ident)
            last.then_inc(v_turned, 1)
            for j in range(SAMPLE_UNITS):
                if j == 2:
                    pe.wait_ge(q_side, 1)
                    pe.wait_ge(caches_in, 32)
                    for b in range(DB):
                        for half in range(2):
                            for g in range(KVH):
                                r = slice(32 * g, 32 * g + 32)
                                out = SB4[:, g, 0:P].rearrange("p (m b i) -> p m b i", m=QG, b=DB)[:, :, b, :]
                                last = pe.matmul(out, KC[r, half, b, :],
                                                 QW[r, half, :, DS * b:DS * b + DS],
                                                 start=(half == 0), stop=(half == 1))
                    last.then_inc(sc_cache, 1)
                if j == 3:
                    pe.wait_ge(sc_copied, 1)
                    pe.wait_ge(v_copied, 2)
                    for g in range(KVH):
                        pe.transpose(TB[:, g * P:g * P + P], CS[:, g, :], ident)
                    for half in range(2):
                        for g in range(KVH):
                            r = slice(32 * g, 32 * g + 32)
                            last = pe.matmul(SB4[:, g, 256:256 + NS], QW[r, half].rearrange("p m t -> p (m t)"),
                                             K2[r, half, SEQ:T], start=(half == 0), stop=(half == 1))
                    last.then_inc(sc_turned, 1)
                if j == 5:
                    pe.wait_ge(s_prob, 1)
                    for g in range(KVH):
                        pe.transpose(TB[:, g * P:g * P + P], SM[:, g, 0:WIN], ident)
                    for g in range(KVH):
                        last = pe.transpose(ps[0:NS, 2, g * P:g * P + P], SM[:, g, WIN:WIN + NS], ident)
                    last.then_inc(s_pt, 1)
                if j == 6:
                    pe.wait_ge(s_ptc, 2)
                    pn = SM[0:NS, 0:2, :].rearrange("p a (b c) -> p (a b) c", b=2)
                    for g in range(KVH):
                        r = slice(64 * (g % 2), 64 * (g % 2) + 64)
                        out = OB[r, P * (g // 2):P * (g // 2) + P]
                        vs = slice(g * HD, g * HD + HD)
                        pe.matmul(out, VS[0:NS, vs], pn[:, g, :], start=True, stop=False)
                        for b in range(DB):
                            cols = out.rearrange("p (m b i) -> p m b i", m=QG, b=DB)[:, :, b, :]
                            pc = CS[:, g, :].rearrange("p (m b i) -> p m b i", m=QG, b=DB)[:, :, b, :]
                            last = pe.matmul(cols, VC[:, b, vs], pc, start=False, stop=(b == DB - 1))
                    last.then_inc(s_pv, 1)
                gate_unit(0, j)

            pe.wait_ge(s_ol, 1)
            with pe.Fori(0, QG) as m:
                first = SAMPLE_UNITS + HEAD_UNITS * m
                for j in range(HEAD_UNITS):
                    if j == 0:
                        pe.wait_ge(h_q, m + 1)
                        pe.wait_ge(h_prob, 2 * m + 1)
                        pe.wait_ge(h_ol, 2 * m + 1)
                        for c in range(2):
                            for half in range(2):
                                for g in range(KVH):
                                    r = slice(32 * g, 32 * g + 32)
                                    out = SB4[:, g, 0:WIN] if c == 0 else SB4[:, g, WIN:3 * WIN]
                                    last = pe.matmul(out, QS[r, half, c * P:c * P + P],
                                                     K2[r, half, 0:WIN * (c + 1)],
                                                     start=(half == 0), stop=(half == 1))
                            last.then_inc(h_scores, 1)
                    if j in (3, 4, 5):
                        n = j - 3
                        c, kb = ((0, 0), (1, 0), (1, 1))[n]
                        pe.wait_ge(h_prob, 2 * m + c + 2)
                        pe.wait_ge(h_ptc, 3 * m + n + 1)
                        src = SM if c == 0 else SP_
                        for g in range(KVH):
                            last = pe.transpose(TB[:, g * P:g * P + P], src[:, g, kb * P:kb * P + P], ident)
                        last.then_inc(h_pt, 1)
                    if j == 5:
                        pe.wait_ge(h_ptc, 3 * m + 2)
                        last = values(pe, 0, [CS])
                        last.then_inc(h_pv, 1)
                    gate_unit(first, j)
                pe.wait_ge(h_ptc, 3 * m + 4)
                pe.wait_ge(h_prob, 2 * m + 3)
                last = values(pe, 1, [PS[:, 0], PS[:, 1]])
                last.then_inc(h_pv, 1)

            pe.wait_ge(ev_act, ACT_EV0["gates"] + 32)
            for u in range(2):
                for o in range(8):
                    n = 8 * u + o
                    if n >= 2:
                        pe.wait_ge(ev_dve, n - 1)
                    g = n // 4
                    product(n % 2, u, [(2 * o, 2 * g), (2 * o + 1, 2 * g + 1)], a_op(bh), a_op(bl),
                            UNIT0["pool"] + u)

            def pairs(phase, first, i, j, mh, ml):
                for o in range(2):
                    pe.wait_ge(ev_dve, DVE_EV0[phase] + 2 * i + 2 * j + o - 1)
                    product(o, j % 2, [(8 * o + k, k) for k in range(8)], mh, ml, UNIT0[phase] + i + j)

            pe.wait_ge(h_ol, 2 * QG + 1)
            with pe.Fori(0, 4) as i:
                for j in range(2):
                    pairs("attn", 0, 2 * i, j, lambda k: bh[:, 8 + k, :], lambda k: bl[:, 8 + k, :])
            pe.wait_ge(m_split, 16)
            units("out", 16, 0, ev_dve, DVE_EV0["out"], (ah, al))

            def norm_pe(n, evs):
                pe.wait_ge(ones_set, 1)
                pe.wait_ge(ev_dve, evs)
                for e in range(KT):
                    last = pe.matmul(TB[:, 0:T], ones[:, :], R[:, e, :], start=(e == 0), stop=(e == KT - 1))
                last.then_inc(ln_pe, 1)
                for e in range(KT):
                    pe.wait_ge(ln_act, (KT + 3) * n + e + 2)
                    last = pe.matmul(OB[:, 0:T], ones[:, :], SQ[:, e, :], start=(e == 0), stop=(e == KT - 1))
                last.then_inc(ln_pe, 1)

            norm_pe(0, DVE_EV0["out"] + 16)
            pe.wait_ge(n_lo, KT)

            def q_unit(i, j):
                unit("query", ev_act, ACT_EV0["query"], i, j, a_op(bh), a_op(bl))

            def key_scores(l, j):
                pe.wait_ge(ev_act, ACT_EV0["query"] + l + 1)
                pe.wait_ge(sc_ev, l + 1)
                rhs = SK[:, bass.ds(l, 1), :] if not isinstance(l, int) else SK[:, l:l + 1, :]
                for c, n in ((0, P), (1, P), (2, NS)):
                    last = pe.matmul(ps[0:n, 2 + j:3 + j, c * P:c * P + P], QT[:, j, c * P:c * P + n], rhs,
                                     start=True, stop=True)
                last.then_inc(r_pe, 1)

            q_unit(0, 0)
            pe.wait_ge(keys_in, 16)
            with pe.Fori(0, 7) as i:
                q_unit(2 * i, 1)
                key_scores(2 * i, 0)
                q_unit(2 * i + 2, 0)
                key_scores(2 * i + 1, 1)
            q_unit(14, 1)
            key_scores(14, 0)
            key_scores(15, 1)

            def u_unit(i, j):
                unit("peer_u", ev_act, ACT_EV0["peer_u"], i, j, a_op(bh), a_op(bl))

            with pe.Fori(0, BEFORE) as i:
                for j in range(8):
                    u_unit(8 * i, j)
            pe.wait_ge(r_idx, NHALF + PH + 1)
            for src, dst in ((I1, ps[:, 4, :]), (I2, ps[:, 5, :]), (GA, TB)):
                for c, n in ((0, P), (1, P), (2, NS)):
                    last = pe.transpose(dst[:, c * P:c * P + n],
                                        src[0:n, c].rearrange("p h k -> p (h k)"), ident[0:n, 0:n])
                last.then_inc(r_pe, 1)
            with pe.Fori(0, WITH) as i:
                for j in range(8):
                    n = 8 * i + j
                    pe.wait_ge(oh_ready, n + 1)
                    if j >= 2:
                        pe.wait_ge(g_ev, n)
                    else:
                        pe.wait_ge(g_ev, 8 * i + 1)
                    for t in range(TOKS):
                        last = pe.matmul(ps[:, 2 + j % 2, t * P:t * P + P], OH[:, j % 2, 0, t, :],
                                         OH[:, j % 2, 1, t, :], start=True, stop=True)
                    last.then_inc(r_pe, 1)
                    u_unit(8 * (BEFORE + i), j)
            with pe.Fori(BEFORE + WITH, BLOCKS) as i:
                for j in range(8):
                    u_unit(8 * i, j)

            pe.wait_ge(ev_act, ACT_EV0["peer_u"] + 128)
            pe.wait_ge(act_ready, 8)
            with pe.Fori(0, BLOCKS // 2) as i:
                for s in range(2):
                    pe.wait_ge(act_ready, 16 * i + 8 * s + 8)
                    for j in range(8):
                        pairs("peer_v", 0, 16 * i + 8 * s, j,
                              lambda k, s=s: ah[:, 8 * s + k, :], lambda k, s=s: al[:, 8 * s + k, :])
            norm_pe(1, DVE_EV0["peer_v"] + 256)

def _axes(a, shape, order):
    return np.ascontiguousarray(a.reshape(shape).transpose(order))


def kernel(x_prompt, x_sample, cache_k, cache_v, state_pool, w_in, b_in, attn_sinks, w_attn_br,
           w_pool, pool_scale, w_out, ln1_g, ln1_b, w_query, sub_keys, peer_u, peer_v, ln2_g, ln2_b):
    import concourse.bacc as bacc
    from concourse.bass_utils import run_bass_kernel_spmd

    r = np.arange(32)
    halves = [np.concatenate([h * HD + 32 * s + r for h in hs])
              for hs in [[QG * g + m for g in range(KVH)] for m in range(QG)] for s in range(2)]
    keys = [AW + np.concatenate([g * HD + 32 * s + r for g in range(KVH)]) for s in range(2)]
    cols = np.concatenate([np.arange(AW + 2 * KW, AW + 2 * KW + PW), *keys, np.arange(AW + KW, AW + 2 * KW),
                           *halves, np.arange(AW + 2 * KW + PW, w_in.shape[1])])
    rows = np.concatenate([(QG * (2 * gh + gl) + m) * HD + np.arange(HD)
                           for gh in range(2) for m in range(QG) for gl in range(2)])
    x = np.concatenate([np.asarray(x_prompt).reshape(SEQ, D), np.asarray(x_sample).reshape(NS, D)])
    (cache_k, cache_v, state_pool, w_in, b_in, attn_sinks, w_attn_br, w_pool, pool_scale, w_out, ln1_g, ln1_b,
     w_query, sub_keys, peer_u, peer_v, ln2_g, ln2_b) = (np.asarray(a) for a in (
         cache_k, cache_v, state_pool, w_in, b_in, attn_sinks, w_attn_br, w_pool, pool_scale, w_out, ln1_g,
         ln1_b, w_query, sub_keys, peer_u, peer_v, ln2_g, ln2_b))
    unit = KT * P
    st = np.zeros((P, 8, 16 + DB * 16), np.float32)
    st[:, :, 16:].reshape(P, 8, DB, 16)[..., 1:] = state_pool.reshape(DB, HIST, 8, P).transpose(3, 2, 0, 1)
    vecs = np.concatenate([
        b_in[cols].reshape(52, P).T, pool_scale.reshape(16, P).T,
        np.broadcast_to(attn_sinks.reshape(KVH, QG).T.reshape(1, HEADS), (P, HEADS)),
        np.repeat(attn_sinks.reshape(KVH, QG).T, NS, axis=0),
        ln1_g.reshape(KT, P).T, ln1_b.reshape(KT, P).T, ln2_g.reshape(KT, P).T, ln2_b.reshape(KT, P).T], axis=1)
    ins = {
        "xT": _axes(x, (T, KT, P), (2, 1, 0)),
        "w_in": _axes(w_in[:, cols], (KT, P, 52, P), (2, 1, 0, 3)).reshape(52, P, unit),
        "w_pool": _axes(w_pool, (2, 2, 2, P, 4, P), (0, 3, 1, 4, 2, 5)).reshape(2, P, unit),
        "w_attn": _axes(w_attn_br[rows], (8, P, 8, 2, P), (2, 1, 3, 0, 4)).reshape(8, P, unit),
        "w_out": _axes(w_out, (KT, P, KT, P), (2, 1, 0, 3)).reshape(16, P, unit),
        "w_query": _axes(w_query, (KT, P, NHALF, P), (2, 1, 0, 3)).reshape(16, P, unit),
        "keysT": _axes(sub_keys, (NHALF, NK, HK), (2, 0, 1)),
        "peer_u": _axes(peer_u, (P, P, KT, P), (0, 3, 2, 1)).reshape(128, P, unit),
        "peer_v": _axes(peer_v, (BLOCKS, 8, P, 8, 2, P), (0, 3, 2, 4, 1, 5)).reshape(128, P, unit),
        "vecs": np.ascontiguousarray(vecs),
        "consts": const_table(),
        "kcT": _axes(cache_k, (DB, WIN, KVH, 2, 32), (2, 4, 3, 0, 1)).reshape(P, 2, DB, WIN),
        "vc": _axes(cache_v, (DB, WIN, KW), (1, 0, 2)),
        "stT": st,
        "k_nat": np.ascontiguousarray(cache_k.reshape(DB, WIN, KW)),
        "st_nat": np.ascontiguousarray(state_pool),
    }
    outs = {"yT": (P, KT, T), "kT": (P, 2, T), "vT": (P, 2, T), "uT": (P, 8, HIST), "us": (P, 8, DB, DS),
            "k_shift": (DB, WIN - DS, KW), "v_shift": (WIN - DS, DB, KW), "st_shift": (DB, HIST - DS, PW)}
    nc = bacc.Bacc("TRN2", target_bir_lowering=False, num_devices=1)
    args = [nc.dram_tensor(f"in_{k}", a.shape, F32, kind="ExternalInput").ap() for k, a in ins.items()]
    args += [nc.dram_tensor(f"out_{k}", s, F32, kind="ExternalOutput").ap() for k, s in outs.items()]
    layer(nc, *args)
    got = run_bass_kernel_spmd(nc, [{f"in_{k}": a for k, a in ins.items()}], core_ids=[0]).results[0]
    yT, kT, vT, uT, us, k_shift, v_shift, st_shift = (got[f"out_{k}"] for k in outs)
    y = yT.transpose(2, 1, 0).reshape(T, D)
    k = kT.reshape(KVH, 32, 2, T).transpose(3, 0, 2, 1).reshape(T, KVH, HD)
    v = vT.transpose(2, 1, 0).reshape(T, KVH, HD)
    u_new = us.transpose(2, 3, 1, 0).reshape(DB, DS, PW)
    k_new, v_new = (a[SEQ:].reshape(DB, DS, KVH, HD) for a in (k, v))
    return (np.ascontiguousarray(y[:SEQ]).reshape(1, SEQ, D), np.ascontiguousarray(y[SEQ:]).reshape(DB, DS, D),
            np.ascontiguousarray(k[SEQ - WIN:SEQ])[None], np.ascontiguousarray(v[SEQ - WIN:SEQ])[None],
            np.ascontiguousarray(uT.transpose(2, 1, 0).reshape(1, HIST, PW)),
            np.concatenate([k_shift.reshape(DB, WIN - DS, KVH, HD), k_new], axis=1),
            np.concatenate([v_shift.transpose(1, 0, 2).reshape(DB, WIN - DS, KVH, HD), v_new], axis=1),
            np.concatenate([st_shift, u_new], axis=1))
```

```python
from contextlib import ExitStack

import numpy as np

import concourse.bass as bass
from concourse import mybir

F32 = mybir.dt.float32
F32R = mybir.dt.float32r
U32 = mybir.dt.uint32
ALU = mybir.AluOpType
ACT = mybir.ActivationFunctionType
AX_X = mybir.AxisListType.X

P = 128
D = 2048
SEQ = 256
DB, DS = 8, 4
NS = DB * DS
T = SEQ + NS
PAST = 2048
HEADS, KVH, HD = 16, 4, 64
QG = HEADS // KVH
AW, KW = HEADS * HD, KVH * HD
WIN = 128
PW = D // 2
HIST = 15
PG = 4
PH, NK, HK, TOPK = 8, 128, 128, 16
ALPHA = 2.0 ** 0.25
EPS = 1e-5
NEG = -1e30
SCALE = HD ** -0.5
KT = D // P
HU = KT * P // 2
CH = 3
NHALF = 2 * PH

PHASES = {"u": (8, 1), "kv": (4, 1), "q": (8, 1), "gates": (32, 1), "pool": (2, 8), "attn": (8, 2),
          "out": (16, 1), "query": (16, 1), "peer_u": (128, 1), "peer_v": (128, 2)}
UNIT0, OUT0 = {}, {}
_u = _o = 0
for _name, (_n, _k) in PHASES.items():
    UNIT0[_name], OUT0[_name] = _u, _o
    _u += _n
    _o += _n * _k
UNITS = _u
ACT_EV0 = {"u": 0, "kv": 8, "q": 12, "gates": 20, "query": 52, "peer_u": 68}
DVE_EV0 = {"pool": 0, "attn": 16, "out": 32, "peer_v": 48}

SAMPLE_UNITS = 8
HEAD_UNITS = (32 - SAMPLE_UNITS) // QG
BLOCKS = 16
BEFORE, WITH = 5, 9
TOKS = T // (WITH * 8)
TG = TOKS * 8

CONST = {}
_c = 0
for _name, _n in (("ident", 128), ("cos", T), ("sin", T), ("mask", 2 * WIN), ("smask", WIN + NS),
                  ("ratio", PG * 16), ("iota", 128)):
    CONST[_name] = (_c, _c + _n)
    _c += _n
CONSTS = _c
VEC = {}
_c = 0
for _name, _n in (("b_in", 52), ("scale", 16), ("sink", 16), ("ssink", 4), ("g1", 16), ("b1", 16),
                  ("g2", 16), ("b2", 16)):
    VEC[_name] = (_c, _c + _n)
    _c += _n
VECS = _c


def const_table():
    t = np.zeros((P, CONSTS), np.float32)

    def put(name, a):
        t[:, CONST[name][0]:CONST[name][1]] = a

    put("ident", np.eye(P))
    half = HD // 2
    inv = np.float32(10000.0) ** (-np.arange(half, dtype=np.float32) / np.float32(half))
    pos = np.concatenate([np.arange(SEQ), PAST + np.tile(np.arange(DS), DB)]).astype(np.float32)
    ang = (pos[None, :] * inv.astype(np.float32)[:, None]).astype(np.float32)
    put("cos", np.tile(np.cos(ang), (4, 1)))
    put("sin", np.tile(np.sin(ang), (4, 1)))
    i, j = np.arange(P)[:, None], np.arange(2 * WIN)[None, :]
    put("mask", np.where((j <= WIN + i) & (j > i), 0.0, NEG))
    row = np.arange(P)[:, None]
    b, i = row % NS // DS, row % DS
    j = np.arange(WIN)[None, :]
    new = np.arange(NS)[None, :]
    put("smask", np.concatenate([np.where(j > i, 0.0, NEG),
                                 np.where((new // DS == b) & (new % DS <= i), 0.0, NEG)], 1))
    w = np.array([2, 4, 8, 16])[:, None]
    put("ratio", (w / np.minimum(w, np.arange(16)[None, :] + 1)).astype(np.float32).reshape(1, -1))
    put("iota", np.arange(128)[None, :])
    return t


class Tally:

    def __init__(self, sem):
        self.sem, self.base, self.k = sem, 0, 0

    def inc(self, instruction):
        instruction.then_inc(self.sem, 1)
        self.k += 1
        return self.base + self.k

    def start(self, i, per):
        self.saved, self.per = self.k, per
        self.base, self.k = self.saved + i * per, 0

    def stop(self, n):
        assert self.k == self.per, (self.k, self.per)
        self.base, self.k = 0, self.saved + n * self.per


def layer(nc, xT, w_in, w_pool, w_attn, w_out, w_query, keysT, peer_u, peer_v, vecs, consts,
          kcT, vc, stT, k_nat, st_nat,
          yT, kT, vT, uT, us, k_shift, v_shift, st_shift):
    ctx = ExitStack()
    with ctx:
        def sb(name, shape, dt=F32):
            return ctx.enter_context(nc.sbuf_tensor(name, shape, dt))

        def sem(name):
            return ctx.enter_context(nc.semaphore(name))

        a_dram = nc.dram_tensor("gelu_scratch", (2 * BLOCKS, P, 4 * T), F32, kind="Internal").ap()
        g_dram = nc.dram_tensor("gate_scratch", (BLOCKS, P, WITH, 8 * TG), F32, kind="Internal").ap()

        raw = sb("raw", [P, 2, KT * P])
        wh = sb("w_hi", [P, 2, KT * P], F32R)
        wl = sb("w_lo", [P, 2, KT * P], F32R)
        R = sb("R", [P, KT, T])
        bh = sb("b_hi", [P, KT, T], F32R)
        bl = sb("b_lo", [P, KT, T], F32R)
        vec = sb("vec", [P, VECS])
        cst = sb("cst", [P, CONSTS])
        ones = sb("ones", [P, P])
        tiny = sb("tiny", [P, 2])
        with (nc.sbuf_tensor("g_stage", [P, 2, P, TG], F32) as gs,
              nc.sbuf_tensor("gate_T", [P, T], F32) as gT,
              nc.sbuf_tensor("gate_hi", [P, T], F32R) as gh,
              nc.sbuf_tensor("gate_lo", [P, T], F32R) as gl):
            pass
        ah = sb("a_hi", [P, KT, T], F32R)
        al = sb("a_lo", [P, KT, T], F32R)
        head = 2 * 4 * T + 2 * 2 * 8 * T
        with (nc.sbuf_tensor("arena_head", [P, head], F32),
              nc.sbuf_tensor("onehots", [P, 2, 3, TOKS, P], F32R) as OH):
            pass
        F = sb("F", [P, (212863 - 4 * (6 * KT * P + 5 * KT * T + VECS + CONSTS + P)) // 4 - 64])

        def carve(off, *shape):
            n = int(np.prod(shape))
            assert off + n <= F.shape[1], (off, shape, F.shape)
            ap = F[:, off:off + n]
            names = "abcd"[:len(shape)]
            if len(shape) > 1:
                ap = ap.rearrange(f"p ({' '.join(names)}) -> p {' '.join(names)}",
                                  **dict(zip(names, shape)))
            return ap, off + n

        GG, o_front = carve(0, 32, T)
        UP, o = carve(o_front, 8, 16 + SEQ)
        US, o = carve(o, 8, DB, 20)
        PT = []
        for _ in range(2):
            t1, o = carve(o, 2, 16 + SEQ)
            t2, o = carve(o, 2, DB, 20)
            PT.append((t1, t2))
        PD, o = carve(o, 2, T)
        QK = R[:, 0:8, :]
        K2 = R[:, 8:10, :]
        V2 = R[:, 10:12, :]
        RT = [R[:, 12:16, :], None]
        RT[1], _ = carve(o_front + 8 * (16 + SEQ) + 8 * DB * 20, 4, T)
        KC, o = carve(o_front, 2, DB, P)
        VC, o = carve(o, DB, KW)
        CS, o2 = carve(o_front + 2 * DB * P + DB * KW, 4, P)
        SM, o2 = carve(o2, 4, 2 * WIN)
        VN, o2 = carve(o2, 2, KW)
        VS, o2 = carve(o2, KW)
        SX, o2 = carve(o2, 4, 8)
        QW, o2 = carve(o2, 2, QG, NS)
        PS, o = carve(o_front, 2, 4, P)
        QS, o = carve(o, 2, T)
        SP_, o = carve(o, 4, 2 * WIN)
        SQ = GG[:, 0:16, :]
        MEAN, VAR, RSTD, TMP = (GG[:, 16 + n, :] for n in range(4))
        ST, o_st = carve(0, 2, 4, T)
        SK, o = carve(0, NHALF, P)
        QT, o = carve(o, 2, T)
        SC, o = carve(o, CH, NHALF, P)
        TV, o = carve(o, CH, NHALF, TOPK)
        TI, o = carve(o, CH, NHALF, TOPK)
        CV, o = carve(o, CH, PH, TOPK)
        CI, o = carve(o, CH, PH, TOPK)
        LS, o = carve(o, CH, TOPK * TOPK)
        LV, o = carve(o, CH, TOPK)
        LI, o = carve(o, CH, TOPK)
        X1, o = carve(o, CH, PH, TOPK)
        X2, o = carve(o, CH, PH, TOPK)
        GA, o = carve(o, CH, PH, TOPK)
        I1, o = carve(o, CH, PH, TOPK)
        I2, o = carve(o, CH, PH, TOPK)
        CS1, o = carve(o, CH, PH, 1)
        E4, _ = carve(o, PH * TOPK, TOPK)
        AB, o_ab = carve(o_st, 2, 8, T)
        GB, o_ab = carve(o_ab, 2, WITH, 8 * TG)
        assert o_ab == head
        I1T, o_ab = carve(max(o, o_ab + 6 * TOKS * P), T)
        I2T, o_ab = carve(o_ab, T)

        ps = ctx.enter_context(nc.psum_tensor("ps", [P, 8, 512], F32))
        SB4 = ps[:, 2:6, :]
        TB = ps[:, 6, :]
        OB = ps[:, 7, :]
        HO = (OB, ps[:, 3, :])
        ident = cst[:, CONST["ident"][0]:CONST["ident"][1]]

        def C(name):
            return cst[:, CONST[name][0]:CONST[name][1]]

        def V(name):
            return vec[:, VEC[name][0]:VEC[name][1]]

        loaded = [sem(f"half_loaded_{n}") for n in range(4)]
        hi_ready, lo_ready = sem("hi_ready"), sem("lo_ready")
        outs_done = sem("outs_done")
        ev_act, ev_dve = sem("evicted_by_act"), sem("evicted_by_dve")
        x_loaded = [sem(f"x_loaded_{n}") for n in range(4)]
        vec_in = sem("vec_in")
        x_hi, x_lo = sem("x_hi_ready"), sem("x_lo_ready")
        consts_in, caches_in, state_in, keys_in, x_again = (
            sem(n) for n in ("consts_in", "caches_in", "state_in", "keys_in", "x_again"))
        d_split, k_rope, q_rope = sem("pooled_split"), sem("k_rotated"), sem("q_rotated")
        q_side = sem("sample_q_side_by_side")
        dve = sem("dve_order")
        v_turned, v_copied = sem("v_turned"), sem("v_copied")
        sc_cache, sc_copied, sc_turned = sem("s_cache_scores"), sem("s_scores_copied"), sem("s_scores_turned")
        s_sm, s_exp, s_prob = sem("s_shifted"), sem("s_exp"), sem("s_probs")
        s_pt, s_ptc, s_pv, s_oh, s_ol = (sem(n) for n in (
            "s_probs_turned", "s_probs_copied", "s_pv", "s_o_hi", "s_o_lo"))
        h_q, h_scores, h_masked, h_sm, h_exp, h_prob = (sem(n) for n in (
            "h_q_staged", "h_scores", "h_masked", "h_shifted", "h_exp", "h_probs"))
        h_pt, h_ptc, h_pv, h_oh, h_ol = (sem(n) for n in (
            "h_probs_turned", "h_probs_copied", "h_pv", "h_o_hi", "h_o_lo"))
        m_split = sem("merged_split")
        ln_pe, ln_act, ln_dve, n_aff, n_hi, n_lo = (sem(n) for n in (
            "ln_pe", "ln_act", "ln_dve", "ln_affine", "h_hi", "h_lo"))
        ln_scaled = sem("ln_scaled")
        sc_ev = sem("key_scores_copied")
        r_pe, r_exp_in, r_exp, r_idx, r_turned = (sem(n) for n in (
            "route_pe", "route_shifted", "route_exp", "route_choices", "route_turned"))
        oh_ready, g_ev, g_stored = sem("onehots_ready"), sem("gates_evicted"), sem("gates_stored")
        a_stored = [sem("gelu_stored_0"), sem("gelu_stored_1")]
        blk_in = [sem("block_in_0"), sem("block_in_1")]
        act_ready, y_init = sem("gated_ready"), sem("y_init")
        stored, u_stored, kv_stored = sem("outputs_stored"), sem("u_stored"), sem("kv_stored")
        ones_set = sem("ones_set")

        block = ctx.enter_context(nc.Block())

        def bc(ap, axis, n):
            a = ap.unsqueeze(axis)
            shape = list(a.shape)
            shape[axis] = n
            return a.broadcast_to(shape)

        def block_piece(sp, b, s, n, i=None):
            if n < 2:
                dst, src = AB[:, s, 4 * n:4 * n + 4, :].rearrange("p e t -> p (e t)"), \
                    a_dram[bass.ds(2 * b + n, 1)].rearrange("a p n -> p (a n)")
            else:
                w = slice(0, 5) if n == 2 else slice(5, WITH)
                dst, src = GB[:, s, w, :], g_dram[bass.ds(b, 1), :, w, :].rearrange("a p w n -> p (a w) n")
            if n == 0 and i is not None:
                sp.wait_ge(act_ready, 8 * (2 * i + s + 1))
                for m in range(2):
                    sp.wait_ge(a_stored[m], 16 * (2 * i + s + 3) + 1)
            sp.dma_start(dst, src).then_inc(blk_in[s], 16)

        def o_tiles(t, m, c):
            return t[:, 8:16, c * P:c * P + P].rearrange("p (a b) t -> p a b t", a=2)[
                :, :, bass.ds(m, 1), :].rearrange("p a b t -> p a (b t)")

        def norm_act(act, n):
            act.wait_ge(ln_pe, 2 * n + 1)
            act.activation(MEAN, TB[:, 0:T], ACT.Copy, scale=1.0 / D).then_inc(ln_act, 1)
            for e in range(KT):
                act.wait_ge(ln_dve, KT * n + e + 1)
                act.activation(SQ[:, e, :], R[:, e, :], ACT.Square).then_inc(ln_act, 1)
            act.wait_ge(ln_pe, 2 * n + 2)
            act.activation(TMP, OB[:, 0:T], ACT.Copy, scale=1.0 / D, bias=EPS).then_inc(ln_act, 1)
            act.wait_ge(ln_act, (KT + 3) * n + KT + 2)
            act.activation(VAR, TMP, ACT.Sqrt).then_inc(ln_act, 1)

        def norm_dve(ve, link, n):
            ve.wait_ge(ln_act, (KT + 3) * n + 1)
            for e in range(KT):
                ve.tensor_tensor(R[:, e, :], R[:, e, :], MEAN, ALU.subtract).then_inc(ln_dve, 1)
            ve.wait_ge(ln_act, (KT + 3) * (n + 1))
            link(ve.reciprocal(RSTD, VAR))
            link(ve.tensor_tensor(VAR, RSTD, RSTD, ALU.mult))
            link(ve.tensor_tensor(VAR, VAR, TMP, ALU.mult))
            link(ve.tensor_scalar(VAR, VAR, -0.5, 1.5, ALU.mult, ALU.add))
            link(ve.tensor_tensor(RSTD, RSTD, VAR, ALU.mult))
            g, b = (V("g1"), V("b1")) if n == 0 else (V("g2"), V("b2"))
            for e in range(KT + 1):
                if e < KT:
                    ve.tensor_tensor(R[:, e, :], R[:, e, :], RSTD, ALU.mult).then_inc(ln_scaled, 1)
                if e > 0:
                    ve.wait_ge(ln_scaled, KT * n + e)
                    ve.tensor_scalar(R[:, e - 1, :], R[:, e - 1, :], g[:, e - 1:e], b[:, e - 1:e],
                                     ALU.mult, ALU.add).then_inc(n_aff, 1)

        def values(pe, c, probs):
            for g in range(KVH):
                r = slice(64 * (g % 2), 64 * (g % 2) + 64)
                out = HO[c][r, P * (g // 2):P * (g // 2) + P]
                for kb, pr in enumerate(probs):
                    last = pe.matmul(out, VN[:, kb, g * HD:g * HD + HD], pr[:, g, :],
                                     start=(kb == 0), stop=(kb == len(probs) - 1))
            return last


        @block.sync
        def _(sp):
            def load(src, u0, i, j, wait=True):
                for h in range(2):
                    if wait:
                        sp.wait_ge(lo_ready, 2 * (u0 + j) + h - 3 + i * 4)
                    sp.dma_start(raw[:, j % 2, h * HU:h * HU + HU], src[:, h * HU:h * HU + HU])\
                        .then_inc(loaded[2 * (j % 2) + h], 16)

            def stream(src, u0, n, first=0):
                with sp.Fori(0, n // 2) as i:
                    for j in range(2):
                        load(src[first + 2 * i + j], u0, i, j)

            for n in range(4):
                sp.dma_start(R[:, 4 * n:4 * n + 4, :], xT[:, 4 * n:4 * n + 4, :]).then_inc(x_loaded[n], 16)
                if n in (0, 3):
                    load(w_in[n // 3], 0, 0, n // 3, wait=False)
            sp.dma_start(vec[:, :], vecs).then_inc(vec_in, 16)
            stream(w_in, 2, 2, first=2)
            sp.dma_start(cst[:, :], consts).then_inc(consts_in, 16)
            sp.dma_start(UP[:, :, 0:16], stT[:, 0:8, 0:16]).then_inc(state_in, 16)
            sp.dma_start(US[:, :, :, 0:16], stT[:, :, 16:16 + DB * 16].rearrange("p a (b s) -> p a b s", b=DB))\
                .then_inc(state_in, 16)
            stream(w_in, 4, 18, first=4)
            sp.wait_ge(d_split, PG)
            sp.wait_ge(u_stored, 32)
            sp.wait_ge(q_rope, 1)
            sp.dma_start(KC, kcT).then_inc(caches_in, 16)
            sp.dma_start(VC, vc).then_inc(caches_in, 16)
            stream(w_in, 22, 30, first=22)
            for n in range(2):
                load(w_pool[n], UNIT0["pool"], 0, n)
            stream(w_attn, UNIT0["attn"], 8)
            sp.wait_ge(h_pv, 2 * QG)
            sp.wait_ge(kv_stored, 32)
            sp.dma_start(R[:, :, :], xT).then_inc(x_again, 16)
            stream(w_out, UNIT0["out"], 16)
            stream(w_query, UNIT0["query"], 2)
            sp.wait_ge(n_lo, KT)
            sp.dma_start(SK, keysT).then_inc(keys_in, 16)
            stream(w_query, UNIT0["query"] + 2, 14, first=2)
            stream(peer_u, UNIT0["peer_u"], (BLOCKS - 1) * 8)
            sp.wait_ge(g_stored, 64 * WITH + 65)
            for n in range(2):
                sp.wait_ge(a_stored[n], 33)
            for j in range(8):
                load(peer_u[(BLOCKS - 1) * 8 + j], UNIT0["peer_u"] + (BLOCKS - 1) * 8, 0, j)
                block_piece(sp, j // 4, j // 4, j % 4)
            with sp.Fori(0, BLOCKS // 2 - 1) as i:
                for s in range(2):
                    for j in range(8):
                        load(peer_v[16 * i + 8 * s + j], UNIT0["peer_v"] + 8 * s, 8 * i, j)
                        if j < 4:
                            block_piece(sp, 2 * i + s + 2, s, j, i)
            stream(peer_v, UNIT0["peer_v"] + 112, 16, first=112)
            sp.wait_ge(stored, 16 * (3 + KT // 2))

        @block.gpsimd
        def _(pool):
            def lower(i, j):
                for h in range(2):
                    pool.wait_ge(hi_ready, 4 * i + 2 * j + h + 1)
                    s = slice(h * HU, h * HU + HU)
                    pool.tensor_tensor(wl[:, j, s], raw[:, j, s], wh[:, j, s].bitcast(F32),
                                       ALU.subtract).then_inc(lo_ready, 1)

            q0 = UNIT0["query"] // 2
            with pool.Fori(0, q0) as i:
                for j in range(2):
                    lower(i, j)
            lower(q0, 0)
            for e in range(KT):
                pool.wait_ge(n_hi, e + 1)
                pool.tensor_tensor(bl[:, e, :], R[:, e, :], bh[:, e, :].bitcast(F32), ALU.subtract).then_inc(n_lo, 1)
            lower(q0, 1)
            with pool.Fori(q0 + 1, UNITS // 2) as i:
                for j in range(2):
                    lower(i, j)

        @block.scalar
        def _(act):

            def hi(phase, i, j):
                units, per = PHASES[phase]
                act.wait_ge(outs_done, OUT0[phase] + (i + j) * per + 1)
                k = (j + 1) % 2
                for h in range(2):
                    act.wait_ge(loaded[2 * k + h], 16 * (UNIT0[phase] // 2 + (j + 1) // 2 + 1) + i * 8)
                    s = slice(h * HU, h * HU + HU)
                    act.activation(wh[:, k, s], raw[:, k, s], ACT.Copy).then_inc(hi_ready, 1)

            def wait_out(phase, n):
                act.wait_ge(outs_done, OUT0[phase] + n + 2)

            def units(phase, n, first, body, step=2, skip_last=False):
                with act.Fori(0, n // step) as i:
                    for j in range(step):
                        hi(phase, first + step * i, j)
                        body(first + step * i, j)

            for s in (h_ptc, *a_stored):
                act.sem_inc(s, 1)
            act.sem_inc(g_stored, 65)
            for n in range(4):
                act.wait_ge(x_loaded[n], 16)
                act.activation(ah[:, 4 * n:4 * n + 4, :], R[:, 4 * n:4 * n + 4, :], ACT.Copy).then_inc(x_hi, 1)
                if n == 0:
                    for h in range(2):
                        act.wait_ge(loaded[h], 16)
                        s = slice(h * HU, h * HU + HU)
                        act.activation(wh[:, 0, s], raw[:, 0, s], ACT.Copy).then_inc(hi_ready, 1)
            act.wait_ge(vec_in, 16)

            def ev_u(i, j):
                wait_out("u", i + j)
                bias = V("b_in")[:, bass.ds(i + j, 1)]
                act.activation(UP[:, bass.ds(i + j, 1), 16:16 + SEQ], ps[:, j:j + 1, 0:SEQ], ACT.Identity, bias=bias)
                act.activation(US[:, bass.ds(i + j, 1), :, 16:20].rearrange("p a b s -> p (a b) s"),
                               ps[:, j, SEQ:T].rearrange("p (b s) -> p b s", b=DB),
                               ACT.Identity, bias=bias).then_inc(ev_act, 1)

            units("u", 8, 0, ev_u)
            act.wait_ge(ev_act, 8)
            act.dma_start(uT, UP[:, :, 16 + SEQ - HIST:]).then_inc(u_stored, 16)
            act.dma_start(us, US[:, :, :, 16:20]).then_inc(u_stored, 16)
            act.wait_ge(x_lo, 4)

            def ev_kv(i, j):
                wait_out("kv", i + j)
                act.activation(R[:, bass.ds(8 + i + j, 1), :], ps[:, j:j + 1, 0:T], ACT.Identity,
                               bias=V("b_in")[:, bass.ds(8 + i + j, 1)]).then_inc(ev_act, 1)

            def ev_q(i, j):
                wait_out("q", i + j)
                act.activation(R[:, bass.ds(i + j, 1), :], ps[:, j:j + 1, 0:T], ACT.Identity,
                               bias=V("b_in")[:, bass.ds(12 + i + j, 1)]).then_inc(ev_act, 1)

            def ev_gate(i, j):
                wait_out("gates", i + j)
                act.activation(GG[:, bass.ds(i + j, 1), :], ps[:, j % 2:j % 2 + 1, 0:T], ACT.Sigmoid,
                               bias=V("b_in")[:, bass.ds(20 + i + j, 1)]).then_inc(ev_act, 1)

            units("kv", 4, 0, ev_kv)
            units("q", 8, 0, ev_q)
            act.wait_ge(k_rope, 1)
            act.dma_start(kT, K2).then_inc(kv_stored, 16)
            act.dma_start(vT, V2).then_inc(kv_stored, 16)
            act.dma_start(k_shift, k_nat[:, DS:, :]).then_inc(stored, 16)
            act.dma_start(v_shift, vc[DS:, :, :]).then_inc(stored, 16)
            act.dma_start(st_shift, st_nat[:, DS:, :]).then_inc(stored, 16)

            for j in range(SAMPLE_UNITS):
                if j == 0:
                    act.wait_ge(v_turned, 1)
                    act.wait_ge(d_split, PG)
                    act.activation(VN, TB.rearrange("p (a b) -> p a b", a=2), ACT.Copy).then_inc(v_copied, 1)
                    act.activation(VS[0:NS, :], OB[0:NS, 0:KW], ACT.Copy).then_inc(v_copied, 1)
                if j == 2:
                    act.wait_ge(sc_cache, 1)
                    act.activation(CS, SB4[:, :, 0:P], ACT.Copy).then_inc(sc_copied, 1)
                if j == 4:
                    act.wait_ge(s_sm, 2)
                    act.activation(SM[:, :, 0:WIN + NS], SM[:, :, 0:WIN + NS], ACT.Exp).then_inc(s_exp, 1)
                    act.activation(SX[:, 1, 0:4], SX[:, 1, 0:4], ACT.Exp).then_inc(s_exp, 1)
                if j == 5:
                    act.wait_ge(s_pt, 1)
                    act.activation(CS, TB.rearrange("p (a b) -> p a b", a=4), ACT.Copy).then_inc(s_ptc, 1)
                    act.activation(SM[0:NS, 0:2, :].rearrange("p a b -> p (a b)"),
                                   ps[0:NS, 2, :], ACT.Copy).then_inc(s_ptc, 1)
                if j == 7:
                    act.wait_ge(s_pv, 1)
                    act.activation(bh[:, 8:16, SEQ:T], OB[:, 0:256].rearrange("p (a b) -> p a b", a=8),
                                   ACT.Copy).then_inc(s_oh, 1)
                hi("gates", 0, j)
                ev_gate(0, j)

            with act.Fori(0, QG) as m:
                first = SAMPLE_UNITS + HEAD_UNITS * m
                for j in range(HEAD_UNITS):
                    if j == 1:
                        for c, n in ((0, WIN), (1, 2 * WIN)):
                            buf = SM if c == 0 else SP_
                            act.wait_ge(h_sm, 4 * m + 2 * c + 2)
                            act.activation(buf[:, :, 0:n], buf[:, :, 0:n], ACT.Exp).then_inc(h_exp, 1)
                            act.activation(SX[:, 1, 4 * c:4 * c + 4], SX[:, 1, 4 * c:4 * c + 4],
                                           ACT.Exp).then_inc(h_exp, 1)
                    if j in (3, 4, 5):
                        n = j - 3
                        act.wait_ge(h_pt, 3 * m + n + 1)
                        dst = (CS, PS[:, 0], PS[:, 1])[n]
                        act.activation(dst, TB.rearrange("p (a b) -> p a b", a=4), ACT.Copy).then_inc(h_ptc, 1)
                    hi("gates", first, j)
                    ev_gate(first, j)
                for c in range(2):
                    act.wait_ge(h_pv, 2 * m + c + 1)
                    act.activation(o_tiles(bh, m, c), HO[c][:, 0:256].rearrange("p (a b) -> p a b", a=2),
                                   ACT.Copy).then_inc(h_oh, 1)

            for j in range(2):
                hi("pool", 0, j)
            units("attn", 8, 0, lambda i, j: None)
            units("out", 16, 0, lambda i, j: None)

            norm_act(act, 0)
            for e in range(KT):
                act.wait_ge(n_aff, e + 1)
                act.activation(bh[:, e, :], R[:, e, :], ACT.Copy).then_inc(n_hi, 1)

            def ev_query(i, j):
                wait_out("query", i + j)
                act.activation(QT[:, j, :], ps[:, j, 0:T], ACT.Copy).then_inc(ev_act, 1)

            units("query", 16, 0, ev_query)

            def ev_peer(i, j):
                wait_out("peer_u", 8 * i + j)
                if j % 4 == 0:
                    act.wait_ge(a_stored[j // 4], 16 * i + 1)
                act.activation(ST[:, j // 4, j % 4, :], ps[:, j % 2, 0:T], ACT.Gelu).then_inc(ev_act, 1)

            def store_half(i, half):
                act.wait_ge(ev_act, ACT_EV0["peer_u"] + 8 * i + 4 * half + 4)
                act.dma_start(a_dram[2 * i + half], ST[:, half, :, :].rearrange("p e t -> p (e t)"))\
                    .then_inc(a_stored[half], 16)

            def store_gates(w, n):
                if n == 0:
                    act.wait_ge(g_ev, 8 * w + 9)
                    act.wait_ge(g_stored, 64 * w + 65)
                act.dma_start(g_dram[4 * n:4 * n + 4, :, bass.ds(w, 1), :].rearrange("b p w n -> p b (w n)"),
                              gs[:, bass.ds(w % 2, 1), 32 * n:32 * n + 32, :].rearrange(
                                  "p a (b e) t -> p b (a e t)", b=4)).then_inc(g_stored, 16)

            def peer_block(i, w=None):
                for j in range(8):
                    hi("peer_u", 8 * i, j)
                    if w is not None and j < 4:
                        store_gates(w, j)
                    if j == 4:
                        store_half(i, 0)
                    ev_peer(i, j)
                store_half(i, 1)

            act.wait_ge(sc_ev, NHALF + 2)
            with act.Fori(0, 3) as i:
                peer_block(i)
            act.wait_ge(r_exp_in, 1)
            act.activation(CV, CV, ACT.Exp).then_inc(r_exp, 1)
            with act.Fori(3, BEFORE + 1) as i:
                peer_block(i)
            with act.Fori(1, WITH) as i:
                peer_block(BEFORE + i, i - 1)
            peer_block(BEFORE + WITH, WITH - 1)
            with act.Fori(BEFORE + WITH + 1, BLOCKS) as i:
                peer_block(i)
            with act.Fori(0, 63) as i:
                for j in range(2):
                    hi("peer_v", 2 * i, j)
            hi("peer_v", 126, 0)
            norm_act(act, 1)
            for e in range(0, KT, 2):
                act.wait_ge(n_aff, KT + e + 2)
                act.dma_start(yT[:, e:e + 2, :], R[:, e:e + 2, :]).then_inc(stored, 16)

        @block.vector
        def _(ve):
            own = Tally(dve)

            def link(instruction):
                ve.wait_ge(dve, own.inc(instruction))

            for s in (h_prob, h_ol, g_ev):
                ve.sem_inc(s, 1)
            ve.memset(tiny[:, :], 0.0)
            ve.memset(ones[:, :], 1.0).then_inc(ones_set, 1)
            ve.wait_ge(ones_set, 1)
            for n in range(4):
                ve.wait_ge(x_hi, n + 1)
                s = slice(4 * n, 4 * n + 4)
                ve.tensor_tensor(al[:, s, :], R[:, s, :], ah[:, s, :].bitcast(F32), ALU.subtract).then_inc(x_lo, 1)

            ve.wait_ge(ev_act, 8)
            ve.wait_ge(consts_in, 16)
            ve.wait_ge(state_in, 32)
            ratio = C("ratio").rearrange("p (g s) -> p g s", g=PG)
            for g in range(PG):
                t = slice(2 * g, 2 * g + 2)
                src = (UP[:, t], US[:, t])
                for level in range(g + 1):
                    step = 1 << level
                    lo = 2 * step
                    dst = PT[level % 2]
                    ve.tensor_tensor(dst[0][:, :, lo:], src[0][:, :, lo:], src[0][:, :, lo - step:-step], ALU.add)
                    link(ve.tensor_tensor(dst[1][:, :, :, lo:], src[1][:, :, :, lo:],
                                          src[1][:, :, :, lo - step:-step], ALU.add))
                    src = dst
                link(ve.tensor_tensor(src[0][:, :, 16:32], src[0][:, :, 16:32], bc(ratio[:, g, :], 1, 2), ALU.mult))
                w = 1.0 / (2 << g)
                ve.scalar_tensor_tensor(out=PD[:, :, 0:SEQ], in0=src[0][:, :, 16:], scalar=w,
                                        in1=UP[:, t, 16:], op0=ALU.mult, op1=ALU.subtract)
                for k in range(2):
                    last = ve.scalar_tensor_tensor(
                        out=PD[:, k, SEQ:T].rearrange("p (b s) -> p b s", b=DB), in0=src[1][:, k, :, 16:],
                        scalar=w, in1=US[:, 2 * g + k, :, 16:], op0=ALU.mult, op1=ALU.subtract)
                link(last)
                link(ve.tensor_copy(bh[:, t, :], PD))
                ve.tensor_tensor(bl[:, t, :], PD, bh[:, t, :].bitcast(F32), ALU.subtract).then_inc(d_split, 1)
                ve.wait_ge(d_split, g + 1)

            def rope(a, b, t0, t1, n, done):
                cos, sin = bc(C("cos"), 1, n), bc(C("sin"), 1, n)
                ve.tensor_tensor(t0, b, sin, ALU.mult)
                link(ve.tensor_tensor(t1, a, sin, ALU.mult))
                ve.tensor_tensor(a, a, cos, ALU.mult)
                link(ve.tensor_tensor(b, b, cos, ALU.mult))
                ve.tensor_tensor(a, a, t0, ALU.subtract)
                last = ve.tensor_tensor(b, b, t1, ALU.add)
                last.then_inc(done, 1)

            ve.wait_ge(ev_act, 12)
            rope(K2[:, 0:1], K2[:, 1:2], RT[0][:, 0:1], RT[1][:, 0:1], 1, k_rope)
            ve.wait_ge(ev_act, 20)
            ve.wait_ge(k_rope, 1)
            qp = QK.rearrange("p (m h) t -> p h m t", h=2)
            rope(qp[:, 0], qp[:, 1], RT[0], RT[1], 4, q_rope)

            def softmax(buf, n, sink, x, shifted):
                link(ve.tensor_reduce(SX[:, 0, x], buf[:, :, 0:n], AX_X, ALU.max))
                link(ve.tensor_tensor(SX[:, 0, x], SX[:, 0, x], sink, ALU.max))
                ve.tensor_tensor(SX[:, 1, x], sink, SX[:, 0, x], ALU.subtract).then_inc(shifted, 1)
                ve.tensor_tensor(buf[:, :, 0:n], buf[:, :, 0:n], bc(SX[:, 0, x], 2, n), ALU.subtract)\
                    .then_inc(shifted, 1)

            def divide(buf, n, x, exped, value, done):
                ve.wait_ge(exped, value)
                link(ve.tensor_reduce(SX[:, 2, x], buf[:, :, 0:n], AX_X, ALU.add))
                link(ve.tensor_tensor(SX[:, 2, x], SX[:, 2, x], SX[:, 1, x], ALU.add))
                link(ve.reciprocal(SX[:, 3, x], SX[:, 2, x]))
                ve.tensor_tensor(buf[:, :, 0:n], buf[:, :, 0:n], bc(SX[:, 3, x], 2, n), ALU.mult)\
                    .then_inc(done, 1)

            ve.wait_ge(q_rope, 1)
            for half in range(2):
                last = ve.tensor_copy(QW[:, half], qp[:, half, :, SEQ:T])
            last.then_inc(q_side, 1)

            ve.wait_ge(sc_turned, 1)
            mask = C("smask")
            ve.scalar_tensor_tensor(out=SM[:, :, 0:WIN], in0=TB.rearrange("p (a b) -> p a b", a=4), scalar=SCALE,
                                    in1=bc(mask[:, 0:WIN], 1, 4), op0=ALU.mult, op1=ALU.add)
            link(ve.scalar_tensor_tensor(out=SM[:, :, WIN:WIN + NS], in0=SB4[:, :, 256:256 + NS], scalar=SCALE,
                                         in1=bc(mask[:, WIN:], 1, 4), op0=ALU.mult, op1=ALU.add))
            softmax(SM, WIN + NS, V("ssink"), slice(0, 4), s_sm)
            divide(SM, WIN + NS, slice(0, 4), s_exp, 2, s_prob)
            ve.wait_ge(s_oh, 1)
            ve.tensor_tensor(bl[:, 8:16, SEQ:T], OB[:, 0:256].rearrange("p (a b) -> p a b", a=8),
                             bh[:, 8:16, SEQ:T].bitcast(F32), ALU.subtract).then_inc(s_ol, 1)

            ve.wait_ge(s_ol, 1)
            with ve.Fori(0, QG) as m:
                own.start(m, 2 * 6)
                ve.wait_ge(h_scores, 2 * m + 1)
                ve.tensor_copy(QS, R[:, bass.ds(2 * m, 2), :]).then_inc(h_q, 1)
                sink = V("sink")[:, bass.ds(4 * m, 4)]
                for c, n in ((0, WIN), (1, 2 * WIN)):
                    buf = SM if c == 0 else SP_
                    x = slice(4 * c, 4 * c + 4)
                    ve.wait_ge(h_scores, 2 * m + 3)
                    link(ve.scalar_tensor_tensor(
                        out=buf[:, :, 0:n], in0=SB4[:, :, 0:WIN] if c == 0 else SB4[:, :, WIN:3 * WIN],
                        scalar=SCALE, in1=bc(C("mask")[:, 2 * WIN - n:], 1, 4), op0=ALU.mult, op1=ALU.add))
                    softmax(buf, n, sink, x, h_sm)
                for c, n in ((0, WIN), (1, 2 * WIN)):
                    divide(SM if c == 0 else SP_, n, slice(4 * c, 4 * c + 4), h_exp, 4 * m + 2 * c + 2, h_prob)
                for c in range(2):
                    ve.wait_ge(h_oh, 2 * m + c + 1)
                    ve.tensor_tensor(o_tiles(bl, m, c), HO[c][:, 0:256].rearrange("p (a b) -> p a b", a=2),
                                     o_tiles(bh, m, c).bitcast(F32), ALU.subtract).then_inc(h_ol, 1)
                own.stop(QG)

            for o in range(16):
                ve.wait_ge(outs_done, OUT0["pool"] + o + 2)
                ve.scalar_tensor_tensor(out=GG[:, o, :], in0=ps[:, o % 2, 0:T], scalar=V("scale")[:, o:o + 1],
                                        in1=GG[:, o, :], op0=ALU.mult, op1=ALU.mult).then_inc(ev_dve, 1)
            ve.wait_ge(ev_dve, 16)
            with ve.Fori(0, 8) as i:
                own.start(i, 2 * 2)
                for j in range(2):
                    o = 2 * i + j
                    ve.wait_ge(outs_done, OUT0["attn"] + o + 2)
                    ve.tensor_tensor(GG[:, bass.ds(16 + o, 1), :], ps[:, j:j + 1, 0:T],
                                     GG[:, bass.ds(16 + o, 1), :], ALU.mult).then_inc(ev_dve, 1)
                    ve.wait_ge(ev_dve, DVE_EV0["attn"] + o + 1)
                    link(ve.tensor_tensor(GG[:, bass.ds(o, 1), :], GG[:, bass.ds(16 + o, 1), :],
                                          GG[:, bass.ds(o, 1), :], ALU.add))
                    link(ve.tensor_copy(ah[:, bass.ds(o, 1), :], GG[:, bass.ds(o, 1), :]))
                    ve.tensor_tensor(al[:, bass.ds(o, 1), :], GG[:, bass.ds(o, 1), :],
                                     ah[:, bass.ds(o, 1), :].bitcast(F32), ALU.subtract).then_inc(m_split, 1)
                own.stop(8)

            ve.wait_ge(x_again, 16)
            with ve.Fori(0, 8) as i:
                for j in range(2):
                    o = 2 * i + j
                    ve.wait_ge(outs_done, OUT0["out"] + o + 2)
                    ve.scalar_tensor_tensor(out=R[:, bass.ds(o, 1), :], in0=R[:, bass.ds(o, 1), :], scalar=ALPHA,
                                            in1=ps[:, j:j + 1, 0:T], op0=ALU.mult, op1=ALU.add).then_inc(ev_dve, 1)
            norm_dve(ve, link, 0)
            ve.wait_ge(n_lo, KT)
            ve.tensor_scalar(R[:, :, :], R[:, :, :], ALPHA, None, ALU.mult).then_inc(y_init, 1)
            ve.sem_inc(sc_ev, 1)
            ve.memset(SC[:, 2], 0.0).then_inc(sc_ev, 1)
            ve.wait_ge(sc_ev, 2)
            with ve.Fori(0, NHALF // 2) as i:
                for j in range(2):
                    ve.wait_ge(r_pe, 2 * i + j + 1)
                    ve.tensor_copy(SC[:, 0:2, bass.ds(2 * i + j, 1), :].rearrange("p c a n -> p c (a n)"),
                                   ps[:, 2 + j, 0:256].rearrange("p (c n) -> p c n", c=2))
                    ve.tensor_copy(SC[0:NS, 2, bass.ds(2 * i + j, 1), :], ps[0:NS, 2 + j, 256:384].unsqueeze(1))\
                        .then_inc(sc_ev, 1)
            ve.wait_ge(sc_ev, NHALF + 2)

            def hold(mark):
                ve.wait_ge(dve, mark)
                ve.tensor_copy(tiny[:, 1:2], tiny[:, 0:1])

            def top16(scores, best, index):
                def stage(make):
                    for c in range(CH):
                        mark = own.inc(make(c))
                    return mark

                hold(stage(lambda c: ve.max(best[c][:, 0:8], scores[c])))
                hold(stage(lambda c: ve.max_index(index[c][:, 0:8], best[c][:, 0:8], scores[c])))
                hold(stage(lambda c: ve.match_replace(scores[c], best[c][:, 0:8], scores[c], -3.0e38)))
                hold(stage(lambda c: ve.max(best[c][:, 8:16], scores[c])))
                ve.wait_ge(dve, stage(lambda c: ve.max_index(index[c][:, 8:16], best[c][:, 8:16], scores[c])))

            with ve.Fori(0, NHALF) as i:
                own.start(i, 1 + 15)
                hold(own.inc(ve.tensor_copy(LS[:, :, 0:P],
                                            SC[:, :, bass.ds(i, 1), :].rearrange("p c a n -> p c (a n)"))))
                top16([LS[:, c, 0:P] for c in range(CH)], [LV[:, c, :] for c in range(CH)],
                      [LI[:, c, :].bitcast(U32) for c in range(CH)])
                ve.tensor_copy(TV[:, :, bass.ds(i, 1), :].rearrange("p c a n -> p c (a n)"), LV)
                ve.tensor_copy(TI[:, :, bass.ds(i, 1), :].rearrange("p c a n -> p c (a n)"),
                               LI.bitcast(U32)).then_inc(r_idx, 1)
                ve.wait_ge(r_idx, i + 1)
                own.stop(NHALF)
            with ve.Fori(0, PH) as h:
                own.start(h, CH + 15)
                for c in range(CH):
                    a = TV[:, c, bass.ds(2 * h, 1), :].rearrange("p a n -> p (a n)")
                    b = TV[:, c, bass.ds(2 * h + 1, 1), :].rearrange("p a n -> p (a n)")
                    mark = own.inc(ve.tensor_tensor(LS[:, c, :].rearrange("p (a b) -> p a b", a=16),
                                                    bc(a, 2, 16), bc(b, 1, 16), ALU.add))
                hold(mark)
                top16([LS[:, c, :] for c in range(CH)], [LV[:, c, :] for c in range(CH)],
                      [LI[:, c, :].bitcast(U32) for c in range(CH)])
                ve.tensor_copy(CV[:, :, bass.ds(h, 1), :].rearrange("p c a n -> p c (a n)"), LV)
                ve.tensor_copy(CI[:, :, bass.ds(h, 1), :].rearrange("p c a n -> p c (a n)").bitcast(U32),
                               LI.bitcast(U32)).then_inc(r_idx, 1)
                ve.wait_ge(r_idx, NHALF + h + 1)
                own.stop(PH)

            link(ve.tensor_copy(CS1, CV[:, :, :, 0:1]))
            flat = lambda t: t.rearrange("p c h k -> p (c h) k")
            ve.tensor_tensor(flat(CV), flat(CV), flat(CS1).broadcast_to([P, CH * PH, TOPK]), ALU.subtract)\
                .then_inc(r_exp_in, 1)
            cu = CI.bitcast(U32)
            ve.tensor_scalar(I1.bitcast(U32), cu, 4, None, ALU.logical_shift_right)
            link(ve.tensor_scalar(I2.bitcast(U32), cu, 15, None, ALU.bitwise_and))
            ve.tensor_copy(X1, I1.bitcast(U32))
            link(ve.tensor_copy(X2, I2.bitcast(U32)))
            iota16 = C("iota")[:, 0:16]
            for c in range(CH):
                for half, (x, out) in enumerate(((X1, I1), (X2, I2))):
                    e4 = E4.rearrange("p (h k) j -> p h k j", h=PH)
                    ks = bc(bc(iota16, 1, PH), 2, TOPK)
                    link(ve.tensor_tensor(e4, bc(x[:, c], 3, 16), ks, ALU.is_equal))
                    names = TI[:, c].rearrange("p (h s) j -> p s h j", s=2)[:, half]
                    link(ve.tensor_tensor(e4, e4, bc(names, 2, TOPK), ALU.mult))
                    link(ve.tensor_reduce(out[:, c].rearrange("p h k -> p (h k)"), E4, AX_X, ALU.add))
            ve.wait_ge(r_exp, 1)
            link(ve.tensor_reduce(flat(CS1).rearrange("p a b -> p (a b)"), flat(CV), AX_X, ALU.add))
            link(ve.reciprocal(CS1, CS1))
            ve.tensor_tensor(flat(GA), flat(CV), flat(CS1).broadcast_to([P, CH * PH, TOPK]), ALU.mult)\
                .then_inc(r_idx, 1)
            for n, dst in enumerate((I1T, I2T, gT[:, :])):
                ve.wait_ge(r_pe, NHALF + n + 1)
                link(ve.tensor_copy(dst, ps[:, 4 + n, 0:T]))
            link(ve.tensor_copy(gh[:, :], gT[:, :]))
            link(ve.tensor_tensor(gl[:, :], gT[:, :], gh[:, :].bitcast(F32), ALU.subtract))
            iota = C("iota")

            with ve.Fori(0, WITH) as i:
                for j in range(8):
                    n = 8 * i + j
                    ve.wait_ge(r_pe, NHALF + 3 + n - 1)
                    for t in range(TOKS):
                        tok = bass.ds(TG * i + TOKS * j + t, 1)
                        ve.tensor_scalar(OH[:, j % 2, 0, t, :], iota, I2T[:, tok], None, ALU.is_equal)
                        for half, g in enumerate((gh, gl)):
                            last = ve.tensor_scalar(OH[:, j % 2, 1 + half, t, :], iota, I1T[:, tok],
                                                    g[:, tok].bitcast(F32), ALU.is_equal, ALU.mult)
                    last.then_inc(oh_ready, 1)
                    ve.wait_ge(r_pe, NHALF + 3 + n + 1)
                    if j == 0:
                        ve.wait_ge(g_stored, 64 * i + 1)
                    ve.tensor_copy(gs[:, bass.ds(i % 2, 1), :, TOKS * j:TOKS * j + TOKS].rearrange(
                                       "p a e t -> p t (a e)"),
                                   ps[:, 2 + j % 2, :].rearrange("p (t e) -> p t e", t=TOKS)).then_inc(g_ev, 1)

            def gate(s, e):
                a = AB[:, s, e, :].rearrange("p (w t) -> p w t", w=WITH)
                g = GB[:, s].rearrange("p w (e t) -> p w e t", e=8)[:, :, e, :]
                link(ve.tensor_tensor(a, a, g, ALU.mult))
                link(ve.tensor_copy(ah[:, 8 * s + e, :], AB[:, s, e, :]))
                ve.tensor_tensor(al[:, 8 * s + e, :], AB[:, s, e, :], ah[:, 8 * s + e, :].bitcast(F32),
                                 ALU.subtract).then_inc(act_ready, 1)

            def take(o, j, i):
                ve.wait_ge(outs_done, OUT0["peer_v"] + i + o + 2)
                ve.tensor_tensor(R[:, j, :], R[:, j, :], ps[:, o % 2, 0:T], ALU.add).then_inc(ev_dve, 1)

            ve.wait_ge(g_ev, 8 * WITH + 1)
            ve.wait_ge(blk_in[0], 64)
            for e in range(8):
                gate(0, e)
            ve.wait_ge(y_init, 1)

            def v_block(i, s, prepare):
                if prepare:
                    ve.wait_ge(blk_in[1 - s], 64 * (i + s + 1))
                    ve.wait_ge(outs_done, OUT0["peer_v"] + 32 * i + 16 * s + 1)
                for u in range(8):
                    if prepare:
                        gate(1 - s, u)
                    for j in range(2):
                        take(16 * s + 2 * u + j, 2 * u + j, 32 * i)

            with ve.Fori(0, BLOCKS // 2 - 1) as i:
                own.start(i, 32)
                for s in range(2):
                    v_block(i, s, True)
                own.stop(BLOCKS // 2 - 1)
            v_block(BLOCKS // 2 - 1, 0, True)
            v_block(BLOCKS // 2 - 1, 1, False)
            norm_dve(ve, link, 1)

        @block.tensor
        def _(pe):
            def product(bank, slot, tiles, mh, ml, u, m_wait=None):
                out = ps[:, bank, 0:T]
                for n, (t, k) in enumerate(tiles):
                    w = wh[:, slot, t * P:t * P + P]
                    if t % 8 == 0:
                        pe.wait_ge(hi_ready, 2 * u + t // 8 + 1)
                    if m_wait and n % m_wait[1] == 0:
                        pe.wait_ge(m_wait[0], n // m_wait[1] + 1)
                    pe.matmul(out, w, mh(k), start=(n == 0), stop=False)
                    pe.matmul(out, w, ml(k), start=False, stop=False)
                for n, (t, k) in enumerate(tiles):
                    if t % 8 == 0:
                        pe.wait_ge(lo_ready, 2 * u + t // 8 + 1)
                    last = pe.matmul(out, wl[:, slot, t * P:t * P + P], mh(k), start=False,
                                     stop=(n == len(tiles) - 1))
                last.then_inc(outs_done, 1)

            def a_op(t):
                return lambda k: t[:, k, :]

            FULL = [(k, k) for k in range(KT)]

            def unit(phase, evicted, ev0, i, j, mh, ml, wait=True, m_wait=None):
                if wait:
                    pe.wait_ge(evicted, ev0 + i + j - 1)
                product(j % 2, j % 2, FULL, mh, ml, UNIT0[phase] + i + j, m_wait)

            def units(phase, n, first, evicted, ev0, t, step=2):
                with pe.Fori(0, n // step) as i:
                    for j in range(step):
                        unit(phase, evicted, ev0, first + step * i, j, a_op(t[0]), a_op(t[1]))

            for s in (h_scores, outs_done):
                pe.sem_inc(s, 1)
            x = (ah, al)
            unit("u", ev_act, 0, 0, 0, a_op(ah), a_op(al), wait=False, m_wait=(x_lo, 4))
            unit("u", ev_act, 0, 0, 1, a_op(ah), a_op(al), wait=False)
            units("u", 6, 2, ev_act, 0, x)
            units("kv", 4, 0, ev_act, ACT_EV0["kv"], x)
            units("q", 8, 0, ev_act, ACT_EV0["q"], x)

            def gate_unit(first, j):
                unit("gates", ev_act, ACT_EV0["gates"], first, j, a_op(ah), a_op(al))

            pe.wait_ge(ev_act, 12)
            pe.wait_ge(consts_in, 16)
            for c in range(2):
                for v in range(2):
                    pe.transpose(TB[:, (2 * c + v) * P:(2 * c + v + 1) * P], V2[:, v, c * P:c * P + P], ident)
            for v in range(2):
                last = pe.transpose(OB[0:NS, v * P:v * P + P], V2[:, v, SEQ:T], ident)
            last.then_inc(v_turned, 1)
            for j in range(SAMPLE_UNITS):
                if j == 2:
                    pe.wait_ge(q_side, 1)
                    pe.wait_ge(caches_in, 32)
                    for b in range(DB):
                        for half in range(2):
                            for g in range(KVH):
                                r = slice(32 * g, 32 * g + 32)
                                out = SB4[:, g, 0:P].rearrange("p (m b i) -> p m b i", m=QG, b=DB)[:, :, b, :]
                                last = pe.matmul(out, KC[r, half, b, :],
                                                 QW[r, half, :, DS * b:DS * b + DS],
                                                 start=(half == 0), stop=(half == 1))
                    last.then_inc(sc_cache, 1)
                if j == 3:
                    pe.wait_ge(sc_copied, 1)
                    pe.wait_ge(v_copied, 2)
                    for g in range(KVH):
                        pe.transpose(TB[:, g * P:g * P + P], CS[:, g, :], ident)
                    for half in range(2):
                        for g in range(KVH):
                            r = slice(32 * g, 32 * g + 32)
                            last = pe.matmul(SB4[:, g, 256:256 + NS], QW[r, half].rearrange("p m t -> p (m t)"),
                                             K2[r, half, SEQ:T], start=(half == 0), stop=(half == 1))
                    last.then_inc(sc_turned, 1)
                if j == 5:
                    pe.wait_ge(s_prob, 1)
                    for g in range(KVH):
                        pe.transpose(TB[:, g * P:g * P + P], SM[:, g, 0:WIN], ident)
                    for g in range(KVH):
                        last = pe.transpose(ps[0:NS, 2, g * P:g * P + P], SM[:, g, WIN:WIN + NS], ident)
                    last.then_inc(s_pt, 1)
                if j == 6:
                    pe.wait_ge(s_ptc, 2)
                    pn = SM[0:NS, 0:2, :].rearrange("p a (b c) -> p (a b) c", b=2)
                    for g in range(KVH):
                        r = slice(64 * (g % 2), 64 * (g % 2) + 64)
                        out = OB[r, P * (g // 2):P * (g // 2) + P]
                        vs = slice(g * HD, g * HD + HD)
                        pe.matmul(out, VS[0:NS, vs], pn[:, g, :], start=True, stop=False)
                        for b in range(DB):
                            cols = out.rearrange("p (m b i) -> p m b i", m=QG, b=DB)[:, :, b, :]
                            pc = CS[:, g, :].rearrange("p (m b i) -> p m b i", m=QG, b=DB)[:, :, b, :]
                            last = pe.matmul(cols, VC[:, b, vs], pc, start=False, stop=(b == DB - 1))
                    last.then_inc(s_pv, 1)
                gate_unit(0, j)

            pe.wait_ge(s_ol, 1)
            with pe.Fori(0, QG) as m:
                first = SAMPLE_UNITS + HEAD_UNITS * m
                for j in range(HEAD_UNITS):
                    if j == 0:
                        pe.wait_ge(h_q, m + 1)
                        pe.wait_ge(h_prob, 2 * m + 1)
                        pe.wait_ge(h_ol, 2 * m + 1)
                        for c in range(2):
                            for half in range(2):
                                for g in range(KVH):
                                    r = slice(32 * g, 32 * g + 32)
                                    out = SB4[:, g, 0:WIN] if c == 0 else SB4[:, g, WIN:3 * WIN]
                                    last = pe.matmul(out, QS[r, half, c * P:c * P + P],
                                                     K2[r, half, 0:WIN * (c + 1)],
                                                     start=(half == 0), stop=(half == 1))
                            last.then_inc(h_scores, 1)
                    if j in (3, 4, 5):
                        n = j - 3
                        c, kb = ((0, 0), (1, 0), (1, 1))[n]
                        pe.wait_ge(h_prob, 2 * m + c + 2)
                        pe.wait_ge(h_ptc, 3 * m + n + 1)
                        src = SM if c == 0 else SP_
                        for g in range(KVH):
                            last = pe.transpose(TB[:, g * P:g * P + P], src[:, g, kb * P:kb * P + P], ident)
                        last.then_inc(h_pt, 1)
                    if j == 5:
                        pe.wait_ge(h_ptc, 3 * m + 2)
                        last = values(pe, 0, [CS])
                        last.then_inc(h_pv, 1)
                    gate_unit(first, j)
                pe.wait_ge(h_ptc, 3 * m + 4)
                pe.wait_ge(h_prob, 2 * m + 3)
                last = values(pe, 1, [PS[:, 0], PS[:, 1]])
                last.then_inc(h_pv, 1)

            pe.wait_ge(ev_act, ACT_EV0["gates"] + 32)
            for u in range(2):
                for o in range(8):
                    n = 8 * u + o
                    if n >= 2:
                        pe.wait_ge(ev_dve, n - 1)
                    g = n // 4
                    product(n % 2, u, [(2 * o, 2 * g), (2 * o + 1, 2 * g + 1)], a_op(bh), a_op(bl),
                            UNIT0["pool"] + u)

            def pairs(phase, first, i, j, mh, ml):
                for o in range(2):
                    pe.wait_ge(ev_dve, DVE_EV0[phase] + 2 * i + 2 * j + o - 1)
                    product(o, j % 2, [(8 * o + k, k) for k in range(8)], mh, ml, UNIT0[phase] + i + j)

            pe.wait_ge(h_ol, 2 * QG + 1)
            with pe.Fori(0, 4) as i:
                for j in range(2):
                    pairs("attn", 0, 2 * i, j, lambda k: bh[:, 8 + k, :], lambda k: bl[:, 8 + k, :])

            def tile_sum(e, first=False, last=False, done=None):
                if done is not None:
                    pe.wait_ge(ev_dve, done)
                r = R[:, e:e + 1, :] if isinstance(e, int) else R[:, bass.ds(e, 1), :]
                mm = pe.matmul(TB[:, 0:T].unsqueeze(1), ones[:, :], r, start=first, stop=last)
                if last:
                    mm.then_inc(ln_pe, 1)

            def out_unit(i, j, m_wait=None):
                unit("out", ev_dve, DVE_EV0["out"], i, j, a_op(ah), a_op(al), m_wait=m_wait)

            e0 = DVE_EV0["out"]
            out_unit(0, 0, m_wait=(m_split, 1))
            out_unit(0, 1)
            tile_sum(0, first=True, done=e0 + 1)
            with pe.Fori(1, 8) as i:
                out_unit(2 * i, 0)
                tile_sum(2 * i - 1, done=e0 + 2 * i)
                out_unit(2 * i, 1)
                tile_sum(2 * i, done=e0 + 2 * i + 1)
            tile_sum(15, last=True, done=e0 + 16)

            def norm_pe(n):
                for e in range(KT):
                    pe.wait_ge(ln_act, (KT + 3) * n + e + 2)
                    last = pe.matmul(OB[:, 0:T], ones[:, :], SQ[:, e, :], start=(e == 0), stop=(e == KT - 1))
                last.then_inc(ln_pe, 1)

            norm_pe(0)

            def q_unit(i, j, m_wait=None):
                unit("query", ev_act, ACT_EV0["query"], i, j, a_op(bh), a_op(bl), m_wait=m_wait)

            def key_scores(l, j):
                pe.wait_ge(ev_act, ACT_EV0["query"] + l + 1)
                pe.wait_ge(sc_ev, l + 1)
                rhs = SK[:, bass.ds(l, 1), :] if not isinstance(l, int) else SK[:, l:l + 1, :]
                for c, n in ((0, P), (1, P), (2, NS)):
                    last = pe.matmul(ps[0:n, 2 + j:3 + j, c * P:c * P + P], QT[:, j, c * P:c * P + n], rhs,
                                     start=True, stop=True)
                last.then_inc(r_pe, 1)

            q_unit(0, 0, m_wait=(n_lo, 1))
            pe.wait_ge(keys_in, 16)
            with pe.Fori(0, 7) as i:
                q_unit(2 * i, 1)
                key_scores(2 * i, 0)
                q_unit(2 * i + 2, 0)
                key_scores(2 * i + 1, 1)
            q_unit(14, 1)
            key_scores(14, 0)
            key_scores(15, 1)

            def u_unit(i, j):
                unit("peer_u", ev_act, ACT_EV0["peer_u"], i, j, a_op(bh), a_op(bl))

            with pe.Fori(0, BEFORE) as i:
                for j in range(8):
                    u_unit(8 * i, j)
            pe.wait_ge(r_idx, NHALF + PH + 1)
            for src, dst in ((I1, ps[:, 4, :]), (I2, ps[:, 5, :]), (GA, ps[:, 6, :])):
                for c, n in ((0, P), (1, P), (2, NS)):
                    last = pe.transpose(dst[:, c * P:c * P + n],
                                        src[0:n, c].rearrange("p h k -> p (h k)"), ident[0:n, 0:n])
                last.then_inc(r_pe, 1)
            with pe.Fori(0, WITH) as i:
                for j in range(8):
                    n = 8 * i + j
                    pe.wait_ge(oh_ready, n + 1)
                    if j >= 2:
                        pe.wait_ge(g_ev, n)
                    else:
                        pe.wait_ge(g_ev, 8 * i + 1)
                    for t in range(TOKS):
                        for half in range(2):
                            last = pe.matmul(ps[:, 2 + j % 2, t * P:t * P + P], OH[:, j % 2, 0, t, :],
                                             OH[:, j % 2, 1 + half, t, :], start=(half == 0), stop=(half == 1))
                    last.then_inc(r_pe, 1)
                    u_unit(8 * (BEFORE + i), j)
            with pe.Fori(BEFORE + WITH, BLOCKS) as i:
                for j in range(8):
                    u_unit(8 * i, j)

            pe.wait_ge(ev_act, ACT_EV0["peer_u"] + 128)
            pe.wait_ge(act_ready, 8)

            def v_unit(i, s, j):
                pairs("peer_v", 0, 16 * i + 8 * s, j,
                      lambda k: ah[:, 8 * s + k, :], lambda k: al[:, 8 * s + k, :])

            with pe.Fori(0, BLOCKS // 2 - 1) as i:
                for s in range(2):
                    pe.wait_ge(act_ready, 16 * i + 8 * s + 8)
                    for j in range(8):
                        v_unit(i, s, j)
            pe.wait_ge(act_ready, 8 * BLOCKS - 8)
            with pe.Fori(0, 4) as n:
                for j in range(2):
                    pairs("peer_v", 0, 112 + 2 * n, j, a_op(ah), a_op(al))
            pe.wait_ge(act_ready, 8 * BLOCKS)
            e0 = DVE_EV0["peer_v"] + 16 * (BLOCKS - 1)
            for j in range(8):
                v_unit(BLOCKS // 2 - 1, 1, j)
                if j > 0:
                    for e in (2 * j - 2, 2 * j - 1):
                        tile_sum(e, first=(e == 0), done=e0 + e + 1)
            for e in (14, 15):
                tile_sum(e, last=(e == 15), done=e0 + e + 1)
            norm_pe(1)


def _axes(a, shape, order):
    return np.ascontiguousarray(a.reshape(shape).transpose(order))


def kernel(x_prompt, x_sample, cache_k, cache_v, state_pool, w_in, b_in, attn_sinks, w_attn_br,
           w_pool, pool_scale, w_out, ln1_g, ln1_b, w_query, sub_keys, peer_u, peer_v, ln2_g, ln2_b):
    import concourse.bacc as bacc
    from concourse.bass_utils import run_bass_kernel_spmd

    r = np.arange(32)
    halves = [np.concatenate([h * HD + 32 * s + r for h in hs])
              for hs in [[QG * g + m for g in range(KVH)] for m in range(QG)] for s in range(2)]
    keys = [AW + np.concatenate([g * HD + 32 * s + r for g in range(KVH)]) for s in range(2)]
    cols = np.concatenate([np.arange(AW + 2 * KW, AW + 2 * KW + PW), *keys, np.arange(AW + KW, AW + 2 * KW),
                           *halves, np.arange(AW + 2 * KW + PW, w_in.shape[1])])
    rows = np.concatenate([(QG * (2 * gh + gl) + m) * HD + np.arange(HD)
                           for gh in range(2) for m in range(QG) for gl in range(2)])
    x = np.concatenate([np.asarray(x_prompt).reshape(SEQ, D), np.asarray(x_sample).reshape(NS, D)])
    (cache_k, cache_v, state_pool, w_in, b_in, attn_sinks, w_attn_br, w_pool, pool_scale, w_out, ln1_g, ln1_b,
     w_query, sub_keys, peer_u, peer_v, ln2_g, ln2_b) = (np.asarray(a) for a in (
         cache_k, cache_v, state_pool, w_in, b_in, attn_sinks, w_attn_br, w_pool, pool_scale, w_out, ln1_g,
         ln1_b, w_query, sub_keys, peer_u, peer_v, ln2_g, ln2_b))
    unit = KT * P
    st = np.zeros((P, 8, 16 + DB * 16), np.float32)
    st[:, :, 16:].reshape(P, 8, DB, 16)[..., 1:] = state_pool.reshape(DB, HIST, 8, P).transpose(3, 2, 0, 1)
    vecs = np.concatenate([
        b_in[cols].reshape(52, P).T, pool_scale.reshape(16, P).T,
        np.broadcast_to(attn_sinks.reshape(KVH, QG).T.reshape(1, HEADS), (P, HEADS)),
        np.repeat(attn_sinks.reshape(KVH, QG).T, NS, axis=0),
        ln1_g.reshape(KT, P).T, ln1_b.reshape(KT, P).T, ln2_g.reshape(KT, P).T, ln2_b.reshape(KT, P).T], axis=1)
    ins = {
        "xT": _axes(x, (T, KT, P), (2, 1, 0)),
        "w_in": _axes(w_in[:, cols], (KT, P, 52, P), (2, 1, 0, 3)).reshape(52, P, unit),
        "w_pool": _axes(w_pool, (2, 2, 2, P, 4, P), (0, 3, 1, 4, 2, 5)).reshape(2, P, unit),
        "w_attn": _axes(w_attn_br[rows], (8, P, 8, 2, P), (2, 1, 3, 0, 4)).reshape(8, P, unit),
        "w_out": _axes(w_out, (KT, P, KT, P), (2, 1, 0, 3)).reshape(16, P, unit),
        "w_query": _axes(w_query, (KT, P, NHALF, P), (2, 1, 0, 3)).reshape(16, P, unit),
        "keysT": _axes(sub_keys, (NHALF, NK, HK), (2, 0, 1)),
        "peer_u": _axes(peer_u, (P, P, KT, P), (0, 3, 2, 1)).reshape(128, P, unit),
        "peer_v": _axes(peer_v, (BLOCKS, 8, P, 8, 2, P), (0, 3, 2, 4, 1, 5)).reshape(128, P, unit),
        "vecs": np.ascontiguousarray(vecs),
        "consts": const_table(),
        "kcT": _axes(cache_k, (DB, WIN, KVH, 2, 32), (2, 4, 3, 0, 1)).reshape(P, 2, DB, WIN),
        "vc": _axes(cache_v, (DB, WIN, KW), (1, 0, 2)),
        "stT": st,
        "k_nat": np.ascontiguousarray(cache_k.reshape(DB, WIN, KW)),
        "st_nat": np.ascontiguousarray(state_pool),
    }
    outs = {"yT": (P, KT, T), "kT": (P, 2, T), "vT": (P, 2, T), "uT": (P, 8, HIST), "us": (P, 8, DB, DS),
            "k_shift": (DB, WIN - DS, KW), "v_shift": (WIN - DS, DB, KW), "st_shift": (DB, HIST - DS, PW)}
    nc = bacc.Bacc("TRN2", target_bir_lowering=False, num_devices=1)
    args = [nc.dram_tensor(f"in_{k}", a.shape, F32, kind="ExternalInput").ap() for k, a in ins.items()]
    args += [nc.dram_tensor(f"out_{k}", s, F32, kind="ExternalOutput").ap() for k, s in outs.items()]
    layer(nc, *args)
    got = run_bass_kernel_spmd(nc, [{f"in_{k}": a for k, a in ins.items()}], core_ids=[0]).results[0]
    yT, kT, vT, uT, us, k_shift, v_shift, st_shift = (got[f"out_{k}"] for k in outs)
    y = yT.transpose(2, 1, 0).reshape(T, D)
    k = kT.reshape(KVH, 32, 2, T).transpose(3, 0, 2, 1).reshape(T, KVH, HD)
    v = vT.transpose(2, 1, 0).reshape(T, KVH, HD)
    u_new = us.transpose(2, 3, 1, 0).reshape(DB, DS, PW)
    k_new, v_new = (a[SEQ:].reshape(DB, DS, KVH, HD) for a in (k, v))
    return (np.ascontiguousarray(y[:SEQ]).reshape(1, SEQ, D), np.ascontiguousarray(y[SEQ:]).reshape(DB, DS, D),
            np.ascontiguousarray(k[SEQ - WIN:SEQ])[None], np.ascontiguousarray(v[SEQ - WIN:SEQ])[None],
            np.ascontiguousarray(uT.transpose(2, 1, 0).reshape(1, HIST, PW)),
            np.concatenate([k_shift.reshape(DB, WIN - DS, KVH, HD), k_new], axis=1),
            np.concatenate([v_shift.transpose(1, 0, 2).reshape(DB, WIN - DS, KVH, HD), v_new], axis=1),
            np.concatenate([st_shift, u_new], axis=1))
```

```python
from contextlib import ExitStack

import numpy as np

import concourse.bass as bass
from concourse import mybir

F32 = mybir.dt.float32
F32R = mybir.dt.float32r
U32 = mybir.dt.uint32
ALU = mybir.AluOpType
ACT = mybir.ActivationFunctionType
AX_X = mybir.AxisListType.X

P = 128
D = 2048
SEQ = 256
DB, DS = 8, 4
NS = DB * DS
T = SEQ + NS
PAST = 2048
HEADS, KVH, HD = 16, 4, 64
QG = HEADS // KVH
AW, KW = HEADS * HD, KVH * HD
WIN = 128
PW = D // 2
HIST = 15
PG = 4
PH, NK, HK, TOPK = 8, 128, 128, 16
ALPHA = 2.0 ** 0.25
EPS = 1e-5
NEG = -1e30
SCALE = HD ** -0.5
KT = D // P
HU = KT * P // 2
CH = 3
NHALF = 2 * PH

PHASES = {"u": (8, 1), "kv": (4, 1), "q": (8, 1), "gates": (32, 1), "pool": (2, 8), "attn": (8, 2),
          "out": (16, 1), "query": (16, 1), "peer_u": (128, 1), "peer_v": (128, 2)}
UNIT0, OUT0 = {}, {}
_u = _o = 0
for _name, (_n, _k) in PHASES.items():
    UNIT0[_name], OUT0[_name] = _u, _o
    _u += _n
    _o += _n * _k
UNITS = _u
ACT_EV0 = {"u": 0, "kv": 8, "q": 12, "gates": 20, "query": 52, "peer_u": 68}
DVE_EV0 = {"pool": 0, "attn": 16, "out": 32, "peer_v": 48}

SAMPLE_UNITS = 8
HEAD_UNITS = (32 - SAMPLE_UNITS) // QG
POOL_PAIRS = (range(1, 4), range(1, 8))
AFFINE = (0, 12)
BLOCKS = 16
BEFORE, WITH = 5, 9
TOKS = T // (WITH * 8)
TG = TOKS * 8

CONST = {}
_c = 0
for _name, _n in (("ident", 128), ("cos", T), ("sin", T), ("mask", 2 * WIN), ("smask", WIN + NS),
                  ("ratio", PG * 16), ("iota", 128)):
    CONST[_name] = (_c, _c + _n)
    _c += _n
CONSTS = _c
VEC = {}
_c = 0
for _name, _n in (("b_in", 52), ("scale", 16), ("sink", 16), ("ssink", 4), ("g1", 16), ("b1", 16),
                  ("g2", 16), ("b2", 16)):
    VEC[_name] = (_c, _c + _n)
    _c += _n
VECS = _c


def const_table():
    t = np.zeros((P, CONSTS), np.float32)

    def put(name, a):
        t[:, CONST[name][0]:CONST[name][1]] = a

    put("ident", np.eye(P))
    half = HD // 2
    inv = np.float32(10000.0) ** (-np.arange(half, dtype=np.float32) / np.float32(half))
    pos = np.concatenate([np.arange(SEQ), PAST + np.tile(np.arange(DS), DB)]).astype(np.float32)
    ang = (pos[None, :] * inv.astype(np.float32)[:, None]).astype(np.float32)
    put("cos", np.tile(np.cos(ang), (4, 1)))
    put("sin", np.tile(np.sin(ang), (4, 1)))
    i, j = np.arange(P)[:, None], np.arange(2 * WIN)[None, :]
    put("mask", np.where((j <= WIN + i) & (j > i), 0.0, NEG))
    row = np.arange(P)[:, None]
    b, i = row % NS // DS, row % DS
    j = np.arange(WIN)[None, :]
    new = np.arange(NS)[None, :]
    put("smask", np.concatenate([np.where(j > i, 0.0, NEG),
                                 np.where((new // DS == b) & (new % DS <= i), 0.0, NEG)], 1))
    w = np.array([2, 4, 8, 16])[:, None]
    put("ratio", (w / np.minimum(w, np.arange(16)[None, :] + 1)).astype(np.float32).reshape(1, -1))
    put("iota", np.arange(128)[None, :])
    return t


class Tally:

    def __init__(self, sem):
        self.sem, self.base, self.k = sem, 0, 0

    def inc(self, instruction):
        instruction.then_inc(self.sem, 1)
        self.k += 1
        return self.base + self.k

    def start(self, i, per):
        self.saved, self.per = self.k, per
        self.base, self.k = self.saved + i * per, 0

    def stop(self, n):
        assert self.k == self.per, (self.k, self.per)
        self.base, self.k = 0, self.saved + n * self.per


def layer(nc, xT, w_in, w_pool, w_attn, w_out, w_query, keysT, peer_u, peer_v, vecs, consts,
          kcT, vc, stT, k_nat, st_nat,
          yT, kT, vT, uT, us, k_shift, v_shift, st_shift):
    ctx = ExitStack()
    with ctx:
        def sb(name, shape, dt=F32):
            return ctx.enter_context(nc.sbuf_tensor(name, shape, dt))

        def sem(name):
            return ctx.enter_context(nc.semaphore(name))

        a_dram = nc.dram_tensor("gelu_scratch", (2 * BLOCKS, P, 4 * T), F32, kind="Internal").ap()
        g_dram = nc.dram_tensor("gate_scratch", (BLOCKS, P, WITH, 8 * TG), F32, kind="Internal").ap()

        raw = sb("raw", [P, 2, KT * P])
        wh = sb("w_hi", [P, 2, KT * P], F32R)
        wl = sb("w_lo", [P, 2, KT * P], F32R)
        R = sb("R", [P, KT, T])
        bh = sb("b_hi", [P, KT, T], F32R)
        bl = sb("b_lo", [P, KT, T], F32R)
        vec = sb("vec", [P, VECS])
        cst = sb("cst", [P, CONSTS])
        ones = sb("ones", [P, P])
        tiny = sb("tiny", [P, 2])
        with (nc.sbuf_tensor("g_stage", [P, 2, P, TG], F32) as gs,
              nc.sbuf_tensor("gate_T", [P, T], F32) as gT,
              nc.sbuf_tensor("gate_hi", [P, T], F32R) as gh,
              nc.sbuf_tensor("gate_lo", [P, T], F32R) as gl):
            pass
        ah = sb("a_hi", [P, KT, T], F32R)
        al = sb("a_lo", [P, KT, T], F32R)
        head = 2 * 4 * T + 2 * 2 * 8 * T
        with (nc.sbuf_tensor("arena_head", [P, head], F32),
              nc.sbuf_tensor("onehots", [P, 2, 3, TOKS, P], F32R) as OH):
            pass
        F = sb("F", [P, (212863 - 4 * (6 * KT * P + 5 * KT * T + VECS + CONSTS + P)) // 4 - 64])

        def carve(off, *shape):
            n = int(np.prod(shape))
            assert off + n <= F.shape[1], (off, shape, F.shape)
            ap = F[:, off:off + n]
            names = "abcd"[:len(shape)]
            if len(shape) > 1:
                ap = ap.rearrange(f"p ({' '.join(names)}) -> p {' '.join(names)}",
                                  **dict(zip(names, shape)))
            return ap, off + n

        GG, o_front = carve(0, 32, T)
        UP, o = carve(o_front, 8, 16 + SEQ)
        US, o = carve(o, 8, DB, 20)
        PT = []
        for _ in range(2):
            t1, o = carve(o, 2, 16 + SEQ)
            t2, o = carve(o, 2, DB, 20)
            PT.append((t1, t2))
        PD, o = carve(o, 2, T)
        QK = R[:, 0:8, :]
        K2 = R[:, 8:10, :]
        V2 = R[:, 10:12, :]
        KK = R[:, 10:12, :]
        RT = [R[:, 12:16, :], None]
        QD = R[:, 12:16, :].rearrange("p a t -> p (a t)")[:, 0:2 * DB * 64].rearrange(
            "p (h b n) -> p h b n", h=2, b=DB)
        RT[1], _ = carve(o_front + 8 * (16 + SEQ) + 8 * DB * 20, 4, T)
        KC, o = carve(o_front, 2, DB, P)
        VC, o = carve(o, DB, KW)
        CS, o2 = carve(o_front + 2 * DB * P + DB * KW, 4, P)
        SM, o2 = carve(o2, 4, 2 * WIN)
        VN, o2 = carve(o2, 2, KW)
        VS, o2 = carve(o2, KW)
        SX, o2 = carve(o2, 4, 8)
        QW, o2 = carve(o2, 2, QG, NS)
        PS, o = carve(o_front, 2, 4, P)
        QS, o = carve(o, 2, T)
        SP_, o = carve(o, 4, 2 * WIN)
        SUMS = GG[:, 22:26, :].rearrange("p (k j) t -> p k j t", k=2)
        SQ = GG[:, 26:28, :]
        VAR, RSTD, TMP, MEAN = (GG[:, 28 + n, :] for n in range(4))
        ST, o_st = carve(0, 2, 4, T)
        SK, o = carve(0, NHALF, P)
        QT, o = carve(o, 2, T)
        SC, o = carve(o, CH, NHALF, P)
        TV, o = carve(o, CH, NHALF, TOPK)
        TI, o = carve(o, CH, NHALF, TOPK)
        CV, o = carve(o, CH, PH, TOPK)
        CI, o = carve(o, CH, PH, TOPK)
        LS, o = carve(o, CH, TOPK * TOPK)
        LV, o = carve(o, CH, TOPK)
        LI, o = carve(o, CH, TOPK)
        X1, o = carve(o, CH, PH, TOPK)
        X2, o = carve(o, CH, PH, TOPK)
        GA, o = carve(o, CH, PH, TOPK)
        I1, o = carve(o, CH, PH, TOPK)
        I2, o = carve(o, CH, PH, TOPK)
        CS1, o = carve(o, CH, PH, 1)
        E4, _ = carve(o, PH * TOPK, TOPK)
        AB, o_ab = carve(o_st, 2, 8, T)
        GB, o_ab = carve(o_ab, 2, WITH, 8 * TG)
        assert o_ab == head
        I1T, o_ab = carve(max(o, o_ab + 6 * TOKS * P), T)
        I2T, o_ab = carve(o_ab, T)
        GS, o_ab = carve(o_ab, TOKS, P)

        ps = ctx.enter_context(nc.psum_tensor("ps", [P, 8, 512], F32))
        SB4 = ps[:, 2:6, :]
        TB = ps[:, 6, :]
        OB = ps[:, 7, :]
        LNP = (OB[:, 0:T], ps[:, 2, 0:T])
        HO = (OB[:, 0:256], OB[:, 256:512])
        ident = cst[:, CONST["ident"][0]:CONST["ident"][1]]

        def C(name):
            return cst[:, CONST[name][0]:CONST[name][1]]

        def V(name):
            return vec[:, VEC[name][0]:VEC[name][1]]

        loaded = [sem(f"half_loaded_{n}") for n in range(4)]
        hi_ready, lo_ready = sem("hi_ready"), sem("lo_ready")
        outs_done = sem("outs_done")
        ev_act, ev_dve = sem("evicted_by_act"), sem("evicted_by_dve")
        x_loaded = [sem(f"x_loaded_{n}") for n in range(4)]
        vec_in = sem("vec_in")
        x_hi, x_lo = sem("x_hi_ready"), sem("x_lo_ready")
        consts_in, caches_in, state_in, keys_in, x_again = (
            sem(n) for n in ("consts_in", "caches_in", "state_in", "keys_in", "x_again"))
        d_split, k_rope, q_rope = sem("pooled_split"), sem("k_rotated"), sem("q_rotated")
        q_side = sem("sample_q_side_by_side")
        dve = sem("dve_order")
        v_turned, v_copied = sem("v_turned"), sem("v_copied")
        sc_cache, sc_copied, sc_turned = sem("s_cache_scores"), sem("s_scores_copied"), sem("s_scores_turned")
        s_sm, s_exp, s_prob = sem("s_shifted"), sem("s_exp"), sem("s_probs")
        s_pt, s_ptc, s_pv, s_oh, s_ol = (sem(n) for n in (
            "s_probs_turned", "s_probs_copied", "s_pv", "s_o_hi", "s_o_lo"))
        h_q, h_scores, h_sm, h_exp, h_prob = (sem(n) for n in (
            "h_q_staged", "h_scores", "h_shifted", "h_exp", "h_probs"))
        h_pt, h_ptc, h_pv, h_oh, h_ol = (sem(n) for n in (
            "h_probs_turned", "h_probs_copied", "h_pv", "h_o_hi", "h_o_lo"))
        m_split = sem("merged_split")
        ln_pe, ln_dve, n_aff, n_hi, n_lo = (sem(n) for n in (
            "ln_pe", "ln_dve", "ln_scaled", "h_hi", "h_lo"))
        n_full, y_affine = sem("h_ready"), sem("y_affine_by_dve")
        ln_mean, ln_pcentred = sem("ln_mean"), sem("ln_centred_by_pool")
        ln_centred, ln_var, ln_sqrt, y_normed = (sem(n) for n in (
            "ln_centred", "ln_variance", "ln_sqrt", "y_normed"))
        sc_ev = sem("key_scores_copied")
        r_pe, r_exp_in, r_exp, r_idx = (sem(n) for n in (
            "route_pe", "route_shifted", "route_exp", "route_choices"))
        oh_ready, g_ev, g_stored = sem("onehots_ready"), sem("gates_evicted"), sem("gates_stored")
        a_stored = [sem("gelu_stored_0"), sem("gelu_stored_1")]
        blk_in = [sem("block_in_0"), sem("block_in_1")]
        act_ready, y_init = sem("gated_ready"), sem("y_init")
        stored, u_stored, kv_stored = sem("outputs_stored"), sem("u_stored"), sem("kv_stored")
        ones_set = sem("ones_set")

        block = ctx.enter_context(nc.Block())

        def bc(ap, axis, n):
            a = ap.unsqueeze(axis)
            shape = list(a.shape)
            shape[axis] = n
            return a.broadcast_to(shape)

        def block_piece(sp, b, s, n, i=None):
            if n < 2:
                dst, src = AB[:, s, 4 * n:4 * n + 4, :].rearrange("p e t -> p (e t)"), \
                    a_dram[bass.ds(2 * b + n, 1)].rearrange("a p n -> p (a n)")
            else:
                w = slice(0, 5) if n == 2 else slice(5, WITH)
                dst, src = GB[:, s, w, :], g_dram[bass.ds(b, 1), :, w, :].rearrange("a p w n -> p (a w) n")
            if n == 0 and i is not None:
                sp.wait_ge(act_ready, 8 * (2 * i + s + 1))
                for m in range(2):
                    sp.wait_ge(a_stored[m], 16 * (2 * i + s + 3) + 1)
            sp.dma_start(dst, src).then_inc(blk_in[s], 16)

        def gate_bank(j, t):
            return ps[:, 2 + 2 * (j % 2) + t // 2, 256 * (t % 2):256 * (t % 2) + 256].rearrange(
                "p (s e) -> p s e", s=2)

        def own_rows(t, odd):
            return t[64 * odd:64 * odd + 64, 8:16, SEQ:T].rearrange("p (a n) t -> p a n t", a=2)

        def own_cols(odd):
            return OB[64 * odd:64 * odd + 64, :].rearrange("p (a g n t) -> p a g n t", a=2, g=2, n=QG)[:, :, odd]

        def o_tiles(t, m, c):
            return t[:, 8:16, c * P:c * P + P].rearrange("p (a b) t -> p a b t", a=2)[
                :, :, bass.ds(m, 1), :].rearrange("p a b t -> p a (b t)")

        def norm_first(ve, own, link, n, done, take):
            def pair(i):
                return R[:, 2 * i:2 * i + 2, :] if isinstance(i, int) else R[:, bass.ds(2 * i, 2), :]

            def centre(i):
                return ve.scalar_tensor_tensor(out=pair(i), in0=bc(TB[:, 0:T], 1, 2), scalar=-float(KT // 2),
                                               in1=pair(i), op0=ALU.mult, op1=ALU.add)

            def centre_one(e):
                return ve.scalar_tensor_tensor(out=R[:, e, :], in0=TB[:, 0:T], scalar=-float(KT // 2),
                                               in1=R[:, e, :], op0=ALU.mult, op1=ALU.add)

            def add(i, mark):
                mark(centre(i))
                mark(ve.tensor_tensor(SQ, pair(i), pair(i), ALU.mult))
                ve.tensor_tensor(SUMS[:, 0], SUMS[:, 0], pair(i), ALU.add)
                mark(ve.tensor_tensor(SUMS[:, 1], SUMS[:, 1], SQ, ALU.add))

            link(ve.memset(SUMS, 0.0))
            for j in range(2):
                take(0, j)
            ve.wait_ge(ev_dve, done + 2)
            ve.tensor_tensor(SQ[:, 0], R[:, 0, :], R[:, 1, :], ALU.add).then_inc(ln_dve, 1)
            for j in range(2):
                take(1, j)
            ve.wait_ge(ln_pe, 3 * n + 1)
            add(0, link)
            take(2, 0)
            add(1, link)
            take(2, 1)
            with ve.Fori(3, 7) as i:
                own.start(i - 3, 3)
                ve.wait_ge(ev_dve, done + 2 * i)
                add(i - 1, link)
                take(i, 0)
                take(i, 1)
                own.stop(4)
            ve.wait_ge(ev_dve, done + 14)
            add(6, link)
            take(7, 0)
            ve.wait_ge(ev_dve, done + 15)
            link(centre_one(14))
            link(ve.tensor_tensor(SQ[:, 0], R[:, 14, :], R[:, 14, :], ALU.mult))
            ve.tensor_tensor(SUMS[:, 0, 0], SUMS[:, 0, 0], R[:, 14, :], ALU.add)
            link(ve.tensor_tensor(SUMS[:, 1, 0], SUMS[:, 1, 0], SQ[:, 0], ALU.add))
            ve.tensor_tensor(SUMS[:, :, 0], SUMS[:, :, 0], SUMS[:, :, 1], ALU.add).then_inc(ln_dve, 1)
            take(7, 1)
            ve.wait_ge(ev_dve, done + 16)
            centre_one(15).then_inc(ln_dve, 1)
            ve.wait_ge(ln_dve, 4 * n + 3)
            ve.tensor_tensor(SQ[:, 1], R[:, 15, :], R[:, 15, :], ALU.mult).then_inc(ln_dve, 1)

        def norm_last(ve, link, n):
            by_pool = [2 * p + j for p in POOL_PAIRS[n] for j in range(2)]
            own_tiles = [e for e in range(KT) if e not in by_pool]
            affs = len(POOL_PAIRS[0]) * n, (KT - 2 * len(POOL_PAIRS[0])) * n

            def centre(e):
                ve.tensor_tensor(R[:, e, :], R[:, e, :], MEAN, ALU.subtract).then_inc(ln_centred, 1)

            def affine(e):
                if n == 0:
                    ve.wait_ge(n_hi, e + 1)
                    g, b, done = V("g1"), V("b1"), n_full
                else:
                    ve.wait_ge(n_aff, KT + e + 1)
                    g, b, done = V("g2"), V("b2"), y_affine
                ve.tensor_scalar(R[:, e, :], R[:, e, :], g[:, e:e + 1], b[:, e:e + 1], ALU.mult, ALU.add)\
                    .then_inc(done, 1)

            ve.wait_ge(ln_pe, 3 * n + 2)
            ve.tensor_copy(MEAN, LNP[0]).then_inc(ln_mean, 1)
            ve.wait_ge(ln_mean, n + 1)
            link(ve.tensor_tensor(VAR, MEAN, MEAN, ALU.mult))
            ve.wait_ge(ln_pe, 3 * n + 3)
            ve.scalar_tensor_tensor(out=TMP, in0=LNP[1], scalar=EPS, in1=VAR, op0=ALU.add, op1=ALU.subtract)\
                .then_inc(ln_var, 1)
            for e in own_tiles[:2]:
                centre(e)
            ve.wait_ge(ln_sqrt, n + 1)
            link(ve.reciprocal(RSTD, VAR))
            link(ve.tensor_tensor(VAR, RSTD, RSTD, ALU.mult))
            link(ve.scalar_tensor_tensor(out=VAR, in0=VAR, scalar=-0.5, in1=TMP, op0=ALU.mult, op1=ALU.mult))
            link(ve.scalar_tensor_tensor(out=RSTD, in0=VAR, scalar=1.5, in1=RSTD, op0=ALU.add, op1=ALU.mult))
            for e in range(KT):
                if e + 2 < len(own_tiles):
                    centre(own_tiles[e + 2])
                if e in by_pool:
                    ve.wait_ge(ln_pcentred, affs[0] + by_pool.index(e) // 2 + 1)
                else:
                    ve.wait_ge(ln_centred, affs[1] + own_tiles.index(e) + 1)
                ve.tensor_tensor(R[:, e, :], R[:, e, :], RSTD, ALU.mult).then_inc(n_aff, 1)
                if e - 2 >= AFFINE[n]:
                    affine(e - 2)
            for e in range(KT - 2, KT):
                affine(e)

        def norm_pool(pool, n):
            pool.wait_ge(ln_mean, n + 1)
            for p in POOL_PAIRS[n]:
                r = R[:, 2 * p:2 * p + 2, :]
                pool.tensor_tensor(r, r, bc(MEAN, 1, 2), ALU.subtract).then_inc(ln_pcentred, 1)

        def norm_act(act, n):
            act.wait_ge(ln_var, n + 1)
            act.activation(VAR, TMP, ACT.Sqrt).then_inc(ln_sqrt, 1)

        def norm_c(pe, n):
            pe.wait_ge(ln_dve, 4 * n + 1)
            pe.matmul(TB[:, 0:T], ones[:, :], SQ[:, 0], start=True, stop=True).then_inc(ln_pe, 1)

        def norm_sums(pe, n):
            pe.wait_ge(ln_dve, 4 * n + 2)
            for k in range(2):
                pe.matmul(LNP[k], ones[:, :], SUMS[:, k, 0], start=True, stop=False)
            for k, last_tile in enumerate((R[:, 15, :], SQ[:, 1])):
                pe.wait_ge(ln_dve, 4 * n + 3 + k)
                pe.matmul(LNP[k], ones[:, :], last_tile, start=False, stop=True).then_inc(ln_pe, 1)

        def values(pe, c, probs):
            for g in range(KVH):
                r = slice(64 * (g % 2), 64 * (g % 2) + 64)
                out = HO[c][r, P * (g // 2):P * (g // 2) + P]
                for kb, pr in enumerate(probs):
                    last = pe.matmul(out, VN[:, kb, g * HD:g * HD + HD], pr[:, g, :],
                                     start=(kb == 0), stop=(kb == len(probs) - 1))
            return last


        @block.sync
        def _(sp):
            def load(src, u0, i, j):
                for h in range(2):
                    sp.wait_ge(lo_ready, 2 * (u0 + j) + h - 3 + i * 4)
                    sp.dma_start(raw[:, j % 2, h * HU:h * HU + HU], src[:, h * HU:h * HU + HU])\
                        .then_inc(loaded[2 * (j % 2) + h], 16)

            def stream(src, u0, n, first=0):
                with sp.Fori(0, n // 2) as i:
                    for j in range(2):
                        load(src[first + 2 * i + j], u0, i, j)

            for n in range(4):
                sp.dma_start(R[:, 4 * n:4 * n + 4, :], xT[:, 4 * n:4 * n + 4, :]).then_inc(x_loaded[n], 16)
                if n in (0, 1):
                    for j in range(2):
                        sp.dma_start(raw[:, j, n * HU:n * HU + HU], w_in[j, :, n * HU:n * HU + HU])\
                            .then_inc(loaded[2 * j + n], 16)
            sp.dma_start(vec[:, :], vecs).then_inc(vec_in, 16)
            sp.wait_ge(lo_ready, 3)
            stream(w_in, 2, 2, first=2)
            sp.dma_start(cst[:, :], consts).then_inc(consts_in, 16)
            sp.dma_start(UP[:, :, 0:16], stT[:, 0:8, 0:16]).then_inc(state_in, 16)
            sp.dma_start(US[:, :, :, 0:16], stT[:, :, 16:16 + DB * 16].rearrange("p a (b s) -> p a b s", b=DB))\
                .then_inc(state_in, 16)
            stream(w_in, 4, 20, first=4)
            sp.wait_ge(d_split, PG)
            sp.wait_ge(u_stored, 32)
            sp.wait_ge(q_rope, 1)
            sp.dma_start(KC, kcT).then_inc(caches_in, 16)
            sp.dma_start(VC, vc).then_inc(caches_in, 16)
            stream(w_in, 24, 28, first=24)
            for n in range(2):
                load(w_pool[n], UNIT0["pool"], 0, n)
            stream(w_attn, UNIT0["attn"], 8)
            sp.wait_ge(h_pv, 2 * QG)
            sp.wait_ge(kv_stored, 32)
            sp.dma_start(R[:, :, :], xT).then_inc(x_again, 16)
            stream(w_out, UNIT0["out"], 8)
            sp.wait_ge(m_split, KT)
            sp.dma_start(SK, keysT).then_inc(keys_in, 16)
            stream(w_out, UNIT0["out"] + 8, 8, first=8)
            stream(w_query, UNIT0["query"], 16)
            stream(peer_u, UNIT0["peer_u"], (BLOCKS - 1) * 8)
            sp.wait_ge(g_stored, 64 * WITH + 65)
            for n in range(2):
                sp.wait_ge(a_stored[n], 33)
            for j in range(8):
                load(peer_u[(BLOCKS - 1) * 8 + j], UNIT0["peer_u"] + (BLOCKS - 1) * 8, 0, j)
                block_piece(sp, j // 4, j // 4, j % 4)
            with sp.Fori(0, BLOCKS // 2 - 1) as i:
                for s in range(2):
                    for j in range(8):
                        load(peer_v[16 * i + 8 * s + j], UNIT0["peer_v"] + 8 * s, 8 * i, j)
                        if j < 4:
                            block_piece(sp, 2 * i + s + 2, s, j, i)
            stream(peer_v, UNIT0["peer_v"] + 112, 16, first=112)
            for e in range(0, KT, 2):
                if e < AFFINE[1]:
                    sp.wait_ge(y_normed, e + 2)
                else:
                    sp.wait_ge(y_affine, e + 2 - AFFINE[1])
                sp.dma_start(yT[:, e:e + 2, :], R[:, e:e + 2, :]).then_inc(stored, 16)
            sp.wait_ge(stored, 16 * (3 + KT // 2))

        @block.gpsimd
        def _(pool):
            def lower_half(j, h, mark):
                pool.wait_ge(hi_ready, mark)
                s = slice(h * HU, h * HU + HU)
                pool.tensor_tensor(wl[:, j, s], raw[:, j, s], wh[:, j, s].bitcast(F32),
                                   ALU.subtract).then_inc(lo_ready, 1)

            def lower(i, j):
                for h in range(2):
                    lower_half(j, h, 4 * i + 2 * j + h + 1)

            q0 = UNIT0["query"] // 2
            for n, (h, j) in enumerate(((0, 0), (0, 1), (1, 0), (1, 1))):
                lower_half(j, h, n + 1)
            with pool.Fori(1, q0) as i:
                for j in range(2):
                    lower(i, j)
            for j in range(2):
                lower(q0, j)
            norm_pool(pool, 0)
            for e in range(0, KT, 2):
                pool.wait_ge(n_full, e + 2)
                pool.tensor_tensor(bl[:, e:e + 2, :], R[:, e:e + 2, :], bh[:, e:e + 2, :].bitcast(F32),
                                   ALU.subtract).then_inc(n_lo, 1)
            with pool.Fori(q0 + 1, UNITS // 2) as i:
                for j in range(2):
                    lower(i, j)
            norm_pool(pool, 1)

        @block.scalar
        def _(act):

            def hi(phase, i, j):
                units, per = PHASES[phase]
                act.wait_ge(outs_done, OUT0[phase] + (i + j) * per + 1)
                k = (j + 1) % 2
                for h in range(2):
                    act.wait_ge(loaded[2 * k + h], 16 * (UNIT0[phase] // 2 + (j + 1) // 2 + 1) + i * 8)
                    s = slice(h * HU, h * HU + HU)
                    act.activation(wh[:, k, s], raw[:, k, s], ACT.Copy).then_inc(hi_ready, 1)

            def wait_out(phase, n):
                act.wait_ge(outs_done, OUT0[phase] + n + 2)

            def units(phase, n, first, body, step=2):
                with act.Fori(0, n // step) as i:
                    for j in range(step):
                        hi(phase, first + step * i, j)
                        body(first + step * i, j)

            for s in (h_ptc, *a_stored):
                act.sem_inc(s, 1)
            act.sem_inc(g_stored, 65)
            for n in range(4):
                act.wait_ge(x_loaded[n], 16)
                act.activation(ah[:, 4 * n:4 * n + 4, :], R[:, 4 * n:4 * n + 4, :], ACT.Copy).then_inc(x_hi, 1)
                if n in (0, 1):
                    for j in range(2):
                        act.wait_ge(loaded[2 * j + n], 16)
                        s = slice(n * HU, n * HU + HU)
                        act.activation(wh[:, j, s], raw[:, j, s], ACT.Copy).then_inc(hi_ready, 1)
            act.wait_ge(vec_in, 16)

            def ev_u(i, j):
                wait_out("u", i + j)
                bias = V("b_in")[:, bass.ds(i + j, 1)]
                act.activation(UP[:, bass.ds(i + j, 1), 16:16 + SEQ], ps[:, j:j + 1, 0:SEQ], ACT.Identity, bias=bias)
                act.activation(US[:, bass.ds(i + j, 1), :, 16:20].rearrange("p a b s -> p (a b) s"),
                               ps[:, j, SEQ:T].rearrange("p (b s) -> p b s", b=DB),
                               ACT.Identity, bias=bias).then_inc(ev_act, 1)

            hi("u", 0, 1)
            for j in range(2):
                ev_u(0, j)
            units("u", 6, 2, ev_u)
            act.wait_ge(ev_act, 8)
            act.dma_start(uT, UP[:, :, 16 + SEQ - HIST:]).then_inc(u_stored, 16)
            act.dma_start(us, US[:, :, :, 16:20]).then_inc(u_stored, 16)
            act.wait_ge(x_lo, 4)

            def ev_kv(i, j):
                wait_out("kv", i + j)
                act.activation(R[:, bass.ds(8 + i + j, 1), :], ps[:, j:j + 1, 0:T], ACT.Identity,
                               bias=V("b_in")[:, bass.ds(8 + i + j, 1)]).then_inc(ev_act, 1)

            def ev_q(i, j):
                wait_out("q", i + j)
                act.activation(R[:, bass.ds(i + j, 1), :], ps[:, j:j + 1, 0:T], ACT.Identity,
                               bias=V("b_in")[:, bass.ds(12 + i + j, 1)]).then_inc(ev_act, 1)

            def ev_gate(i, j):
                wait_out("gates", i + j)
                act.activation(GG[:, bass.ds(i + j, 1), :], ps[:, j % 2:j % 2 + 1, 0:T], ACT.Sigmoid,
                               bias=V("b_in")[:, bass.ds(20 + i + j, 1)]).then_inc(ev_act, 1)

            units("kv", 4, 0, ev_kv)
            units("q", 8, 0, ev_q)
            act.wait_ge(k_rope, 1)
            act.dma_start(kT, K2).then_inc(kv_stored, 16)
            act.dma_start(vT, V2).then_inc(kv_stored, 16)

            for j in range(SAMPLE_UNITS):
                if j == 0:
                    act.wait_ge(v_turned, 1)
                    act.wait_ge(d_split, PG)
                    act.activation(VN, TB.rearrange("p (a b) -> p a b", a=2), ACT.Copy).then_inc(v_copied, 1)
                    act.activation(VS[0:NS, :], OB[0:NS, 0:KW], ACT.Copy).then_inc(v_copied, 1)
                if j == 3:
                    act.wait_ge(sc_cache, 1)
                    act.activation(CS, ps[:, 2, :].rearrange("p (a b) -> p a b", a=4), ACT.Copy)\
                        .then_inc(sc_copied, 1)
                if j == 5:
                    act.wait_ge(s_sm, 2)
                    act.activation(SM[:, :, 0:WIN + NS], SM[:, :, 0:WIN + NS], ACT.Exp).then_inc(s_exp, 1)
                    act.activation(SX[:, 1, 0:4], SX[:, 1, 0:4], ACT.Exp).then_inc(s_exp, 1)
                if j == 6:
                    act.wait_ge(s_pt, 1)
                    act.activation(CS, TB.rearrange("p (a b) -> p a b", a=4), ACT.Copy).then_inc(s_ptc, 1)
                    act.activation(SM[0:NS, 0:2, :].rearrange("p a b -> p (a b)"),
                                   ps[0:NS, 2, :], ACT.Copy).then_inc(s_ptc, 1)
                hi("gates", 0, j)
                if j == 7:
                    act.wait_ge(s_pv, 1)
                    for odd in range(2):
                        act.activation(own_rows(bh, odd), own_cols(odd), ACT.Copy).then_inc(s_oh, 1)
                ev_gate(0, j)

            def attn_out(m, c):
                act.wait_ge(h_pv, 2 * m + c + 1)
                act.activation(o_tiles(bh, m, c), HO[c].rearrange("p (a b) -> p a b", a=2), ACT.Copy)\
                    .then_inc(h_oh, 1)

            with act.Fori(0, QG) as m:
                first = SAMPLE_UNITS + HEAD_UNITS * m
                for j in range(HEAD_UNITS):
                    if j == 1:
                        for c, n in ((0, WIN), (1, 2 * WIN)):
                            buf = SM if c == 0 else SP_
                            act.wait_ge(h_sm, 4 * m + 2 * c + 2)
                            act.activation(buf[:, :, 0:n], buf[:, :, 0:n], ACT.Exp).then_inc(h_exp, 1)
                            act.activation(SX[:, 1, 4 * c:4 * c + 4], SX[:, 1, 4 * c:4 * c + 4],
                                           ACT.Exp).then_inc(h_exp, 1)
                    if j in (3, 4, 5):
                        n = j - 3
                        act.wait_ge(h_pt, 3 * m + n + 1)
                        dst = (CS, PS[:, 0], PS[:, 1])[n]
                        act.activation(dst, TB.rearrange("p (a b) -> p a b", a=4), ACT.Copy).then_inc(h_ptc, 1)
                    hi("gates", first, j)
                    if j == 5:
                        attn_out(m, 0)
                    ev_gate(first, j)
                attn_out(m, 1)

            act.dma_start(k_shift, k_nat[:, DS:, :]).then_inc(stored, 16)
            act.dma_start(v_shift, vc[DS:, :, :]).then_inc(stored, 16)
            act.dma_start(st_shift, st_nat[:, DS:, :]).then_inc(stored, 16)
            for j in range(2):
                hi("pool", 0, j)
            units("attn", 8, 0, lambda i, j: None)
            units("out", 16, 0, lambda i, j: None)

            hi("query", 0, 0)
            norm_act(act, 0)
            for e in range(KT):
                act.wait_ge(n_aff, e + 1)
                g, b = V("g1")[:, e:e + 1], V("b1")[:, e:e + 1]
                act.activation(bh[:, e, :], R[:, e, :], ACT.Identity, scale=g, bias=b).then_inc(n_hi, 1)

            def ev_query(i, j):
                wait_out("query", i + j)
                act.activation(QT[:, j, :], ps[:, j, 0:T], ACT.Copy).then_inc(ev_act, 1)

            ev_query(0, 0)
            hi("query", 0, 1)
            ev_query(0, 1)
            units("query", 14, 2, ev_query)

            def ev_peer(i, j):
                wait_out("peer_u", 8 * i + j)
                if j % 4 == 0:
                    act.wait_ge(a_stored[j // 4], 16 * i + 1)
                act.activation(ST[:, j // 4, j % 4, :], ps[:, j % 2, 0:T], ACT.Gelu).then_inc(ev_act, 1)

            def store_half(i, half):
                act.wait_ge(ev_act, ACT_EV0["peer_u"] + 8 * i + 4 * half + 4)
                act.dma_start(a_dram[2 * i + half], ST[:, half, :, :].rearrange("p e t -> p (e t)"))\
                    .then_inc(a_stored[half], 16)

            def store_gates(w, n):
                if n == 0:
                    act.wait_ge(g_ev, 8 * w + 9)
                    act.wait_ge(g_stored, 64 * w + 65)
                act.dma_start(g_dram[4 * n:4 * n + 4, :, bass.ds(w, 1), :].rearrange("b p w n -> p b (w n)"),
                              gs[:, bass.ds(w % 2, 1), 32 * n:32 * n + 32, :].rearrange(
                                  "p a (b e) t -> p b (a e t)", b=4)).then_inc(g_stored, 16)

            def peer_block(i, w=None):
                for j in range(8):
                    hi("peer_u", 8 * i, j)
                    if w is not None and j < 4:
                        store_gates(w, j)
                    if j == 4:
                        store_half(i, 0)
                    ev_peer(i, j)
                store_half(i, 1)

            act.wait_ge(sc_ev, NHALF + 2)
            with act.Fori(0, BEFORE - 1) as i:
                peer_block(i)
            act.wait_ge(r_exp_in, 1)
            act.activation(CV, CV, ACT.Exp).then_inc(r_exp, 1)
            with act.Fori(BEFORE - 1, BEFORE + 1) as i:
                peer_block(i)
            with act.Fori(1, WITH) as i:
                peer_block(BEFORE + i, i - 1)
            peer_block(BEFORE + WITH, WITH - 1)
            with act.Fori(BEFORE + WITH + 1, BLOCKS) as i:
                peer_block(i)
            with act.Fori(0, 63) as i:
                for j in range(2):
                    hi("peer_v", 2 * i, j)
            hi("peer_v", 126, 0)
            norm_act(act, 1)
            for e in range(AFFINE[1]):
                act.wait_ge(n_aff, KT + e + 1)
                act.activation(R[:, e, :], R[:, e, :], ACT.Identity, scale=V("g2")[:, e:e + 1],
                               bias=V("b2")[:, e:e + 1]).then_inc(y_normed, 1)

        @block.vector
        def _(ve):
            own = Tally(dve)

            def link(instruction):
                ve.wait_ge(dve, own.inc(instruction))

            for s in (h_prob, h_ol, g_ev):
                ve.sem_inc(s, 1)
            ve.memset(tiny[:, :], 0.0)
            ve.memset(ones[:, :], 1.0 / D).then_inc(ones_set, 1)
            ve.wait_ge(ones_set, 1)
            for n in range(4):
                ve.wait_ge(x_hi, n + 1)
                s = slice(4 * n, 4 * n + 4)
                ve.tensor_tensor(al[:, s, :], R[:, s, :], ah[:, s, :].bitcast(F32), ALU.subtract).then_inc(x_lo, 1)

            ve.wait_ge(ev_act, 8)
            ve.wait_ge(consts_in, 16)
            ve.wait_ge(state_in, 32)
            ratio = C("ratio").rearrange("p (g s) -> p g s", g=PG)
            for g in range(PG):
                t = slice(2 * g, 2 * g + 2)
                src = (UP[:, t], US[:, t])
                for level in range(g + 1):
                    step = 1 << level
                    lo = 2 * step
                    dst = PT[level % 2]
                    ve.tensor_tensor(dst[0][:, :, lo:], src[0][:, :, lo:], src[0][:, :, lo - step:-step], ALU.add)
                    link(ve.tensor_tensor(dst[1][:, :, :, lo:], src[1][:, :, :, lo:],
                                          src[1][:, :, :, lo - step:-step], ALU.add))
                    src = dst
                link(ve.tensor_tensor(src[0][:, :, 16:32], src[0][:, :, 16:32], bc(ratio[:, g, :], 1, 2), ALU.mult))
                w = 1.0 / (2 << g)
                ve.scalar_tensor_tensor(out=PD[:, :, 0:SEQ], in0=src[0][:, :, 16:], scalar=w,
                                        in1=UP[:, t, 16:], op0=ALU.mult, op1=ALU.subtract)
                for k in range(2):
                    last = ve.scalar_tensor_tensor(
                        out=PD[:, k, SEQ:T].rearrange("p (b s) -> p b s", b=DB), in0=src[1][:, k, :, 16:],
                        scalar=w, in1=US[:, 2 * g + k, :, 16:], op0=ALU.mult, op1=ALU.subtract)
                link(last)
                link(ve.tensor_copy(bh[:, t, :], PD))
                ve.tensor_tensor(bl[:, t, :], PD, bh[:, t, :].bitcast(F32), ALU.subtract).then_inc(d_split, 1)
                ve.wait_ge(d_split, g + 1)

            def rope(a, b, t0, t1, n, done):
                cos, sin = bc(C("cos"), 1, n), bc(C("sin"), 1, n)
                ve.tensor_tensor(t0, b, sin, ALU.mult)
                link(ve.tensor_tensor(t1, a, sin, ALU.mult))
                ve.tensor_tensor(a, a, cos, ALU.mult)
                link(ve.tensor_tensor(b, b, cos, ALU.mult))
                ve.tensor_tensor(a, a, t0, ALU.subtract)
                last = ve.tensor_tensor(b, b, t1, ALU.add)
                last.then_inc(done, 1)

            ve.wait_ge(ev_act, 12)
            rope(K2[:, 0:1], K2[:, 1:2], RT[0][:, 0:1], RT[1][:, 0:1], 1, k_rope)
            ve.wait_ge(ev_act, 20)
            ve.wait_ge(k_rope, 1)
            qp = QK.rearrange("p (m h) t -> p h m t", h=2)
            rope(qp[:, 0], qp[:, 1], RT[0], RT[1], 4, q_rope)

            def softmax(buf, n, sink, x, shifted):
                link(ve.tensor_reduce(SX[:, 0, x], buf[:, :, 0:n], AX_X, ALU.max))
                link(ve.tensor_tensor(SX[:, 0, x], SX[:, 0, x], sink, ALU.max))
                ve.tensor_tensor(SX[:, 1, x], sink, SX[:, 0, x], ALU.subtract).then_inc(shifted, 1)
                ve.tensor_tensor(buf[:, :, 0:n], buf[:, :, 0:n], bc(SX[:, 0, x], 2, n), ALU.subtract)\
                    .then_inc(shifted, 1)

            def divide(buf, n, x, exped, value, done):
                ve.wait_ge(exped, value)
                link(ve.tensor_reduce(SX[:, 2, x], buf[:, :, 0:n], AX_X, ALU.add))
                link(ve.tensor_tensor(SX[:, 2, x], SX[:, 2, x], SX[:, 1, x], ALU.add))
                link(ve.reciprocal(SX[:, 3, x], SX[:, 2, x]))
                ve.tensor_tensor(buf[:, :, 0:n], buf[:, :, 0:n], bc(SX[:, 3, x], 2, n), ALU.mult)\
                    .then_inc(done, 1)

            ve.wait_ge(q_rope, 1)
            link(ve.memset(QD, 0.0))
            for g in range(KVH):
                r = slice(32 * g, 32 * g + 32)
                for half in range(2):
                    ve.tensor_copy(QD[r, half, :, 16 * g:16 * g + 16].rearrange("p b (m i) -> p m b i", m=QG),
                                   qp[r, half, :, SEQ:T].rearrange("p m (b i) -> p m b i", b=DB))
            for half in range(2):
                last = ve.tensor_copy(QW[:, half], qp[:, half, :, SEQ:T])
            last.then_inc(q_side, 1)

            def join_halves(dst, src):
                for g in range(KVH):
                    for half in range(2):
                        to = 64 * (g % 2) + 32 * half
                        last = ve.tensor_copy(dst[to:to + 32, g // 2:g // 2 + 1, :],
                                              src(slice(32 * g, 32 * g + 32), half))
                return last

            ve.wait_ge(v_turned, 1)
            ve.wait_ge(kv_stored, 32)
            join_halves(KK, lambda r, half: K2[r, half:half + 1, :])

            ve.wait_ge(sc_turned, 1)
            mask = C("smask")
            ve.scalar_tensor_tensor(out=SM[:, :, 0:WIN], in0=TB.rearrange("p (a b) -> p a b", a=4), scalar=SCALE,
                                    in1=bc(mask[:, 0:WIN], 1, 4), op0=ALU.mult, op1=ALU.add)
            link(ve.scalar_tensor_tensor(out=SM[:, :, WIN:WIN + NS], in0=SB4[:, :, 256:256 + NS], scalar=SCALE,
                                         in1=bc(mask[:, WIN:], 1, 4), op0=ALU.mult, op1=ALU.add))
            softmax(SM, WIN + NS, V("ssink"), slice(0, 4), s_sm)
            divide(SM, WIN + NS, slice(0, 4), s_exp, 2, s_prob)
            ve.wait_ge(s_oh, 2)
            for odd in range(2):
                ve.tensor_tensor(own_rows(bl, odd), own_cols(odd), own_rows(bh, odd).bitcast(F32), ALU.subtract)\
                    .then_inc(s_ol, 1)

            join_halves(QS, lambda r, half: R[r, half:half + 1, :]).then_inc(h_q, 1)
            with ve.Fori(0, QG) as m:
                own.start(m, 2 * 6)
                sink = V("sink")[:, bass.ds(4 * m, 4)]
                for c, n in ((0, WIN), (1, 2 * WIN)):
                    buf = SM if c == 0 else SP_
                    x = slice(4 * c, 4 * c + 4)
                    ve.wait_ge(h_scores, 2 * m + 3)
                    link(ve.scalar_tensor_tensor(
                        out=buf[:, :, 0:n], in0=SB4[:, :, 0:WIN] if c == 0 else SB4[:, :, WIN:3 * WIN],
                        scalar=SCALE, in1=bc(C("mask")[:, 2 * WIN - n:], 1, 4), op0=ALU.mult, op1=ALU.add))
                    softmax(buf, n, sink, x, h_sm)
                join_halves(QS, lambda r, half: R[r, bass.ds(2 * m + 2 + half, 1), :]).then_inc(h_q, 1)
                for c, n in ((0, WIN), (1, 2 * WIN)):
                    divide(SM if c == 0 else SP_, n, slice(4 * c, 4 * c + 4), h_exp, 4 * m + 2 * c + 2, h_prob)
                for c in range(2):
                    ve.wait_ge(h_oh, 2 * m + c + 1)
                    ve.tensor_tensor(o_tiles(bl, m, c), HO[c].rearrange("p (a b) -> p a b", a=2),
                                     o_tiles(bh, m, c).bitcast(F32), ALU.subtract).then_inc(h_ol, 1)
                own.stop(QG)

            for o in range(16):
                ve.wait_ge(outs_done, OUT0["pool"] + o + 2)
                ve.scalar_tensor_tensor(out=GG[:, o, :], in0=ps[:, o % 2, 0:T], scalar=V("scale")[:, o:o + 1],
                                        in1=GG[:, o, :], op0=ALU.mult, op1=ALU.mult).then_inc(ev_dve, 1)
            ve.wait_ge(ev_dve, 16)
            with ve.Fori(0, 8) as i:
                own.start(i, 2 * 2)
                for j in range(2):
                    o = 2 * i + j
                    ve.wait_ge(outs_done, OUT0["attn"] + o + 2)
                    ve.tensor_tensor(GG[:, bass.ds(16 + o, 1), :], ps[:, j:j + 1, 0:T],
                                     GG[:, bass.ds(16 + o, 1), :], ALU.mult).then_inc(ev_dve, 1)
                    ve.wait_ge(ev_dve, DVE_EV0["attn"] + o + 1)
                    link(ve.tensor_tensor(GG[:, bass.ds(o, 1), :], GG[:, bass.ds(16 + o, 1), :],
                                          GG[:, bass.ds(o, 1), :], ALU.add))
                    link(ve.tensor_copy(ah[:, bass.ds(o, 1), :], GG[:, bass.ds(o, 1), :]))
                    ve.tensor_tensor(al[:, bass.ds(o, 1), :], GG[:, bass.ds(o, 1), :],
                                     ah[:, bass.ds(o, 1), :].bitcast(F32), ALU.subtract).then_inc(m_split, 1)
                own.stop(8)

            ve.wait_ge(x_again, 16)

            def take_out(i, j):
                o = 2 * i + j
                r = R[:, bass.ds(o, 1), :] if not isinstance(i, int) else R[:, o:o + 1, :]
                ve.wait_ge(outs_done, OUT0["out"] + o + 2)
                ve.scalar_tensor_tensor(out=r, in0=r, scalar=ALPHA, in1=ps[:, j:j + 1, 0:T],
                                        op0=ALU.mult, op1=ALU.add).then_inc(ev_dve, 1)

            ve.wait_ge(m_split, KT)
            norm_first(ve, own, link, 0, DVE_EV0["out"], take_out)
            norm_last(ve, link, 0)
            ve.wait_ge(n_lo, KT // 2)
            ve.tensor_scalar(R[:, :, :], R[:, :, :], ALPHA, None, ALU.mult).then_inc(y_init, 1)
            ve.sem_inc(sc_ev, 1)
            ve.memset(SC[:, 2], 0.0).then_inc(sc_ev, 1)
            ve.wait_ge(sc_ev, 2)
            with ve.Fori(0, NHALF // 2) as i:
                for j in range(2):
                    ve.wait_ge(r_pe, 2 * i + j + 1)
                    ve.tensor_copy(SC[:, 0:2, bass.ds(2 * i + j, 1), :].rearrange("p c a n -> p c (a n)"),
                                   ps[:, 2 + j, 0:256].rearrange("p (c n) -> p c n", c=2))
                    ve.tensor_copy(SC[0:NS, 2, bass.ds(2 * i + j, 1), :], ps[0:NS, 2 + j, 256:384].unsqueeze(1))\
                        .then_inc(sc_ev, 1)
            ve.wait_ge(sc_ev, NHALF + 2)

            def hold(mark):
                ve.wait_ge(dve, mark)
                ve.tensor_copy(tiny[:, 1:2], tiny[:, 0:1])

            def top16(scores, best, index):
                def stage(make):
                    for c in range(CH):
                        mark = own.inc(make(c))
                    return mark

                hold(stage(lambda c: ve.max(best[c][:, 0:8], scores[c])))
                hold(stage(lambda c: ve.max_index(index[c][:, 0:8], best[c][:, 0:8], scores[c])))
                hold(stage(lambda c: ve.match_replace(scores[c], best[c][:, 0:8], scores[c], -3.0e38)))
                hold(stage(lambda c: ve.max(best[c][:, 8:16], scores[c])))
                ve.wait_ge(dve, stage(lambda c: ve.max_index(index[c][:, 8:16], best[c][:, 8:16], scores[c])))

            with ve.Fori(0, NHALF) as i:
                own.start(i, 1 + 15)
                hold(own.inc(ve.tensor_copy(LS[:, :, 0:P],
                                            SC[:, :, bass.ds(i, 1), :].rearrange("p c a n -> p c (a n)"))))
                top16([LS[:, c, 0:P] for c in range(CH)], [LV[:, c, :] for c in range(CH)],
                      [LI[:, c, :].bitcast(U32) for c in range(CH)])
                ve.tensor_copy(TV[:, :, bass.ds(i, 1), :].rearrange("p c a n -> p c (a n)"), LV)
                ve.tensor_copy(TI[:, :, bass.ds(i, 1), :].rearrange("p c a n -> p c (a n)"),
                               LI.bitcast(U32)).then_inc(r_idx, 1)
                ve.wait_ge(r_idx, i + 1)
                own.stop(NHALF)
            with ve.Fori(0, PH) as h:
                own.start(h, CH + 15)
                for c in range(CH):
                    a = TV[:, c, bass.ds(2 * h, 1), :].rearrange("p a n -> p (a n)")
                    b = TV[:, c, bass.ds(2 * h + 1, 1), :].rearrange("p a n -> p (a n)")
                    mark = own.inc(ve.tensor_tensor(LS[:, c, :].rearrange("p (a b) -> p a b", a=16),
                                                    bc(a, 2, 16), bc(b, 1, 16), ALU.add))
                hold(mark)
                top16([LS[:, c, :] for c in range(CH)], [LV[:, c, :] for c in range(CH)],
                      [LI[:, c, :].bitcast(U32) for c in range(CH)])
                ve.tensor_copy(CV[:, :, bass.ds(h, 1), :].rearrange("p c a n -> p c (a n)"), LV)
                ve.tensor_copy(CI[:, :, bass.ds(h, 1), :].rearrange("p c a n -> p c (a n)").bitcast(U32),
                               LI.bitcast(U32)).then_inc(r_idx, 1)
                ve.wait_ge(r_idx, NHALF + h + 1)
                own.stop(PH)

            link(ve.tensor_copy(CS1, CV[:, :, :, 0:1]))
            flat = lambda t: t.rearrange("p c h k -> p (c h) k")
            ve.tensor_tensor(flat(CV), flat(CV), flat(CS1).broadcast_to([P, CH * PH, TOPK]), ALU.subtract)\
                .then_inc(r_exp_in, 1)
            cu = CI.bitcast(U32)
            ve.tensor_scalar(I1.bitcast(U32), cu, 4, None, ALU.logical_shift_right)
            link(ve.tensor_scalar(I2.bitcast(U32), cu, 15, None, ALU.bitwise_and))
            ve.tensor_copy(X1, I1.bitcast(U32))
            link(ve.tensor_copy(X2, I2.bitcast(U32)))
            iota16 = C("iota")[:, 0:16]
            for c in range(CH):
                for half, (x, out) in enumerate(((X1, I1), (X2, I2))):
                    e4 = E4.rearrange("p (h k) j -> p h k j", h=PH)
                    ks = bc(bc(iota16, 1, PH), 2, TOPK)
                    link(ve.tensor_tensor(e4, bc(x[:, c], 3, 16), ks, ALU.is_equal))
                    names = TI[:, c].rearrange("p (h s) j -> p s h j", s=2)[:, half]
                    link(ve.tensor_tensor(e4, e4, bc(names, 2, TOPK), ALU.mult))
                    link(ve.tensor_reduce(out[:, c].rearrange("p h k -> p (h k)"), E4, AX_X, ALU.add))
            ve.wait_ge(r_exp, 1)
            link(ve.tensor_reduce(flat(CS1).rearrange("p a b -> p (a b)"), flat(CV), AX_X, ALU.add))
            link(ve.reciprocal(CS1, CS1))
            ve.tensor_tensor(flat(GA), flat(CV), flat(CS1).broadcast_to([P, CH * PH, TOPK]), ALU.mult)\
                .then_inc(r_idx, 1)
            for n, dst in enumerate((I1T, I2T, gT[:, :])):
                ve.wait_ge(r_pe, NHALF + n + 1)
                link(ve.tensor_copy(dst, ps[:, 4 + n, 0:T]))
            link(ve.tensor_copy(gh[:, :], gT[:, :]))
            link(ve.tensor_tensor(gl[:, :], gT[:, :], gh[:, :].bitcast(F32), ALU.subtract))
            iota = C("iota")

            with ve.Fori(0, WITH) as i:
                own.start(i, 8)
                for j in range(8):
                    n = 8 * i + j
                    ve.wait_ge(r_pe, NHALF + 3 + n - 1)
                    for t in range(TOKS):
                        tok = bass.ds(TG * i + TOKS * j + t, 1)
                        ve.tensor_scalar(OH[:, j % 2, 0, t, :], iota, I2T[:, tok], None, ALU.is_equal)
                        for half, g in enumerate((gh, gl)):
                            last = ve.tensor_scalar(OH[:, j % 2, 1 + half, t, :], iota, I1T[:, tok],
                                                    g[:, tok].bitcast(F32), ALU.is_equal, ALU.mult)
                    last.then_inc(oh_ready, 1)
                    ve.wait_ge(r_pe, NHALF + 3 + n + 1)
                    if j == 0:
                        ve.wait_ge(g_stored, 64 * i + 1)
                    both = ps[:, 2 + 2 * (j % 2):4 + 2 * (j % 2), :].rearrange("p b (t s e) -> p (b t) s e", t=2, s=2)
                    link(ve.tensor_copy(GS, both[:, :, 1, :]))
                    ve.tensor_tensor(gs[:, bass.ds(i % 2, 1), :, TOKS * j:TOKS * j + TOKS].rearrange(
                                         "p a e t -> p t (a e)"), both[:, :, 0, :], GS, ALU.add).then_inc(g_ev, 1)
                own.stop(WITH)

            def gate(s, e):
                a = AB[:, s, e, :].rearrange("p (w t) -> p w t", w=WITH)
                g = GB[:, s].rearrange("p w (e t) -> p w e t", e=8)[:, :, e, :]
                link(ve.tensor_tensor(a, a, g, ALU.mult))
                link(ve.tensor_copy(ah[:, 8 * s + e, :], AB[:, s, e, :]))
                ve.tensor_tensor(al[:, 8 * s + e, :], AB[:, s, e, :], ah[:, 8 * s + e, :].bitcast(F32),
                                 ALU.subtract).then_inc(act_ready, 1)

            def take(o, j, i):
                ve.wait_ge(outs_done, OUT0["peer_v"] + i + o + 2)
                ve.tensor_tensor(R[:, j, :], R[:, j, :], ps[:, o % 2, 0:T], ALU.add).then_inc(ev_dve, 1)

            ve.wait_ge(g_ev, 8 * WITH + 1)
            ve.wait_ge(blk_in[0], 64)
            for e in range(8):
                gate(0, e)
            ve.wait_ge(y_init, 1)

            def v_block(i, s):
                ve.wait_ge(blk_in[1 - s], 64 * (i + s + 1))
                ve.wait_ge(outs_done, OUT0["peer_v"] + 32 * i + 16 * s + 1)
                for u in range(8):
                    gate(1 - s, u)
                    for j in range(2):
                        take(16 * s + 2 * u + j, 2 * u + j, 32 * i)

            with ve.Fori(0, BLOCKS // 2 - 1) as i:
                own.start(i, 32)
                for s in range(2):
                    v_block(i, s)
                own.stop(BLOCKS // 2 - 1)
            v_block(BLOCKS // 2 - 1, 0)

            def take_last(i, j):
                o = 2 * i + j
                r = R[:, bass.ds(o, 1), :] if not isinstance(i, int) else R[:, o:o + 1, :]
                ve.wait_ge(outs_done, OUT0["peer_v"] + 16 * (BLOCKS - 1) + o + 2)
                ve.tensor_tensor(r, r, ps[:, j:j + 1, 0:T], ALU.add).then_inc(ev_dve, 1)

            ve.wait_ge(act_ready, 8 * BLOCKS)
            norm_first(ve, own, link, 1, DVE_EV0["peer_v"] + 16 * (BLOCKS - 1), take_last)
            norm_last(ve, link, 1)

        @block.tensor
        def _(pe):
            def product(bank, slot, tiles, mh, ml, u, m_wait=None):
                out = ps[:, bank, 0:T]
                for n, (t, k) in enumerate(tiles):
                    w = wh[:, slot, t * P:t * P + P]
                    if t % 8 == 0:
                        pe.wait_ge(hi_ready, 2 * u + t // 8 + 1)
                    if m_wait and n % m_wait[1] == 0:
                        pe.wait_ge(m_wait[0], n // m_wait[1] + 1)
                    pe.matmul(out, w, mh(k), start=(n == 0), stop=False)
                    pe.matmul(out, w, ml(k), start=False, stop=False)
                for n, (t, k) in enumerate(tiles):
                    if t % 8 == 0:
                        pe.wait_ge(lo_ready, 2 * u + t // 8 + 1)
                    last = pe.matmul(out, wl[:, slot, t * P:t * P + P], mh(k), start=False,
                                     stop=(n == len(tiles) - 1))
                last.then_inc(outs_done, 1)

            def a_op(t):
                return lambda k: t[:, k, :]

            FULL = [(k, k) for k in range(KT)]

            def unit(phase, evicted, ev0, i, j, mh, ml, m_wait=None):
                pe.wait_ge(evicted, ev0 + i + j - 1)
                product(j % 2, j % 2, FULL, mh, ml, UNIT0[phase] + i + j, m_wait)

            def units(phase, n, first, evicted, ev0, t, step=2):
                with pe.Fori(0, n // step) as i:
                    for j in range(step):
                        unit(phase, evicted, ev0, first + step * i, j, a_op(t[0]), a_op(t[1]))

            for s in (h_scores, outs_done):
                pe.sem_inc(s, 1)
            x = (ah, al)

            def together(u0, mh, ml, come, groups):
                passes = ((wh, mh), (wh, ml), (wl, mh))

                def step(j, k, n):
                    w, m = passes[n]
                    if n < 2 and k % come[n][1] == 0:
                        pe.wait_ge(come[n][0], k // come[n][1] + 1)
                    if n != 1 and k % 8 == 0:
                        mark = 2 * (k // 8) + j if u0 == 0 else 2 * (u0 + j) + k // 8
                        pe.wait_ge(hi_ready if n == 0 else lo_ready, mark + 1)
                    last = pe.matmul(ps[:, j, 0:T], w[:, j, k * P:k * P + P], m[:, k, :],
                                     start=(k == 0 and n == 0), stop=(k == KT - 1 and n == 2))
                    if k == KT - 1 and n == 2:
                        last.then_inc(outs_done, 1)

                k0 = 0
                for group in groups:
                    ks = range(k0, k0 + group)
                    k0 += group
                    if k0 < KT:
                        order = [(j, k, n) for n in range(3) for k in ks for j in range(2)]
                    else:
                        order = [(j, k, 0) for j in range(2) for k in ks]
                        order += [(j, k, n) for j in range(2) for n in (1, 2) for k in ks]
                    for j, k, n in order:
                        step(j, k, n)

            together(0, ah, al, ((x_hi, 4), (x_lo, 4)), (8, 8))
            units("u", 6, 2, ev_act, 0, x)
            units("kv", 4, 0, ev_act, ACT_EV0["kv"], x)
            units("q", 8, 0, ev_act, ACT_EV0["q"], x)

            def gate_unit(first, j):
                unit("gates", ev_act, ACT_EV0["gates"], first, j, a_op(ah), a_op(al))

            pe.wait_ge(ev_act, 12)
            pe.wait_ge(consts_in, 16)
            for c in range(2):
                for v in range(2):
                    pe.transpose(TB[:, (2 * c + v) * P:(2 * c + v + 1) * P], V2[:, v, c * P:c * P + P], ident)
            for v in range(2):
                last = pe.transpose(OB[0:NS, v * P:v * P + P], V2[:, v, SEQ:T], ident)
            last.then_inc(v_turned, 1)
            for j in range(SAMPLE_UNITS):
                if j == 3:
                    pe.wait_ge(q_side, 1)
                    pe.wait_ge(caches_in, 32)
                    for b in range(DB):
                        out = ps[:, 2, :].rearrange("p (n b i) -> p n b i", n=HEADS, b=DB)[:, :, b, :]
                        for half in range(2):
                            last = pe.matmul(out, KC[:, half, b, :], QD[:, half, b, :],
                                             start=(half == 0), stop=(half == 1))
                    last.then_inc(sc_cache, 1)
                if j == 4:
                    pe.wait_ge(sc_copied, 1)
                    pe.wait_ge(v_copied, 2)
                    for g in range(KVH):
                        pe.transpose(TB[:, g * P:g * P + P], CS[:, g, :], ident)
                    for half in range(2):
                        for g in range(KVH):
                            r = slice(32 * g, 32 * g + 32)
                            last = pe.matmul(SB4[:, g, 256:256 + NS], QW[r, half].rearrange("p m t -> p (m t)"),
                                             K2[r, half, SEQ:T], start=(half == 0), stop=(half == 1))
                    last.then_inc(sc_turned, 1)
                if j == 6:
                    pe.wait_ge(s_prob, 1)
                    for g in range(KVH):
                        pe.transpose(TB[:, g * P:g * P + P], SM[:, g, 0:WIN], ident)
                    for g in range(KVH):
                        last = pe.transpose(ps[0:NS, 2, g * P:g * P + P], SM[:, g, WIN:WIN + NS], ident)
                    last.then_inc(s_pt, 1)
                if j == 7:
                    pe.wait_ge(s_ptc, 2)
                    pn = SM[0:NS, 0:2, :].rearrange("p a (b c) -> p (a b) c", b=2)
                    for two in range(2):
                        vs = slice(P * two, P * two + P)
                        out = OB[:, 2 * P * two:2 * P * two + 2 * P]
                        pe.matmul(out.rearrange("p (g n) -> p g n", g=2), VS[0:NS, vs], pn[:, 2 * two:2 * two + 2, :],
                                  start=True, stop=False)
                        for b in range(DB):
                            cols, pc = (a.rearrange("p (n b i) -> p n b i", n=8, b=DB)[:, :, b, :] for a in (
                                out, CS[:, 2 * two:2 * two + 2, :].rearrange("p g n -> p (g n)")))
                            last = pe.matmul(cols, VC[:, b, vs], pc, start=False, stop=(b == DB - 1))
                    last.then_inc(s_pv, 1)
                gate_unit(0, j)

            pe.wait_ge(s_ol, 2)
            with pe.Fori(0, QG) as m:
                first = SAMPLE_UNITS + HEAD_UNITS * m
                for j in range(HEAD_UNITS):
                    if j == 0:
                        pe.wait_ge(h_q, m + 1)
                        pe.wait_ge(h_prob, 2 * m + 1)
                        for c in range(2):
                            for g in range(KVH):
                                r = slice(64 * (g % 2), 64 * (g % 2) + 64)
                                out = SB4[:, g, 0:WIN] if c == 0 else SB4[:, g, WIN:3 * WIN]
                                last = pe.matmul(out, QS[r, g // 2, c * P:c * P + P],
                                                 KK[r, g // 2, 0:WIN * (c + 1)], start=True, stop=True)
                            last.then_inc(h_scores, 1)
                    if j in (3, 4, 5):
                        n = j - 3
                        c, kb = ((0, 0), (1, 0), (1, 1))[n]
                        pe.wait_ge(h_prob, 2 * m + c + 2)
                        pe.wait_ge(h_ptc, 3 * m + n + 1)
                        src = SM if c == 0 else SP_
                        for g in range(KVH):
                            last = pe.transpose(TB[:, g * P:g * P + P], src[:, g, kb * P:kb * P + P], ident)
                        last.then_inc(h_pt, 1)
                    if j == 5:
                        pe.wait_ge(h_ol, 2 * m + 1)
                        pe.wait_ge(h_ptc, 3 * m + 2)
                        last = values(pe, 0, [CS])
                        last.then_inc(h_pv, 1)
                    gate_unit(first, j)
                pe.wait_ge(h_ol, 2 * m + 2)
                pe.wait_ge(h_ptc, 3 * m + 4)
                pe.wait_ge(h_prob, 2 * m + 3)
                last = values(pe, 1, [PS[:, 0], PS[:, 1]])
                last.then_inc(h_pv, 1)

            pe.wait_ge(ev_act, ACT_EV0["gates"] + 32)
            for u in range(2):
                for o in range(8):
                    n = 8 * u + o
                    if n >= 2:
                        pe.wait_ge(ev_dve, n - 1)
                    g = n // 4
                    product(n % 2, u, [(2 * o, 2 * g), (2 * o + 1, 2 * g + 1)], a_op(bh), a_op(bl),
                            UNIT0["pool"] + u)

            def pairs(phase, i, j, mh, ml):
                for o in range(2):
                    pe.wait_ge(ev_dve, DVE_EV0[phase] + 2 * i + 2 * j + o - 1)
                    product(o, j % 2, [(8 * o + k, k) for k in range(8)], mh, ml, UNIT0[phase] + i + j)

            pe.wait_ge(h_ol, 2 * QG + 1)
            with pe.Fori(0, 4) as i:
                for j in range(2):
                    pairs("attn", 2 * i, j, lambda k: bh[:, 8 + k, :], lambda k: bl[:, 8 + k, :])

            def out_unit(i, j, m_wait=None):
                unit("out", ev_dve, DVE_EV0["out"], i, j, a_op(ah), a_op(al), m_wait=m_wait)

            out_unit(0, 0, m_wait=(m_split, 1))
            out_unit(0, 1)
            for j in range(2):
                out_unit(2, j)
            norm_c(pe, 0)
            with pe.Fori(2, 8) as i:
                for j in range(2):
                    out_unit(2 * i, j)
            norm_sums(pe, 0)

            def q_unit(i, j):
                unit("query", ev_act, ACT_EV0["query"], i, j, a_op(bh), a_op(bl))

            def key_scores(l, j):
                pe.wait_ge(ev_act, ACT_EV0["query"] + l + 1)
                pe.wait_ge(sc_ev, l + 1)
                rhs = SK[:, bass.ds(l, 1), :] if not isinstance(l, int) else SK[:, l:l + 1, :]
                for c, n in ((0, P), (1, P), (2, NS)):
                    last = pe.matmul(ps[0:n, 2 + j:3 + j, c * P:c * P + P], QT[:, j, c * P:c * P + n], rhs,
                                     start=True, stop=True)
                last.then_inc(r_pe, 1)

            for j in range(2):
                pe.wait_ge(ev_act, ACT_EV0["query"] + j - 1)
            together(UNIT0["query"], bh, bl, ((n_hi, 1), (n_lo, 2)), (4, 4, 4, 4))
            pe.wait_ge(keys_in, 16)
            key_scores(0, 0)
            q_unit(2, 0)
            key_scores(1, 1)
            with pe.Fori(1, 7) as i:
                q_unit(2 * i, 1)
                key_scores(2 * i, 0)
                q_unit(2 * i + 2, 0)
                key_scores(2 * i + 1, 1)
            q_unit(14, 1)
            key_scores(14, 0)
            key_scores(15, 1)

            def u_unit(i, j):
                unit("peer_u", ev_act, ACT_EV0["peer_u"], i, j, a_op(bh), a_op(bl))

            with pe.Fori(0, BEFORE - 1) as i:
                for j in range(8):
                    u_unit(8 * i, j)
            for j in range(8):
                if j == 7:
                    pe.wait_ge(r_idx, NHALF + PH + 1)
                    for src, dst in ((I1, ps[:, 4, :]), (I2, ps[:, 5, :]), (GA, ps[:, 6, :])):
                        for c, n in ((0, P), (1, P), (2, NS)):
                            last = pe.transpose(dst[:, c * P:c * P + n],
                                                src[0:n, c].rearrange("p h k -> p (h k)"), ident[0:n, 0:n])
                        last.then_inc(r_pe, 1)
                u_unit(8 * (BEFORE - 1), j)
            with pe.Fori(0, WITH) as i:
                for j in range(8):
                    n = 8 * i + j
                    pe.wait_ge(oh_ready, n + 1)
                    if j >= 2:
                        pe.wait_ge(g_ev, n)
                    else:
                        pe.wait_ge(g_ev, 8 * i + 1)
                    for t in range(TOKS):
                        last = pe.matmul(gate_bank(j, t), OH[:, j % 2, 0, t, :], OH[:, j % 2, 1:3, t, :],
                                         start=True, stop=True)
                    last.then_inc(r_pe, 1)
                    u_unit(8 * (BEFORE + i), j)
            with pe.Fori(BEFORE + WITH, BLOCKS) as i:
                for j in range(8):
                    u_unit(8 * i, j)

            pe.wait_ge(ev_act, ACT_EV0["peer_u"] + 128)
            pe.wait_ge(act_ready, 8)

            def v_unit(i, s, j):
                pairs("peer_v", 16 * i + 8 * s, j,
                      lambda k: ah[:, 8 * s + k, :], lambda k: al[:, 8 * s + k, :])

            with pe.Fori(0, BLOCKS // 2 - 1) as i:
                for s in range(2):
                    pe.wait_ge(act_ready, 16 * i + 8 * s + 8)
                    for j in range(8):
                        v_unit(i, s, j)
            pe.wait_ge(act_ready, 8 * BLOCKS - 8)
            with pe.Fori(0, 4) as n:
                for j in range(2):
                    pairs("peer_v", 112 + 2 * n, j, a_op(ah), a_op(al))
            pe.wait_ge(act_ready, 8 * BLOCKS)
            for j in range(8):
                v_unit(BLOCKS // 2 - 1, 1, j)
                if j == 1:
                    norm_c(pe, 1)
            norm_sums(pe, 1)


def _axes(a, shape, order):
    return np.ascontiguousarray(a.reshape(shape).transpose(order))


def kernel(x_prompt, x_sample, cache_k, cache_v, state_pool, w_in, b_in, attn_sinks, w_attn_br,
           w_pool, pool_scale, w_out, ln1_g, ln1_b, w_query, sub_keys, peer_u, peer_v, ln2_g, ln2_b):
    import concourse.bacc as bacc
    from concourse.bass_utils import run_bass_kernel_spmd

    r = np.arange(32)
    halves = [np.concatenate([h * HD + 32 * s + r for h in hs])
              for hs in [[QG * g + m for g in range(KVH)] for m in range(QG)] for s in range(2)]
    keys = [AW + np.concatenate([g * HD + 32 * s + r for g in range(KVH)]) for s in range(2)]
    cols = np.concatenate([np.arange(AW + 2 * KW, AW + 2 * KW + PW), *keys, np.arange(AW + KW, AW + 2 * KW),
                           *halves, np.arange(AW + 2 * KW + PW, w_in.shape[1])])
    rows = np.concatenate([(QG * (2 * gh + gl) + m) * HD + np.arange(HD)
                           for gh in range(2) for m in range(QG) for gl in range(2)])
    x = np.concatenate([np.asarray(x_prompt).reshape(SEQ, D), np.asarray(x_sample).reshape(NS, D)])
    (cache_k, cache_v, state_pool, w_in, b_in, attn_sinks, w_attn_br, w_pool, pool_scale, w_out, ln1_g, ln1_b,
     w_query, sub_keys, peer_u, peer_v, ln2_g, ln2_b) = (np.asarray(a) for a in (
         cache_k, cache_v, state_pool, w_in, b_in, attn_sinks, w_attn_br, w_pool, pool_scale, w_out, ln1_g,
         ln1_b, w_query, sub_keys, peer_u, peer_v, ln2_g, ln2_b))
    unit = KT * P
    st = np.zeros((P, 8, 16 + DB * 16), np.float32)
    st[:, :, 16:].reshape(P, 8, DB, 16)[..., 1:] = state_pool.reshape(DB, HIST, 8, P).transpose(3, 2, 0, 1)
    vecs = np.concatenate([
        b_in[cols].reshape(52, P).T, pool_scale.reshape(16, P).T,
        np.broadcast_to(attn_sinks.reshape(KVH, QG).T.reshape(1, HEADS), (P, HEADS)),
        np.repeat(attn_sinks.reshape(KVH, QG).T, NS, axis=0),
        ln1_g.reshape(KT, P).T, ln1_b.reshape(KT, P).T, ln2_g.reshape(KT, P).T, ln2_b.reshape(KT, P).T], axis=1)
    ins = {
        "xT": _axes(x, (T, KT, P), (2, 1, 0)),
        "w_in": _axes(w_in[:, cols], (KT, P, 52, P), (2, 1, 0, 3)).reshape(52, P, unit),
        "w_pool": _axes(w_pool, (2, 2, 2, P, 4, P), (0, 3, 1, 4, 2, 5)).reshape(2, P, unit),
        "w_attn": _axes(w_attn_br[rows], (8, P, 8, 2, P), (2, 1, 3, 0, 4)).reshape(8, P, unit),
        "w_out": _axes(w_out, (KT, P, KT, P), (2, 1, 0, 3)).reshape(16, P, unit),
        "w_query": _axes(w_query, (KT, P, NHALF, P), (2, 1, 0, 3)).reshape(16, P, unit),
        "keysT": _axes(sub_keys, (NHALF, NK, HK), (2, 0, 1)),
        "peer_u": _axes(peer_u, (P, P, KT, P), (0, 3, 2, 1)).reshape(128, P, unit),
        "peer_v": _axes(peer_v, (BLOCKS, 8, P, 8, 2, P), (0, 3, 2, 4, 1, 5)).reshape(128, P, unit),
        "vecs": np.ascontiguousarray(vecs),
        "consts": const_table(),
        "kcT": _axes(cache_k, (DB, WIN, KVH, 2, 32), (2, 4, 3, 0, 1)).reshape(P, 2, DB, WIN),
        "vc": _axes(cache_v, (DB, WIN, KW), (1, 0, 2)),
        "stT": st,
        "k_nat": np.ascontiguousarray(cache_k.reshape(DB, WIN, KW)),
        "st_nat": np.ascontiguousarray(state_pool),
    }
    outs = {"yT": (P, KT, T), "kT": (P, 2, T), "vT": (P, 2, T), "uT": (P, 8, HIST), "us": (P, 8, DB, DS),
            "k_shift": (DB, WIN - DS, KW), "v_shift": (WIN - DS, DB, KW), "st_shift": (DB, HIST - DS, PW)}
    nc = bacc.Bacc("TRN2", target_bir_lowering=False, num_devices=1)
    args = [nc.dram_tensor(f"in_{k}", a.shape, F32, kind="ExternalInput").ap() for k, a in ins.items()]
    args += [nc.dram_tensor(f"out_{k}", s, F32, kind="ExternalOutput").ap() for k, s in outs.items()]
    layer(nc, *args)
    got = run_bass_kernel_spmd(nc, [{f"in_{k}": a for k, a in ins.items()}], core_ids=[0]).results[0]
    yT, kT, vT, uT, us, k_shift, v_shift, st_shift = (got[f"out_{k}"] for k in outs)
    y = yT.transpose(2, 1, 0).reshape(T, D)
    k = kT.reshape(KVH, 32, 2, T).transpose(3, 0, 2, 1).reshape(T, KVH, HD)
    v = vT.transpose(2, 1, 0).reshape(T, KVH, HD)
    u_new = us.transpose(2, 3, 1, 0).reshape(DB, DS, PW)
    k_new, v_new = (a[SEQ:].reshape(DB, DS, KVH, HD) for a in (k, v))
    return (np.ascontiguousarray(y[:SEQ]).reshape(1, SEQ, D), np.ascontiguousarray(y[SEQ:]).reshape(DB, DS, D),
            np.ascontiguousarray(k[SEQ - WIN:SEQ])[None], np.ascontiguousarray(v[SEQ - WIN:SEQ])[None],
            np.ascontiguousarray(uT.transpose(2, 1, 0).reshape(1, HIST, PW)),
            np.concatenate([k_shift.reshape(DB, WIN - DS, KVH, HD), k_new], axis=1),
            np.concatenate([v_shift.transpose(1, 0, 2).reshape(DB, WIN - DS, KVH, HD), v_new], axis=1),
            np.concatenate([st_shift, u_new], axis=1))
```
